# Optimizing a Trainium2 kernel written in Bass

```python
import jax
import jax.numpy as jnp
from jax import lax
import numpy as np
import math
import jax, jax.numpy as jnp

D_MODEL = 1024
BATCH = 1
SEQ = 512
DEPTH = 2

HEAD_DIM = 64
N_HEADS = D_MODEL // HEAD_DIM
SB_HEADS = N_HEADS // 2
NSA_HEADS = N_HEADS - SB_HEADS
NSA_KV_GROUPS = 2
FOX_HEADS = N_HEADS
CMP_LEN = 32
CMP_STRIDE = 16
SEL_LEN = 64
SEL_TOP = 16
WINDOW = 512
N_BRANCH = 3
Q_BLOCK = 128
ROPE_THETA = 500000.0
ROT_DIM = HEAD_DIM // 4
D_FF = 256 * ((8 * D_MODEL // 3 + 255) // 256)
CONV_WIDTH = 3
NORM_EPS = 1e-6
N_EVEN = (DEPTH + 1) // 2
N_ODD = DEPTH // 2
SB_W = SB_HEADS * HEAD_DIM
NSA_QW = NSA_HEADS * HEAD_DIM
NSA_KVW = NSA_KV_GROUPS * HEAD_DIM
EVEN_SPLITS = (SB_W, SB_W, SB_W, NSA_QW) + (NSA_KVW,) * 6 + (NSA_HEADS * N_BRANCH,)
EVEN_IN = sum(EVEN_SPLITS)
FOX_W = FOX_HEADS * HEAD_DIM
ODD_SPLITS = (FOX_W, FOX_W, FOX_W, FOX_HEADS)
ODD_IN = sum(ODD_SPLITS)


def rmsnorm(x, g):
    x32 = x.astype(jnp.float32)
    y = x32 * lax.rsqrt(jnp.mean(x32 * x32, axis=-1, keepdims=True) + NORM_EPS)
    return y.astype(x.dtype) * g

def split_cols(h, sizes):
    offs = np.cumsum(sizes)[:-1].tolist()
    return jnp.split(h, offs, axis=-1)

def partial_rope(x, pos):
    half = ROT_DIM // 2
    inv_freq = ROPE_THETA ** (-(jnp.arange(half, dtype=jnp.float32) * 2.0 / ROT_DIM))
    ang = pos[:, None] * inv_freq[None, :]
    cos = jnp.cos(ang)[None, :, None, :].astype(x.dtype)
    sin = jnp.sin(ang)[None, :, None, :].astype(x.dtype)
    x1 = x[..., :half]
    x2 = x[..., half:ROT_DIM]
    return jnp.concatenate([x1 * cos - x2 * sin, x1 * sin + x2 * cos, x[..., ROT_DIM:]], axis=-1)

def masked_softmax(s, mask):
    s = jnp.where(mask, s, -jnp.inf)
    m = jnp.max(s, axis=-1, keepdims=True)
    m = jnp.where(jnp.isfinite(m), m, 0.0)
    e = jnp.where(mask, jnp.exp(s - m), 0.0)
    d = jnp.sum(e, axis=-1, keepdims=True)
    return e / jnp.where(d > 0, d, 1.0)

def sweep_query_blocks(fn, seq):
    out = lax.map(fn, jnp.arange(seq // Q_BLOCK))
    nb, bsz, q, nh, dh = out.shape
    return jnp.moveaxis(out, 0, 1).reshape(bsz, nb * q, nh, dh)

def stick_breaking_attention(q, k, v):
    bsz, seq, nh, dh = q.shape
    scale = dh ** -0.5
    kpos = jnp.arange(seq)

    def block(i):
        q0 = i * Q_BLOCK
        qb = lax.dynamic_slice_in_dim(q, q0, Q_BLOCK, axis=1)
        tpos = q0 + jnp.arange(Q_BLOCK)
        z = jnp.einsum('bqhd,bshd->bhqs', qb, k, preferred_element_type=jnp.float32) * scale
        mask = kpos[None, :] < tpos[:, None]
        log_keep = jnp.where(mask, jax.nn.log_sigmoid(-z), 0.0)
        after = lax.cumsum(log_keep, axis=3, reverse=True) - log_keep
        a = jnp.where(mask, jnp.exp(jax.nn.log_sigmoid(z) + after), 0.0)
        return jnp.einsum('bhqs,bshd->bqhd', a.astype(v.dtype), v)

    return sweep_query_blocks(block, seq)

def forgetting_attention(q, k, v, log_f):
    bsz, seq, nh, dh = q.shape
    scale = dh ** -0.5
    kpos = jnp.arange(seq)
    cum = jnp.transpose(jnp.cumsum(log_f, axis=1), (0, 2, 1))

    def block(i):
        q0 = i * Q_BLOCK
        qb = lax.dynamic_slice_in_dim(q, q0, Q_BLOCK, axis=1)
        cq = lax.dynamic_slice_in_dim(cum, q0, Q_BLOCK, axis=2)
        tpos = q0 + jnp.arange(Q_BLOCK)
        s = jnp.einsum('bqhd,bshd->bhqs', qb, k, preferred_element_type=jnp.float32) * scale
        s = s + (cq[..., :, None] - cum[..., None, :])
        p = masked_softmax(s, kpos[None, :] <= tpos[:, None])
        return jnp.einsum('bhqs,bshd->bqhd', p.astype(v.dtype), v)

    return sweep_query_blocks(block, seq)

def nsa_attention(q, k_cmp, v_cmp, k_slc, v_slc, k_win, v_win, gates, pos_k, pos_v, w_ck, w_cv):
    bsz, seq, nh, dh = q.shape
    ng = k_cmp.shape[2]
    rep = nh // ng
    scale = dh ** -0.5
    n_cmp = (seq - CMP_LEN) // CMP_STRIDE + 1
    c_start = jnp.arange(n_cmp) * CMP_STRIDE
    cidx = c_start[:, None] + jnp.arange(CMP_LEN)[None, :]

    def compress(t, pe, w):
        blocks = t[:, cidx] + pe[None, None, :, None, :]
        blocks = jnp.moveaxis(blocks, 3, 2).reshape(bsz, n_cmp, ng, CMP_LEN * dh)
        return blocks @ w

    cmp_end = c_start + CMP_LEN - 1
    kc = partial_rope(compress(k_cmp, pos_k, w_ck), cmp_end.astype(jnp.float32))
    vc = compress(v_cmp, pos_v, w_cv)
    n_sel = seq // SEL_LEN
    top = min(SEL_TOP, n_sel)
    ks = k_slc.reshape(bsz, n_sel, SEL_LEN, ng, dh).transpose(0, 3, 1, 2, 4)
    vs = v_slc.reshape(bsz, n_sel, SEL_LEN, ng, dh).transpose(0, 3, 1, 2, 4)
    sel_start = jnp.arange(n_sel) * SEL_LEN
    overlap = (c_start[:, None] < sel_start[None, :] + SEL_LEN) & (c_start[:, None] + CMP_LEN > sel_start[None, :])
    cmp_to_sel = overlap.astype(jnp.float32)
    blk = jnp.arange(n_sel)
    bi = jnp.arange(bsz)[:, None, None, None]
    gi = jnp.arange(ng)[None, :, None, None]
    kw = jnp.pad(k_win, ((0, 0), (WINDOW, 0), (0, 0), (0, 0)))
    vw = jnp.pad(v_win, ((0, 0), (WINDOW, 0), (0, 0), (0, 0)))

    def block(i):
        q0 = i * Q_BLOCK
        tpos = q0 + jnp.arange(Q_BLOCK)
        qb = lax.dynamic_slice_in_dim(q, q0, Q_BLOCK, axis=1).reshape(bsz, Q_BLOCK, ng, rep, dh)
        sc = jnp.einsum('bqgrd,bcgd->bgrqc', qb, kc, preferred_element_type=jnp.float32) * scale
        pc = masked_softmax(sc, cmp_end[None, :] <= tpos[:, None])
        o_cmp = jnp.einsum('bgrqc,bcgd->bqgrd', pc.astype(vc.dtype), vc)
        imp = jnp.einsum('bgrqc,cn->bgqn', pc, cmp_to_sel)
        cur = tpos // SEL_LEN
        causal = blk[None, :] <= cur[:, None]
        forced = (blk[None, :] == 0) | (blk[None, :] == cur[:, None]) | (blk[None, :] == cur[:, None] - 1)
        score = jnp.where(causal, jnp.where(forced, jnp.inf, imp), -jnp.inf)
        top_val, top_idx = lax.top_k(score, top)
        sel_ok = top_val > -jnp.inf
        kg = ks[bi, gi, top_idx]
        vg = vs[bi, gi, top_idx]
        kpos = top_idx[..., None] * SEL_LEN + jnp.arange(SEL_LEN)
        smask = sel_ok[..., None] & (kpos <= tpos[None, None, :, None, None])
        ss = jnp.einsum('bqgrd,bgqnld->bgrqnl', qb, kg, preferred_element_type=jnp.float32) * scale
        ps = masked_softmax(ss.reshape(bsz, ng, rep, Q_BLOCK, top * SEL_LEN),
                            smask.reshape(bsz, ng, 1, Q_BLOCK, top * SEL_LEN))
        ps = ps.reshape(bsz, ng, rep, Q_BLOCK, top, SEL_LEN)
        o_slc = jnp.einsum('bgrqnl,bgqnld->bqgrd', ps.astype(vg.dtype), vg)
        kwb = lax.dynamic_slice_in_dim(kw, q0, Q_BLOCK + WINDOW, axis=1)
        vwb = lax.dynamic_slice_in_dim(vw, q0, Q_BLOCK + WINDOW, axis=1)
        wpos = q0 - WINDOW + jnp.arange(Q_BLOCK + WINDOW)
        wmask = (wpos[None, :] >= 0) & (wpos[None, :] <= tpos[:, None]) & (wpos[None, :] > tpos[:, None] - WINDOW)
        sw = jnp.einsum('bqgrd,bkgd->bgrqk', qb, kwb, preferred_element_type=jnp.float32) * scale
        pw = masked_softmax(sw, wmask)
        o_win = jnp.einsum('bgrqk,bkgd->bqgrd', pw.astype(vwb.dtype), vwb)
        gb = lax.dynamic_slice_in_dim(gates, q0, Q_BLOCK, axis=1).reshape(bsz, Q_BLOCK, ng, rep, N_BRANCH)
        o = gb[..., 0:1] * o_cmp + gb[..., 1:2] * o_slc + gb[..., 2:3] * o_win
        return o.reshape(bsz, Q_BLOCK, nh, dh)

    return sweep_query_blocks(block, seq)

def even_mixer(h, w_in, pos_k, pos_v, w_ck, w_cv, w_out):
    bsz, seq, _ = h.shape
    sq, sk, sv, nq, kc, vc, ksl, vsl, kwn, vwn, g = split_cols(h @ w_in, EVEN_SPLITS)
    pos = jnp.arange(seq, dtype=jnp.float32)

    def heads(t):
        return t.reshape(bsz, seq, -1, HEAD_DIM)

    o_sb = stick_breaking_attention(heads(sq), heads(sk), heads(sv))
    o_nsa = nsa_attention(partial_rope(heads(nq), pos), heads(kc), heads(vc),
                          partial_rope(heads(ksl), pos), heads(vsl),
                          partial_rope(heads(kwn), pos), heads(vwn),
                          jax.nn.sigmoid(g.reshape(bsz, seq, NSA_HEADS, N_BRANCH)),
                          pos_k, pos_v, w_ck, w_cv)
    o = jnp.concatenate([o_sb.reshape(bsz, seq, SB_W), o_nsa.reshape(bsz, seq, NSA_QW)], axis=-1)
    return o @ w_out

def odd_mixer(h, w_in, b_f, w_out):
    bsz, seq, _ = h.shape
    q, k, v, f = split_cols(h @ w_in, ODD_SPLITS)
    log_f = jax.nn.log_sigmoid((f + b_f).astype(jnp.float32))
    o = forgetting_attention(q.reshape(bsz, seq, FOX_HEADS, HEAD_DIM),
                             k.reshape(bsz, seq, FOX_HEADS, HEAD_DIM),
                             v.reshape(bsz, seq, FOX_HEADS, HEAD_DIM), log_f)
    return o.reshape(bsz, seq, FOX_W) @ w_out

def conv_glu_ffn(h, w_in, conv_w, conv_b, w_out):
    a, b = jnp.split(h @ w_in, 2, axis=-1)
    taps = conv_w[:, None, :]
    a = lax.conv_general_dilated(a, taps, window_strides=(1,), padding=[(CONV_WIDTH - 1, 0)],
                                 dimension_numbers=('NWC', 'WIO', 'NWC'),
                                 feature_group_count=a.shape[-1]) + conv_b
    return (jax.nn.silu(a) * b) @ w_out

def first_inputs(seed: int = 0) -> dict:
    key = jax.random.key(seed)
    k = jax.random.split(key, 17)

    def nrm(kk, shape, scale):
        return jax.random.normal(kk, shape, jnp.float32) * scale

    d = D_MODEL
    lc = CMP_LEN * HEAD_DIM
    return {
        'x': nrm(k[0], (BATCH, SEQ, d), 1.0),
        'attn_norm': 1.0 + nrm(k[1], (DEPTH, d), 0.02),
        'ffn_norm': 1.0 + nrm(k[2], (DEPTH, d), 0.02),
        'ev_w_in': nrm(k[3], (N_EVEN, d, EVEN_IN), d ** -0.5),
        'ev_cmp_pos_k': nrm(k[4], (N_EVEN, CMP_LEN, HEAD_DIM), 0.2),
        'ev_cmp_pos_v': nrm(k[5], (N_EVEN, CMP_LEN, HEAD_DIM), 0.2),
        'ev_cmp_w_k': nrm(k[6], (N_EVEN, lc, HEAD_DIM), lc ** -0.5),
        'ev_cmp_w_v': nrm(k[7], (N_EVEN, lc, HEAD_DIM), lc ** -0.5),
        'ev_w_out': nrm(k[8], (N_EVEN, SB_W + NSA_QW, d), (SB_W + NSA_QW) ** -0.5),
        'od_w_in': nrm(k[9], (N_ODD, d, ODD_IN), d ** -0.5),
        'od_b_f': 2.0 + nrm(k[10], (N_ODD, FOX_HEADS), 0.5),
        'od_w_out': nrm(k[11], (N_ODD, FOX_W, d), FOX_W ** -0.5),
        'ffn_w_in': nrm(k[12], (DEPTH, d, 2 * D_FF), d ** -0.5),
        'ffn_conv_w': nrm(k[13], (DEPTH, CONV_WIDTH, D_FF), CONV_WIDTH ** -0.5),
        'ffn_conv_b': nrm(k[14], (DEPTH, D_FF), 0.02),
        'ffn_w_out': nrm(k[15], (DEPTH, D_FF, d), D_FF ** -0.5),
        'final_norm': 1.0 + nrm(k[16], (d,), 0.02),
    }

def first_block(x, attn_norm, ffn_norm, ev_w_in, ev_cmp_pos_k, ev_cmp_pos_v, ev_cmp_w_k, ev_cmp_w_v,
              ev_w_out, od_w_in, od_b_f, od_w_out, ffn_w_in, ffn_conv_w, ffn_conv_b, ffn_w_out,
              final_norm):
    for layer in range(DEPTH):
        h = rmsnorm(x, attn_norm[layer])
        if layer % 2 == 0:
            e = layer // 2
            x = x + even_mixer(h, ev_w_in[e], ev_cmp_pos_k[e], ev_cmp_pos_v[e],
                               ev_cmp_w_k[e], ev_cmp_w_v[e], ev_w_out[e])
        else:
            o = layer // 2
            x = x + odd_mixer(h, od_w_in[o], od_b_f[o], od_w_out[o])
        x = x + conv_glu_ffn(rmsnorm(x, ffn_norm[layer]), ffn_w_in[layer], ffn_conv_w[layer],
                             ffn_conv_b[layer], ffn_w_out[layer])
    return rmsnorm(x, final_norm)


N_ATT_HEADS = 8
ATT_W = N_ATT_HEADS * HEAD_DIM
N_IDX_HEADS = 4
IDX_DIM = HEAD_DIM
INDEX_TOPK_MAX = 256
D_SSM = D_MODEL
SSM_HEAD_DIM = 64
N_SSM_HEADS = D_SSM // SSM_HEAD_DIM
N_GROUPS = 2
D_STATE = 128
CONV_K = 4
CHUNK = 128
CONV_CH = D_SSM + 2 * N_GROUPS * D_STATE
ROPE_THETA_2 = 10000.0
EPS = 1e-6
NEG = -1e30
IN_SIZES = (ATT_W, HEAD_DIM, HEAD_DIM, ATT_W,
            N_IDX_HEADS * IDX_DIM, IDX_DIM, N_IDX_HEADS,
            D_SSM, CONV_CH, N_SSM_HEADS,
            D_MODEL, D_MODEL)
N_IN = sum(IN_SIZES)


def _rmsnorm(u, g):
    u32 = u.astype(jnp.float32)
    y = u32 * lax.rsqrt(jnp.mean(u32 * u32, axis=-1, keepdims=True) + EPS)
    return (y * g.astype(jnp.float32)).astype(u.dtype)

def _split_cols(p, sizes):
    offs, acc = [], 0
    for s in sizes[:-1]:
        acc += s
        offs.append(acc)
    return jnp.split(p, offs, axis=-1)

def _rope_tables(L):
    inv = ROPE_THETA_2 ** (-jnp.arange(0, HEAD_DIM, 2, dtype=jnp.float32) / HEAD_DIM)
    ang = jnp.arange(L, dtype=jnp.float32)[:, None] * inv[None, :]
    ang = jnp.concatenate([ang, ang], axis=-1)
    return jnp.cos(ang), jnp.sin(ang)

def _rope(u, cos, sin):
    u32 = u.astype(jnp.float32)
    half = u32.shape[-1] // 2
    rot = jnp.concatenate([-u32[..., half:], u32[..., :half]], axis=-1)
    return (u32 * cos + rot * sin).astype(u.dtype)

def _causal_dwconv(u, w, b):
    out = lax.conv_general_dilated(u, w[:, None, :], window_strides=(1,), padding=((CONV_K - 1, 0),),
                                   dimension_numbers=('NWC', 'WIO', 'NWC'), feature_group_count=u.shape[-1])
    return out + b

def _dsa_attention(q, k, v, qi, ki, wi, topk):
    B, L = q.shape[0], q.shape[1]
    nb = L // Q_BLOCK
    kv = jnp.concatenate([k, v], axis=-1)
    key_pos = jnp.arange(L, dtype=jnp.int32)
    ki32 = ki.astype(jnp.float32)

    def blocks(u):
        return u.reshape((B, nb, Q_BLOCK) + u.shape[2:]).swapaxes(0, 1)

    starts = jnp.arange(nb, dtype=jnp.int32) * Q_BLOCK

    def one_block(inp):
        qb, qib, wb, t0 = inp
        qpos = t0 + jnp.arange(Q_BLOCK, dtype=jnp.int32)
        dots = jnp.einsum('bqhd,bsd->bqhs', qib.astype(jnp.float32), ki32) * IDX_DIM ** -0.5
        score = jnp.einsum('bqhs,bqh->bqs', jax.nn.relu(dots), wb.astype(jnp.float32))
        admissible = key_pos[None, :] <= qpos[:, None]
        score = jnp.where(admissible[None], score, NEG)
        _, sel = lax.top_k(score, topk)
        valid = sel <= qpos[None, :, None]
        kvg = jax.vmap(lambda t, i: t[i])(kv, sel)
        kg, vg = kvg[..., :HEAD_DIM], kvg[..., HEAD_DIM:]
        logits = jnp.einsum('bqhd,bqkd->bqhk', qb.astype(jnp.float32), kg.astype(jnp.float32)) * HEAD_DIM ** -0.5
        logits = jnp.where(valid[:, :, None, :], logits, NEG)
        p = jax.nn.softmax(logits, axis=-1)
        o = jnp.einsum('bqhk,bqkd->bqhd', p, vg.astype(jnp.float32))
        return o.astype(q.dtype)

    out = lax.map(one_block, (blocks(q), blocks(qi), blocks(wi), starts))
    return out.swapaxes(0, 1).reshape(B, L, ATT_W)

def _ssd_chunked(xh, dt, a, bm, cm):
    Bsz, L, H, P = xh.shape
    G, N = bm.shape[2], bm.shape[3]
    R = H // G
    nc = L // CHUNK
    xd = (xh * dt[..., None]).reshape(Bsz, nc, CHUNK, G, R, P)
    adt = (dt * a).reshape(Bsz, nc, CHUNK, G, R).transpose(0, 3, 4, 1, 2)
    a_cs = jnp.cumsum(adt, axis=-1)
    bm = bm.reshape(Bsz, nc, CHUNK, G, N)
    cm = cm.reshape(Bsz, nc, CHUNK, G, N)
    tril = jnp.tril(jnp.ones((CHUNK, CHUNK), dtype=bool))
    seg = a_cs[..., :, None] - a_cs[..., None, :]
    decay = jnp.exp(jnp.where(tril, seg, -jnp.inf))
    cb = jnp.einsum('bclgn,bcsgn->bgcls', cm, bm)
    y_diag = jnp.einsum('bgcls,bgrcls,bcsgrp->bclgrp', cb, decay, xd)
    decay_states = jnp.exp(a_cs[..., -1:] - a_cs)
    states = jnp.einsum('bclgn,bgrcl,bclgrp->bcgrpn', bm, decay_states, xd)
    chunk_decay = jnp.exp(a_cs[..., -1])

    def step(h, inp):
        s, d = inp
        return h * d[..., None, None] + s, h

    h0 = jnp.zeros((Bsz, G, R, P, N), dtype=xd.dtype)
    _, prev = lax.scan(step, h0, (states.transpose(1, 0, 2, 3, 4, 5), chunk_decay.transpose(3, 0, 1, 2)))
    prev = prev.transpose(1, 0, 2, 3, 4, 5)
    y_off = jnp.einsum('bclgn,bcgrpn,bgrcl->bclgrp', cm, prev, jnp.exp(a_cs))
    return (y_diag + y_off).reshape(Bsz, L, H, P)

def _layer(x, c, w_ada, b_ada, norm_g, w_in, conv_w, conv_b, dt_bias, a_log, d_skip, ssm_norm_g,
           w_branch_a, w_branch_s, w_out, cos, sin, topk):
    B, L, _ = x.shape
    mod = jax.nn.silu(c) @ w_ada + b_ada
    shift, scale, gate = jnp.split(mod, 3, axis=-1)
    h = _rmsnorm(x, norm_g) * (1.0 + scale[:, None, :]) + shift[:, None, :]
    proj = h @ w_in
    (q, k, v, g_att, qi, ki, wi, z, xbc, dt_raw, gl_att, gl_ssd) = _split_cols(proj, IN_SIZES)

    q = _rope(q.reshape(B, L, N_ATT_HEADS, HEAD_DIM), cos[:, None, :], sin[:, None, :])
    k = _rope(k, cos, sin)
    qi = _rope(qi.reshape(B, L, N_IDX_HEADS, IDX_DIM), cos[:, None, :], sin[:, None, :])
    ki = _rope(ki, cos, sin)
    wi = wi * N_IDX_HEADS ** -0.5
    o_att = _dsa_attention(q, k, v, qi, ki, wi, topk)
    y_att = (o_att * jax.nn.silu(g_att)) @ w_branch_a

    xbc = jax.nn.silu(_causal_dwconv(xbc, conv_w, conv_b))
    xs, bm, cm = jnp.split(xbc, [D_SSM, D_SSM + N_GROUPS * D_STATE], axis=-1)
    xh = xs.reshape(B, L, N_SSM_HEADS, SSM_HEAD_DIM).astype(jnp.float32)
    dt = jax.nn.softplus(dt_raw.astype(jnp.float32) + dt_bias.astype(jnp.float32))
    a = -jnp.exp(a_log.astype(jnp.float32))
    y = _ssd_chunked(xh, dt, a,
                     bm.reshape(B, L, N_GROUPS, D_STATE).astype(jnp.float32),
                     cm.reshape(B, L, N_GROUPS, D_STATE).astype(jnp.float32))
    y = y + d_skip.astype(jnp.float32)[:, None] * xh
    y = y.reshape(B, L, D_SSM) * jax.nn.silu(z.astype(jnp.float32))
    y = y.reshape(B, L, N_GROUPS, D_SSM // N_GROUPS)
    y = y * lax.rsqrt(jnp.mean(y * y, axis=-1, keepdims=True) + EPS)
    y = (y.reshape(B, L, D_SSM) * ssm_norm_g.astype(jnp.float32)).astype(x.dtype)
    y_ssd = y @ w_branch_s

    merged = jax.nn.sigmoid(gl_att) * y_att + jax.nn.sigmoid(gl_ssd) * y_ssd
    return x + gate[:, None, :] * (merged @ w_out)

def second_inputs(seed: int = 0) -> dict:
    key = jax.random.key(seed)
    ks = jax.random.split(key, 16)
    f32 = jnp.float32
    x = jax.random.normal(ks[0], (BATCH, SEQ, D_MODEL), f32)
    c = jax.random.normal(ks[1], (BATCH, D_MODEL), f32)
    w_ada = jax.random.normal(ks[2], (DEPTH, D_MODEL, 3 * D_MODEL), f32) * (0.5 * D_MODEL ** -0.5)
    b_ada = jax.random.normal(ks[3], (DEPTH, 3 * D_MODEL), f32) * 0.02
    norm_g = 1.0 + 0.05 * jax.random.normal(ks[4], (DEPTH, D_MODEL), f32)
    w_in = jax.random.normal(ks[5], (DEPTH, D_MODEL, N_IN), f32) * D_MODEL ** -0.5
    conv_w = jax.random.normal(ks[6], (DEPTH, CONV_K, CONV_CH), f32) * CONV_K ** -0.5
    conv_b = jax.random.normal(ks[7], (DEPTH, CONV_CH), f32) * 0.02
    dt0 = jnp.exp(jax.random.uniform(ks[8], (DEPTH, N_SSM_HEADS), f32, math.log(1e-3), math.log(1e-1)))
    dt_bias = dt0 + jnp.log(-jnp.expm1(-dt0))
    a_log = jnp.log(jax.random.uniform(ks[9], (DEPTH, N_SSM_HEADS), f32, 1.0, 16.0))
    d_skip = 1.0 + 0.1 * jax.random.normal(ks[10], (DEPTH, N_SSM_HEADS), f32)
    ssm_norm_g = 1.0 + 0.05 * jax.random.normal(ks[11], (DEPTH, D_SSM), f32)
    w_branch_a = jax.random.normal(ks[12], (DEPTH, ATT_W, D_MODEL), f32) * ATT_W ** -0.5
    w_branch_s = jax.random.normal(ks[13], (DEPTH, D_SSM, D_MODEL), f32) * D_SSM ** -0.5
    w_out = jax.random.normal(ks[14], (DEPTH, D_MODEL, D_MODEL), f32) * D_MODEL ** -0.5
    final_g = 1.0 + 0.05 * jax.random.normal(ks[15], (D_MODEL,), f32)
    return {'x': x, 'c': c, 'w_ada': w_ada, 'b_ada': b_ada, 'norm_g': norm_g, 'w_in': w_in,
            'conv_w': conv_w, 'conv_b': conv_b, 'dt_bias': dt_bias, 'a_log': a_log, 'd_skip': d_skip,
            'ssm_norm_g': ssm_norm_g, 'w_branch_a': w_branch_a, 'w_branch_s': w_branch_s,
            'w_out': w_out, 'final_g': final_g}

def second_block(x, c, w_ada, b_ada, norm_g, w_in, conv_w, conv_b, dt_bias, a_log, d_skip,
              ssm_norm_g, w_branch_a, w_branch_s, w_out, final_g):
    L = x.shape[1]
    topk = min(INDEX_TOPK_MAX, L // 4)
    cos, sin = _rope_tables(L)
    for i in range(DEPTH):
        x = _layer(x, c, w_ada[i], b_ada[i], norm_g[i], w_in[i], conv_w[i], conv_b[i], dt_bias[i],
                   a_log[i], d_skip[i], ssm_norm_g[i], w_branch_a[i], w_branch_s[i], w_out[i],
                   cos, sin, topk)
    return _rmsnorm(x, final_g)


def setup_inputs(seed=0):
    out = dict(first_inputs(seed))
    for name, value in second_inputs(seed + 1).items():
        if name != "x":
            out[name + "_2"] = value
    return out


def reference(
    x, attn_norm, ffn_norm, ev_w_in, ev_cmp_pos_k, ev_cmp_pos_v, ev_cmp_w_k, ev_cmp_w_v,
    ev_w_out, od_w_in, od_b_f, od_w_out, ffn_w_in, ffn_conv_w, ffn_conv_b, ffn_w_out,
    final_norm, c_2, w_ada_2, b_ada_2, norm_g_2, w_in_2, conv_w_2, conv_b_2, dt_bias_2, a_log_2,
    d_skip_2, ssm_norm_g_2, w_branch_a_2, w_branch_s_2, w_out_2, final_g_2,
):
    x = first_block(
        x, attn_norm, ffn_norm, ev_w_in, ev_cmp_pos_k, ev_cmp_pos_v, ev_cmp_w_k, ev_cmp_w_v,
        ev_w_out, od_w_in, od_b_f, od_w_out, ffn_w_in, ffn_conv_w, ffn_conv_b, ffn_w_out,
        final_norm,
    )
    return second_block(
        x, c_2, w_ada_2, b_ada_2, norm_g_2, w_in_2, conv_w_2, conv_b_2, dt_bias_2, a_log_2,
        d_skip_2, ssm_norm_g_2, w_branch_a_2, w_branch_s_2, w_out_2, final_g_2,
    )


_drawn_inputs = setup_inputs


def setup_inputs(seed=0):
    import zlib

    import numpy as np

    out = dict(_drawn_inputs(seed))
    spreads = {}
    factors = {'attn_norm': 3.016,
     'ev_cmp_pos_k': 8.0,
     'ffn_conv_b': 3.983,
     'final_norm': 2.742,
     'b_ada_2': 2.801,
     'norm_g_2': 3.016,
     'conv_b_2': 8.0,
     'd_skip_2': 3.855,
     'ssm_norm_g_2': 4.88}
    for name, (base, spread) in spreads.items():
        noise = np.random.default_rng([zlib.crc32(name.encode()), seed]).standard_normal(out[name].shape)
        drawn = base * np.exp(spread * noise) if base else spread * noise
        out[name] = jnp.asarray(drawn.astype(out[name].dtype))
    for name, factor in factors.items():
        out[name] = (out[name] * factor).astype(out[name].dtype)
    return out
```

```python
from contextlib import ExitStack

import numpy as np

import concourse.bass as bass
from concourse import mybir

F32 = mybir.dt.float32
BF16 = mybir.dt.bfloat16
ALU = mybir.AluOpType
ACT = mybir.ActivationFunctionType
AX = mybir.AxisListType

P = 128
D = 1024
KD = D // P
SEQ = 512
NT = SEQ // P
DH = 64
SCALE = DH ** -0.5
NEG = -1e30
TAKEN = -3e38
EPS = 1e-6
D_FF = 2816
FC = D_FF // P
NCMP = 31
CMP_LEN = 32
CMP_STRIDE = 16
TOPK = 128
RING = 6
ARENA = 28600
NBANK = 8
LAYERS = 2


def stream():
    tiles = []

    def full(name, layer, cols):
        for k in range(KD):
            tiles.append((name, layer, k * P, cols))

    def proj(name, layer, start, width):
        for i in range(0, width, P):
            full(name, layer, list(range(start + i, start + min(i + P, width))))

    def tall(name, layer, kt):
        for n in range(KD):
            for k in range(kt):
                tiles.append((name, layer, k * P, list(range(n * P, n * P + P))))

    def ffn(layer):
        for n in range(FC):
            proj("ffn_w_in", layer, n * P, P)
            proj("ffn_w_in", layer, D_FF + n * P, P)
        tall("ffn_w_out", layer, FC)

    sq, sk, sv, nq, kc, vc, ksl, vsl, kwn, vwn, g = 0, 512, 1024, 1536, 2048, 2176, 2304, 2432, 2560, 2688, 2816
    proj("ev_w_in", 0, kc, P)
    proj("ev_w_in", 0, vc, P)
    proj("ev_w_in", 0, ksl, P)
    proj("ev_w_in", 0, kwn, P)
    for c in range(4):
        full("ev_w_in", 0, [nq + (gr * 4 + c) * DH + i for gr in range(2) for i in range(DH)])
    proj("ev_w_in", 0, sk, 512)
    proj("ev_w_in", 0, sq, 512)
    proj("ev_w_in", 0, sv, 512)
    proj("ev_w_in", 0, vsl, P)
    proj("ev_w_in", 0, vwn, P)
    proj("ev_w_in", 0, g, 24)
    for name in ("ev_cmp_w_k", "ev_cmp_w_v"):
        for l in range(CMP_LEN):
            tiles.append((name, 0, l * DH, "twice"))
    tall("ev_w_out", 0, KD)
    ffn(0)
    proj("od_w_in", 0, 3072, 16)
    proj("od_w_in", 0, 0, 3072)
    tall("od_w_out", 0, KD)
    ffn(1)
    for layer in range(LAYERS):
        proj("w_ada_2", layer, 0, 3072)
    for layer in range(LAYERS):
        w = "w_in_2"
        proj(w, layer, 1152, 256)
        full(w, layer, [1408 + i for _ in range(2) for i in range(DH)])
        proj(w, layer, 1472, 4)
        proj(w, layer, 0, 512)
        full(w, layer, [512 + i for _ in range(2) for i in range(DH)])
        proj(w, layer, 576, DH)
        proj(w, layer, 4036, 16)
        proj(w, layer, 2500, 1536)
        proj(w, layer, 640, 512)
        proj(w, layer, 1476, 1024)
        for n in range(KD):
            for k in range(4):
                tiles.append(("w_branch_a_2", layer, k * P, list(range(n * P, n * P + P))))
            if n % 2:
                for m in (n - 1, n):
                    proj(w, layer, 4052 + m * P, P)
                    proj(w, layer, 5076 + m * P, P)
                    for k in range(KD):
                        tiles.append(("w_branch_s_2", layer, k * P, list(range(m * P, m * P + P))))
        tall("w_out_2", layer, KD)
    return tiles


def vec_layout():
    at, n = {}, 0
    for name, layer, cols in (
        [("attn_norm", l, KD) for l in range(2)] + [("ffn_norm", l, KD) for l in range(2)]
        + [("conv_w", (l, j), FC) for l in range(2) for j in range(3)] + [("conv_b", l, FC) for l in range(2)]
        + [("final_norm", 0, KD), ("pos_k", 0, CMP_LEN), ("pos_v", 0, CMP_LEN), ("b_f", 0, 1), ("c", 0, KD)]
        + [("b_ada", l, 24) for l in range(2)] + [("norm_g", l, KD) for l in range(2)]
        + [("xconv_w", (l, j), 12) for l in range(2) for j in range(4)] + [("xconv_b", l, 12) for l in range(2)]
        + [("dt_bias", l, 1) for l in range(2)] + [("a_log", l, 1) for l in range(2)]
        + [("d_skip", l, KD) for l in range(2)] + [("ssm_g", l, KD) for l in range(2)] + [("final_g", 0, KD)]
    ):
        at[name, layer] = n
        n += cols
    return at, n


VEC, NVEC = vec_layout()

CF = {}
CB = {}


def _place(table, items):
    n = 0
    for name, w in items:
        table[name] = (n, w)
        n += w
    return n


NCF = _place(CF, [("ident", P), ("tri", P), ("nones", P), ("mean_d", P), ("mean_g", P), ("perm8", P), ("perm32", P),
                  ("cos8", SEQ), ("sin8", SEQ), ("cosc", 32), ("sinc", 32), ("cos32", SEQ), ("sin32", SEQ),
                  ("strict", P), ("causalT", P), ("cmp01", NT * 32), ("sel", 16 * P), ("ones", SEQ)])
NCB = _place(CB, [("ident", P), ("causal", P), ("strictT", P), ("cmp", NT * P), ("selneg", 16 * P)])


def constants():
    f = np.zeros((P, NCF), np.float32)
    b = np.zeros((P, NCB), np.float32)

    def put(t, table, name, a):
        a = np.asarray(a, np.float32).reshape(a.shape[0], -1)
        o, w = table[name]
        assert a.shape[1] == w, name
        t[: a.shape[0], o:o + w] = a

    i = np.arange(P)
    put(f, CF, "ident", np.eye(P))
    put(f, CF, "tri", -(i[:, None] >= i[None, :]).astype(np.float32))
    put(f, CF, "nones", -np.ones((P, P)))
    put(f, CF, "mean_d", np.full((P, P), 1.0 / D))
    put(f, CF, "mean_g", np.full((P, P), 1.0 / 512))

    def rope(rot, theta, pos):
        half = rot // 2
        if rot == 16:
            inv = (np.float32(theta) ** (-(np.arange(half, dtype=np.float32) * np.float32(2.0) / np.float32(rot)))).astype(np.float32)
        else:
            inv = (np.float32(theta) ** (-np.arange(0, rot, 2, dtype=np.float32) / np.float32(rot))).astype(np.float32)
        ang = (pos.astype(np.float32)[:, None] * inv[None, :]).astype(np.float32)
        cos = np.ones((P, len(pos)), np.float32)
        sin = np.zeros((P, len(pos)), np.float32)
        perm = np.zeros((P, P), np.float32)
        for base in (0, DH):
            for j in range(DH):
                if j < half:
                    src, s = j + half, -1.0
                elif j < rot:
                    src, s = j - half, 1.0
                else:
                    perm[base + j, base + j] = 1.0
                    continue
                perm[base + src, base + j] = 1.0
                cos[base + j] = np.cos(ang[:, j % half])
                sin[base + j] = s * np.sin(ang[:, j % half])
        return cos, sin, perm

    pos = np.arange(SEQ)
    cmp_end = np.arange(32) * CMP_STRIDE + CMP_LEN - 1
    c, s, m = rope(16, 500000.0, pos)
    put(f, CF, "cos8", c), put(f, CF, "sin8", s), put(f, CF, "perm8", m)
    c, s, m = rope(16, 500000.0, cmp_end)
    put(f, CF, "cosc", c), put(f, CF, "sinc", s)
    c, s, m = rope(64, 10000.0, pos)
    put(f, CF, "cos32", c), put(f, CF, "sin32", s), put(f, CF, "perm32", m)
    put(f, CF, "strict", (i[:, None] < i[None, :]).astype(np.float32))
    put(f, CF, "causalT", (i[:, None] <= i[None, :]).astype(np.float32))
    seen = (cmp_end[None, None, :] <= (i[:, None, None] + P * np.arange(NT)[None, :, None])) & (np.arange(32) < NCMP)
    put(f, CF, "cmp01", seen.astype(np.float32))
    sel = np.zeros((16, 16, P), np.float32)
    sel[np.arange(16), np.arange(16)] = 1.0
    put(f, CF, "sel", sel)
    put(f, CF, "ones", np.ones((P, SEQ)))
    put(b, CB, "ident", np.eye(P))
    put(b, CB, "causal", np.where(i[None, :] > i[:, None], NEG, 0.0))
    put(b, CB, "strictT", np.where(i[:, None] >= i[None, :], NEG, 0.0))
    put(b, CB, "cmp", np.repeat(np.where(seen, 0.0, NEG)[:, :, None, :], 4, axis=2))
    sn = np.zeros((96, 16, P), np.float32)
    for q in range(3):
        sn[32 * q + np.arange(16), np.arange(16)] = -1.0
    put(b, CB, "selneg", sn)
    return f, b


class Signal:

    def __init__(self, sem, known):
        self.sem, self.known, self.count, self.at = sem, known, 0, {}

    def mark(self, key=None, n=1):
        self.count += n
        assert key is None or key not in self.at, key
        self.at[key] = self.count
        return self.sem, n

    def __getitem__(self, key):
        if self.known is None:
            return self.sem, 1
        return self.sem, self.known[key]


class Banks:

    def __init__(self, aps, signals, order, drained):
        self.aps, self.signals = aps, signals
        self.number = {key: n for n, key in enumerate(order or [])}
        self.known, self.order, self.drained = drained, [], {}

    def take(self, pe, key):
        n = len(self.order)
        self.order.append(key)
        if n >= NBANK:
            name, count = self.known.get(self.order[n - NBANK]) if self.known else (next(iter(self.signals)), 1)
            pe.wait_ge(self.signals[name].sem, count)
        return self.aps[n % NBANK]

    def __getitem__(self, key):
        return self.aps[self.number[key] % NBANK if self.number else 0]

    def drain(self, key, name):
        self.drained[key] = (name, self.signals[name].count)


SIGNALS = ["bank_filled", "act_made", "dve_made", "pool_made"]


def build(nc, ins, out, known=None):
    stream_of, x_in, vec_in, cf_in, cb_in = ins
    n_tiles = stream_of.shape[0] * KD
    with ExitStack() as ctx:
        def sb(name, shape, dt=F32):
            return ctx.enter_context(nc.sbuf_tensor(name, shape, dt))

        ring = sb("ring", [P, RING, KD, P])
        xT = sb("xT", [P, KD, SEQ])
        hT = sb("hT", [P, KD, SEQ])
        vec = sb("vecs", [P, NVEC])
        cf = sb("cf_sb", [P, NCF])
        cb = sb("cb_sb", [P, NCB], BF16)
        small = sb("small", [P, 1024])
        arena = sb("arena", [P, ARENA])
        psum = [ctx.enter_context(nc.psum_tensor(f"bank{i}", [P, SEQ], F32)) for i in range(NBANK)]

        signals = {name: Signal(ctx.enter_context(nc.semaphore(name)), known and known["signals"][name])
                   for name in SIGNALS}
        filled, act_made, dve_made, pool_made = (signals[n] for n in SIGNALS)
        banks = Banks(psum, signals, known and known["order"], known and known["drained"])
        panel_landed = [ctx.enter_context(nc.semaphore(f"panel_landed{i}")) for i in range(RING)]
        panel_used = ctx.enter_context(nc.semaphore("panel_used"))
        x_landed = ctx.enter_context(nc.semaphore("x_landed"))
        const_landed = ctx.enter_context(nc.semaphore("const_landed"))
        out_stored = ctx.enter_context(nc.semaphore("out_stored"))

        def cst(name):
            o, w = CF[name]
            return cf[:, o:o + w]

        def cstb(name):
            o, w = CB[name]
            return cb[:, o:o + w]

        def col(name, layer, k=0, parts=P):
            o = VEC[name, layer] + k
            return vec[0:parts, o:o + 1]

        class Area:

            def __init__(self, base=0):
                self.at = base

            def take(self, *shape):
                n = int(np.prod(shape))
                a = arena[:, self.at:self.at + n]
                self.at += n
                assert self.at <= ARENA, self.at
                if len(shape) == 2:
                    a = a.rearrange("p (a b) -> p a b", a=shape[0])
                elif len(shape) == 3:
                    a = a.rearrange("p (a b c) -> p a b c", a=shape[0], b=shape[1])
                return a

            def take16(self, n):
                a = arena[:, self.at:self.at + n // 2].bitcast(BF16)
                self.at += n // 2
                return a

        ident = cst("ident")
        identb = cstb("ident")
        eps = small[:, 1023:1024]

        tile_no = [0]
        owed = [0]

        def mm(pe, *args, done=None, **kw):
            i = pe.matmul(*args, **kw)
            if done is not None:
                i.then_inc(*filled.mark(done))
            elif owed[0]:
                i.then_inc(panel_used, owed[0])
                owed[0] = 0
            return i

        def tp(pe, *args, done=None):
            i = pe.transpose(*args)
            if done is not None:
                i.then_inc(*filled.mark(done))
            elif owed[0]:
                i.then_inc(panel_used, owed[0])
                owed[0] = 0
            return i

        def tile_of(pe, width=P):
            t = tile_no[0]
            tile_no[0] += 1
            panel, j = divmod(t, KD)
            if j == 0:
                pe.wait_ge(panel_landed[panel % RING], 16 * (panel // RING + 1))
            return ring[:, panel % RING, j, 0:width]

        def tile_done():
            if tile_no[0] % KD == 0:
                owed[0] += 1

        def pe_linear(pe, key, n, rhs, rows, ready, width=P):
            bank = banks.take(pe, (key, n))
            for k in range(rows):
                w = tile_of(pe, width)
                if n == 0 and ready:
                    pe.wait_ge(*ready(k))
                mm(pe, bank[0:width, :], lhsT=w, rhs=rhs[:, k, :], start=(k == 0), stop=(k == rows - 1),
                   done=(key, n) if k == rows - 1 else None)
                tile_done()

        def pe_natural(pe, key, n, lhs, width=P):
            bank = banks.take(pe, (key, n))[:, 0:NT * width].rearrange("p (t w) -> p t w", t=NT)
            tiles = [tile_of(pe, width) for _ in range(KD)]
            for t in range(NT):
                for k in range(KD):
                    mm(pe, bank[:, t, :], lhsT=lhs[:, k, t * P:(t + 1) * P], rhs=tiles[k], start=(k == 0),
                       stop=(k == KD - 1), done=(key, n) if (t, k) == (NT - 1, KD - 1) else None)
            tile_done()

        def act_squares(act, key, src, n, xkey, free):
            if free is not None:
                act.wait_ge(*free)
            for k in range(n):
                for w in xkey(k):
                    act.wait_ge(*w)
                act.activation(hT[:, k, :], src[:, k, :], ACT.Square).then_inc(*act_made.mark((key, "sq", k)))

        def pe_mean(pe, key, mean, ks, tag=0):
            bank = banks.take(pe, (key, "mean", tag))
            for j, k in enumerate(ks):
                pe.wait_ge(*act_made[key, "sq", k])
                mm(pe, bank[:, :], lhsT=cst(mean), rhs=hT[:, k, :], start=(j == 0), stop=(j == len(ks) - 1),
                   done=(key, "mean", tag) if j == len(ks) - 1 else None)

        def dve_inverse(dve, key, r, tag=0):
            dve.wait_ge(*filled[key, "mean", tag])
            dve.tensor_scalar(r, banks[key, "mean", tag][:, :], EPS, None, ALU.add)\
               .then_inc(*dve_made.mark((key, "eps", tag)))
            banks.drain((key, "mean", tag), "dve_made")
            dve.wait_ge(*dve_made[key, "eps", tag])
            dve.reciprocal(r, r).then_inc(*dve_made.mark((key, "inv", tag)))

        def act_root(act, key, r, tag=0):
            act.wait_ge(*dve_made[key, "inv", tag])
            act.activation(r, r, ACT.Sqrt).then_inc(*act_made.mark((key, "rstd", tag)))

        rstd = sb("rstd", [P, 2, SEQ])

        def norm(key, xkey, gain, dst, free=None, mod=None):
            def act_part(act):
                act_squares(act, key, xT, KD, xkey, free)
                act_root(act, key, rstd[:, 0, :])
                if mod is not None:
                    for k in range(KD):
                        act.wait_ge(*dve_made[key, "scaled", k])
                        act.activation(dst[:, k, :], dst[:, k, :], ACT.Identity, bias=mod[1](k))\
                           .then_inc(*act_made.mark((key, k)))

            def pe_part(pe):
                pe_mean(pe, key, "mean_d", range(KD))

            def dve_part(dve):
                dve_inverse(dve, key, rstd[:, 0, :])
                dve.wait_ge(*act_made[key, "rstd", 0])
                for k in range(KD):
                    g = col(*gain, k) if mod is None else mod[0](k)
                    dve.scalar_tensor_tensor(out=dst[:, k, :], in0=xT[:, k, :], scalar=g, in1=rstd[:, 0, :],
                                             op0=ALU.mult, op1=ALU.mult)\
                       .then_inc(*dve_made.mark((key, "scaled", k) if mod is not None else (key, k)))
            return act_part, pe_part, dve_part

        def softmax_maps(key, maps, Pb, PT, mx, sm, ready, deferred=None):
            M = len(maps)
            on_act = [i % 2 == 0 for i in range(M)]

            def pe_part(pe):
                for w in ready:
                    pe.wait_ge(*w)
                for i in range(M + 3):
                    if i < M:
                        m = maps[i]
                        bank = banks.take(pe, (key, "s", i))
                        W = m["width"]
                        extra = m["masks"]
                        mm(pe, bank[:, 0:W], lhsT=m["q"], rhs=m["k"], start=True, stop=not extra,
                           done=None if extra else (key, "s", i))
                        for j, (a, b, c, w) in enumerate(extra):
                            for wt in w:
                                pe.wait_ge(*wt)
                            mm(pe, bank[:, c:c + b.shape[-1]], lhsT=a, rhs=b, start=False, stop=j == len(extra) - 1,
                               done=(key, "s", i) if j == len(extra) - 1 else None)
                    if 2 <= i < M + 2:
                        j = i - 2
                        m = maps[j]
                        n = m["width"] // P
                        pe.wait_ge(*act_made[key, "p", j])
                        bank = banks.take(pe, (key, "t", j))
                        for t in range(n):
                            tp(pe, bank[:, t * P:(t + 1) * P], Pb[:, j % 3, t * P:(t + 1) * P], ident,
                               done=(key, "t", j) if t == n - 1 else None)
                    if i >= 3:
                        j = i - 3
                        m = maps[j]
                        n = m["width"] // P
                        pe.wait_ge(*(act_made if on_act[j] else dve_made)[key, "pt", j])
                        bank = banks.take(pe, (key, "o", j))
                        for t in range(n):
                            mm(pe, bank[:, 0:DH], lhsT=PT[:, j % 3, t * P:(t + 1) * P], rhs=m["v"](t), start=(t == 0),
                               stop=(t == n - 1), done=(key, "o", j) if t == n - 1 else None)

            def act_part(act):
                for i in range(M + 2):
                    if i < M:
                        W = maps[i]["width"]
                        act.wait_ge(*dve_made[key, "max", i])
                        if i >= 3:
                            act.wait_ge(*filled[key, "t", i - 3])
                        act.activation(Pb[:, i % 3, 0:W], banks[key, "s", i][:, 0:W], ACT.Exp, bias=mx(i),
                                       accum_out=sm(i)).then_inc(*act_made.mark((key, "p", i)))
                        banks.drain((key, "s", i), "act_made")
                    if i >= 2 and on_act[i - 2]:
                        j = i - 2
                        W = maps[j]["width"]
                        act.wait_ge(*filled[key, "t", j])
                        if j >= 3:
                            act.wait_ge(*filled[key, "o", j - 3])
                        act.activation(PT[:, j % 3, 0:W], banks[key, "t", j][:, 0:W], ACT.Copy)\
                           .then_inc(*act_made.mark((key, "pt", j)))
                        banks.drain((key, "t", j), "act_made")

            def dve_part(dve):
                for i in range(M + 3):
                    if i < M:
                        W = maps[i]["width"]
                        dve.wait_ge(*filled[key, "s", i])
                        if i >= 3:
                            dve.wait_ge(*act_made[key, "p", i - 3])
                        dve.tensor_reduce(mx(i), banks[key, "s", i][:, 0:W], AX.X, ALU.max, negate=True)\
                           .then_inc(*dve_made.mark((key, "max", i)))
                    if 1 <= i < M + 1:
                        j = i - 1
                        dve.wait_ge(*act_made[key, "p", j])
                        dve.reciprocal(sm(j), sm(j)).then_inc(*dve_made.mark((key, "inv", j)))
                        if maps[j]["gate"] is not None:
                            dve.wait_ge(*dve_made[key, "inv", j])
                            dve.tensor_tensor(sm(j), sm(j), maps[j]["gate"], ALU.mult)\
                               .then_inc(*dve_made.mark((key, "gated", j)))
                    if 2 <= i < M + 2 and not on_act[i - 2]:
                        j = i - 2
                        W = maps[j]["width"]
                        dve.wait_ge(*filled[key, "t", j])
                        if j >= 3:
                            dve.wait_ge(*filled[key, "o", j - 3])
                        dve.tensor_copy(PT[:, j % 3, 0:W], banks[key, "t", j][:, 0:W])\
                           .then_inc(*dve_made.mark((key, "pt", j)))
                        banks.drain((key, "t", j), "dve_made")
                    if i >= 3:
                        j = i - 3
                        m = maps[j]
                        dve.wait_ge(*filled[key, "o", j])
                        dve.wait_ge(*dve_made[key, "gated" if m["gate"] is not None else "inv", j])
                        o = banks[key, "o", j][:, 0:DH]
                        if m["add"] is not None:
                            dve.wait_ge(*m["add"])
                            dve.scalar_tensor_tensor(out=m["out"], in0=o, scalar=sm(j), in1=m["out"], op0=ALU.mult,
                                                     op1=ALU.add).then_inc(*dve_made.mark((key, "out", j)))
                        else:
                            dve.tensor_scalar(m["out"], o, sm(j), None, ALU.mult)\
                               .then_inc(*dve_made.mark((key, "out", j)))
                        banks.drain((key, "o", j), "dve_made")
            return act_part, pe_part, dve_part

        def turned(key, src, dst, n, waits, free=()):
            def pe_part(pe):
                for w in waits:
                    pe.wait_ge(*w)
                for k in range(n):
                    bank = banks.take(pe, (key, k))
                    for t in range(NT):
                        tp(pe, bank[:, t * P:(t + 1) * P], src[:, t, k * P:(k + 1) * P], ident,
                           done=(key, k) if t == NT - 1 else None)

            def act_part(act):
                for w in free:
                    act.wait_ge(*w)
                for k in range(0, n, 2):
                    act.wait_ge(*filled[key, k])
                    act.activation(dst[:, k, :], banks[key, k][:, :], ACT.Copy).then_inc(*act_made.mark((key, k)))
                    banks.drain((key, k), "act_made")

            def dve_part(dve):
                for w in free:
                    dve.wait_ge(*w)
                for k in range(1, n, 2):
                    dve.wait_ge(*filled[key, k])
                    dve.tensor_copy(dst[:, k, :], banks[key, k][:, :]).then_inc(*dve_made.mark((key, k)))
                    banks.drain((key, k), "dve_made")
            return act_part, pe_part, dve_part

        def turned_at(key):
            return lambda k: (act_made if k % 2 == 0 else dve_made)[key, k]

        def dve_residual(dve, key, gate=None):
            for n in range(KD):
                dve.wait_ge(*filled[key, n])
                bank = banks[key, n][:, :]
                if gate is None:
                    i = dve.tensor_tensor(xT[:, n, :], xT[:, n, :], bank, ALU.add)
                else:
                    i = dve.scalar_tensor_tensor(out=xT[:, n, :], in0=bank, scalar=gate(n), in1=xT[:, n, :],
                                                 op0=ALU.mult, op1=ALU.add)
                i.then_inc(*dve_made.mark((key, "x", n)))
                banks.drain((key, n), "dve_made")

        def x_after(key):
            return lambda k: [dve_made[key, "x", k]]

        def act_conv_start(act, key, n, cv, w, b, free):
            act.wait_ge(*filled[key, n])
            for f in free:
                act.wait_ge(*f)
            act.activation(cv, banks[key, n][:, :], ACT.Identity, bias=b, scale=w)\
               .then_inc(*act_made.mark((key, "tap", n)))

        def dve_conv_taps(dve, key, n, cv, ws):
            dve.wait_ge(*act_made[key, "tap", n])
            for j, w in enumerate(ws):
                s = j + 1
                if j:
                    dve.wait_ge(*dve_made[key, "taps", n, j - 1])
                dve.scalar_tensor_tensor(out=cv[:, s:SEQ], in0=banks[key, n][:, 0:SEQ - s], scalar=w,
                                         in1=cv[:, s:SEQ], op0=ALU.mult, op1=ALU.add)\
                   .then_inc(*dve_made.mark((key, "taps", n, j)))
            banks.drain((key, n), "dve_made")

        def rope_parts(key, n, dst, table, width=SEQ):
            perm, cos, sin = table

            def pe_part(pe):
                pe.wait_ge(*act_made[key, "raw", n])
                bank = banks.take(pe, (key, "rot", n))
                mm(pe, bank[:, 0:width], lhsT=cst(perm), rhs=dst, start=True, stop=True, done=(key, "rot", n))

            def dve_part(dve, tmp):
                dve.wait_ge(*filled[key, "rot", n])
                dve.tensor_tensor(tmp, banks[key, "rot", n][:, 0:width], cst(sin)[:, 0:width], ALU.mult)\
                   .then_inc(*dve_made.mark((key, "sin", n)))
                banks.drain((key, "rot", n), "dve_made")
                dve.tensor_tensor(dst, dst, cst(cos)[:, 0:width], ALU.mult).then_inc(*dve_made.mark((key, "cos", n)))
                dve.wait_ge(*dve_made[key, "cos", n])
                dve.tensor_tensor(dst, dst, tmp, ALU.add).then_inc(*dve_made.mark((key, "roped", n)))
            return pe_part, dve_part

        prog = {"act": [], "pe": [], "dve": [], "pool": []}

        def then(parts=None, **kw):
            if parts is not None:
                prog["act"].append(parts[0])
                prog["pe"].append(parts[1])
                prog["dve"].append(parts[2])
            for e, f in kw.items():
                prog[e].append(f)

        A = Area()
        x_nat = A.take(NT, D)

        def pe_start(pe):
            pe.wait_ge(x_landed, 16)
            pe.wait_ge(const_landed, 48)

        def all_consts(eng):
            eng.wait_ge(const_landed, 48)

        then(pe=pe_start, act=all_consts, dve=all_consts, pool=all_consts)
        then(turned("x", x_nat, xT, KD, []))

        def x0(k):
            return [turned_at("x")(k)]

        then(norm("h0", x0, ("attn_norm", 0), hT))
        A = Area()
        sq, sk = A.take(4, SEQ), A.take(4, SEQ)
        sv = A.take(NT, 512)
        nsa_at = A.at
        nq = A.take(4, SEQ)
        kvc = A.take(2, SEQ)
        ksw = A.take(2, SEQ)
        vsw = A.take(2, NT, P)
        gates = A.take(NT, 24)
        kin = A.take(2, CMP_LEN, NCMP)
        kcr = A.take(32)
        vcn = A.take(P)
        onat = A.take(NT, D)
        rtmp = A.take(2, SEQ)
        Pb, PT = A.take(3, SEQ), A.take(3, SEQ)
        cpx, cpt = A.take(256), A.take(2, SEQ)
        work = A.at
        ROPE8 = ("perm8", "cos8", "sin8")
        roped = [("ksw", 0, ksw[:, 0, :]), ("ksw", 1, ksw[:, 1, :])] + [("nq", c, nq[:, c, :]) for c in range(4)]
        ropes = [rope_parts(k, n, d, ROPE8) for k, n, d in roped]

        def h_at(key):
            return lambda k: dve_made[key, k]

        def pe_even_in(pe):
            for n in range(2):
                pe_linear(pe, "kvc", n, hT, KD, h_at("h0"))
            for i, (k, n, _) in enumerate(roped):
                pe_linear(pe, k, n, hT, KD, None)
                if i:
                    ropes[i - 1][0](pe)
            for n in range(4):
                pe_linear(pe, "sk", n, hT, KD, None)
                if n == 0:
                    ropes[-1][0](pe)
            for n in range(4):
                pe_linear(pe, "sq", n, hT, KD, None)
            for n in range(4):
                pe_natural(pe, "sv", n, hT)
            for n in range(2):
                pe_natural(pe, "vsw", n, hT)
            pe_natural(pe, "gates", 0, hT, 24)

        def act_even_in(act):
            for n in range(2):
                act.wait_ge(*filled["kvc", n])
                act.activation(kvc[:, n, :], banks["kvc", n][:, :], ACT.Copy).then_inc(*act_made.mark(("kvc", n)))
                banks.drain(("kvc", n), "act_made")
            for k, n, d in roped:
                act.wait_ge(*filled[k, n])
                act.activation(d, banks[k, n][:, :], ACT.Copy, scale=SCALE if k == "nq" else 1.0)\
                   .then_inc(*act_made.mark((k, "raw", n)))
                banks.drain((k, n), "act_made")
            for key, dst, s in (("sk", sk, 1.0), ("sq", sq, SCALE)):
                for n in range(4):
                    act.wait_ge(*filled[key, n])
                    act.activation(dst[:, n, :], banks[key, n][:, :], ACT.Copy, scale=s)\
                       .then_inc(*act_made.mark((key, n)))
                    banks.drain((key, n), "act_made")
            for key, cnt, dst in (("sv", 4, None), ("vsw", 2, None)):
                for n in range(cnt):
                    act.wait_ge(*filled[key, n])
                    d = sv[:, :, n * P:(n + 1) * P] if key == "sv" else vsw[:, n, :, :]
                    act.activation(d, banks[key, n][:, :].rearrange("p (t w) -> p t w", t=NT), ACT.Copy)\
                       .then_inc(*act_made.mark((key, n)))
                    banks.drain((key, n), "act_made")
            act.wait_ge(*filled["gates", 0])
            act.activation(gates, banks["gates", 0][:, 0:NT * 24].rearrange("p (t w) -> p t w", t=NT), ACT.Sigmoid)\
               .then_inc(*act_made.mark("gates"))
            banks.drain(("gates", 0), "act_made")

        def dve_even_in(dve):
            for n, name in enumerate(("pos_k", "pos_v")):
                dve.wait_ge(*act_made["kvc", n])
                o = VEC[name, 0]
                pos = vec[:, o:o + CMP_LEN].rearrange("p (l c) -> p l c", c=1).to_broadcast([P, CMP_LEN, NCMP])
                for half in range(2):
                    ls = slice(half * CMP_STRIDE, (half + 1) * CMP_STRIDE)
                    first = half * CMP_STRIDE
                    src = kvc[:, n, first:first + NCMP * CMP_STRIDE].rearrange("p (c l) -> p l c", l=CMP_STRIDE)
                    dve.tensor_tensor(kin[:, n, ls, :], src, pos[:, ls, :], ALU.add)\
                       .then_inc(*dve_made.mark(("kin", n, half)))
            for i, r in enumerate(ropes):
                r[1](dve, rtmp[:, i % 2, :])

        then(pe=pe_even_in, act=act_even_in, dve=dve_even_in)

        rope_c = rope_parts("kcr", 0, kcr[:, 0:NCMP], ("perm8", "cosc", "sinc"), NCMP)

        def pe_compress(pe):
            for n in range(2):
                for half in range(2):
                    pe.wait_ge(*dve_made["kin", n, half])
                bank = banks.take(pe, ("cmp", n))
                for l in range(CMP_LEN):
                    w = tile_of(pe)
                    a, b = (w, kin[:, n, l, :]) if n == 0 else (kin[:, n, l, :], w)
                    mm(pe, bank[:, 0:NCMP] if n == 0 else bank[0:NCMP, 0:P], lhsT=a, rhs=b, start=(l == 0),
                       stop=(l == CMP_LEN - 1), done=("cmp", n) if l == CMP_LEN - 1 else None)
                    tile_done()
            rope_c[0](pe)

        def act_compress(act):
            act.wait_ge(*filled["cmp", 0])
            act.activation(kcr[:, 0:NCMP], banks["cmp", 0][:, 0:NCMP], ACT.Copy)\
               .then_inc(*act_made.mark(("kcr", "raw", 0)))
            banks.drain(("cmp", 0), "act_made")
            act.wait_ge(*filled["cmp", 1])
            act.activation(vcn[0:NCMP, :], banks["cmp", 1][0:NCMP, 0:P], ACT.Copy).then_inc(*act_made.mark("vcn"))
            banks.drain(("cmp", 1), "act_made")

        def dve_compress(dve):
            rope_c[1](dve, rtmp[:, 0, 0:NCMP])

        then(pe=pe_compress, act=act_compress, dve=dve_compress)

        nmax, den, dzero = small[:, 0:8], small[:, 8:16], small[:, 16:24]

        def by_head(a, w=32):
            return a.rearrange("p (h c) -> p h c", h=8)

        def pe_cmp(pe):
            pe.wait_ge(*dve_made["kcr", "roped", 0])
            pe.wait_ge(*dve_made["nq", "roped", 3])
            pe.wait_ge(*act_made["vcn"])
            for qt in range(NT):
                for g in range(2):
                    r = slice(DH * g, DH * g + DH)
                    bank = banks.take(pe, ("cs", qt, g))
                    mm(pe, bank[:, 0:P], lhsT=identb, rhs=cstb("cmp")[:, qt * P:(qt + 1) * P], start=True, stop=False)
                    for c in range(4):
                        mm(pe, bank[:, 32 * c:32 * c + NCMP], lhsT=nq[r, c, qt * P:(qt + 1) * P], rhs=kcr[r, 0:NCMP],
                           start=False, stop=(c == 3), done=("cs", qt, g) if c == 3 else None)
                pe.wait_ge(*dve_made["c01", qt])
                for half in range(2):
                    bank = banks.take(pe, ("ct", qt, half))
                    for j in range(4):
                        h = 4 * half + j
                        tp(pe, bank[0:32, j * P:(j + 1) * P], cpx[:, 32 * h:32 * h + 32], ident,
                           done=("ct", qt, half) if j == 3 else None)
                bank = banks.take(pe, ("co", qt))
                for h in range(8):
                    if h % 4 == 0:
                        pe.wait_ge(*act_made["cpt", qt, h // 4])
                    g = h // 4
                    mm(pe, bank[:, h * DH:(h + 1) * DH], lhsT=cpt[0:NCMP, h // 4, (h % 4) * P:(h % 4 + 1) * P],
                       rhs=vcn[0:NCMP, g * DH:(g + 1) * DH], start=True, stop=True,
                       done=("co", qt) if h == 7 else None)

        def act_cmp(act):
            for qt in range(NT):
                act.wait_ge(*dve_made["csub", qt, 1])
                act.activation(cpx, cpx, ACT.Exp).then_inc(*act_made.mark(("cexp", qt)))
                for half in range(2):
                    act.wait_ge(*filled["ct", qt, half])
                    if qt:
                        act.wait_ge(*filled["co", qt - 1])
                    act.activation(cpt[0:32, half, :], banks["ct", qt, half][0:32, :], ACT.Copy)\
                       .then_inc(*act_made.mark(("cpt", qt, half)))
                    banks.drain(("ct", qt, half), "act_made")

        def dve_cmp(dve):
            for qt in range(NT):
                if qt:
                    dve.wait_ge(*filled["ct", qt - 1, 1])
                for g in range(2):
                    dve.wait_ge(*filled["cs", qt, g])
                    bank = banks["cs", qt, g][:, 0:P].rearrange("p (h c) -> p h c", h=4)
                    mine = nmax[:, 4 * g:4 * g + 4]
                    dve.tensor_reduce(mine, bank, AX.X, ALU.max, negate=True)\
                       .then_inc(*dve_made.mark(("cmax", qt, g)))
                    dve.wait_ge(*dve_made["cmax", qt, g])
                    dve.tensor_tensor(cpx[:, P * g:P * g + P].rearrange("p (h c) -> p h c", h=4), bank,
                                      mine.rearrange("p (h c) -> p h c", c=1).to_broadcast([P, 4, 32]), ALU.add)\
                       .then_inc(*dve_made.mark(("csub", qt, g)))
                    banks.drain(("cs", qt, g), "dve_made")
                dve.wait_ge(*act_made["cexp", qt])
                o = CF["cmp01"][0] + 32 * qt
                seen = cf[:, o:o + 32].rearrange("p (h c) -> p h c", h=1).to_broadcast([P, 8, 32])
                dve.tensor_tensor(by_head(cpx), by_head(cpx), seen, ALU.mult).then_inc(*dve_made.mark(("c01", qt)))
                dve.wait_ge(*dve_made["c01", qt])
                dve.tensor_reduce(den, by_head(cpx), AX.X, ALU.add).then_inc(*dve_made.mark(("cden", qt)))
                dve.wait_ge(*dve_made["cden", qt])
                dve.tensor_scalar(dzero, den, 0.0, None, ALU.is_equal).then_inc(*dve_made.mark(("cz", qt)))
                dve.wait_ge(*dve_made["cz", qt])
                dve.tensor_tensor(den, den, dzero, ALU.add).then_inc(*dve_made.mark(("cd1", qt)))
                dve.wait_ge(*dve_made["cd1", qt])
                dve.reciprocal(den, den).then_inc(*dve_made.mark(("cinv", qt)))
                dve.wait_ge(*dve_made["cinv", qt])
                if qt == 0:
                    dve.wait_ge(*act_made["gates"])
                dve.tensor_tensor(den, den, gates[:, qt, 0:24:3], ALU.mult).then_inc(*dve_made.mark(("cg", qt)))
                dve.wait_ge(*dve_made["cg", qt])
                dve.wait_ge(*filled["co", qt])
                dve.tensor_tensor(onat[:, qt, 512:1024].rearrange("p (h c) -> p h c", h=8),
                                  by_head(banks["co", qt][:, :]),
                                  den.rearrange("p (h c) -> p h c", c=1).to_broadcast([P, 8, DH]), ALU.mult)\
                   .then_inc(*dve_made.mark(("cout", qt)))
                banks.drain(("co", qt), "dve_made")

        then(pe=pe_cmp, act=act_cmp, dve=dve_cmp)

        def small_cols(base, i, n=3):
            return small[:, base + i % n:base + i % n + 1]

        maps = []
        for b in range(2):
            for h in range(8):
                g, c = divmod(h, 4)
                r = slice(DH * g, DH * g + DH)
                for qt in range(NT):
                    W = (qt + 1) * P
                    maps.append(dict(
                        q=nq[r, c, qt * P:W], k=ksw[r, b, 0:W], width=W,
                        masks=[(identb, cstb("causal"), qt * P, ())],
                        v=lambda t, b=b, g=g: vsw[:, b, t, g * DH:(g + 1) * DH],
                        out=onat[:, qt, 512 + h * DH:512 + (h + 1) * DH],
                        gate=gates[:, qt, 3 * h + 1 + b:3 * h + 2 + b],
                        add=dve_made["cout", qt] if b == 0 else dve_made["nsa", "out", h * NT + qt]))
        then(softmax_maps("nsa", maps, Pb, PT, lambda i: small_cols(32, i), lambda i: small_cols(36, i, 6),
                          [act_made["vsw", 1], dve_made["nq", "roped", 3]]))

        A = Area(nsa_at)
        za = A.take(2, SEQ)
        sp = A.take(2, NT, SEQ)
        aa = A.take(NT, SEQ)

        def pe_sb(pe):
            pe.wait_ge(*act_made["sv", 3])

            def scores(h):
                r = slice(DH * (h % 2), DH * (h % 2) + DH)
                for kt in range(NT - 1, -1, -1):
                    bank = banks.take(pe, ("z", h, kt))
                    mm(pe, bank[:, kt * P:SEQ], lhsT=sk[r, h // 2, kt * P:(kt + 1) * P], rhs=sq[r, h // 2, kt * P:SEQ],
                       start=True, stop=True, done=("z", h, kt))

            def sums(h):
                for kt in range(NT - 1, -1, -1):
                    bank = banks["z", h, kt]
                    pe.wait_ge(*pool_made["sp", h, kt])
                    mm(pe, bank[:, kt * P:(kt + 1) * P], lhsT=identb, rhs=cstb("strictT"), start=False, stop=False,
                       skip_group_check=True)
                    mm(pe, bank[:, kt * P:SEQ], lhsT=cst("tri"), rhs=sp[:, h % 2, kt, kt * P:SEQ], start=False,
                       stop=(kt == NT - 1), skip_group_check=True, done=("r", h, kt) if kt == NT - 1 else None)
                    for jt in range(kt + 1, NT):
                        mm(pe, bank[:, jt * P:SEQ], lhsT=cst("nones"), rhs=sp[:, h % 2, jt, jt * P:SEQ], start=False,
                           stop=(jt == NT - 1), skip_group_check=True, done=("r", h, kt) if jt == NT - 1 else None)

            def values(h):
                for kt in range(NT):
                    pe.wait_ge(*act_made["a", h, kt])
                bank = banks.take(pe, ("so", h))
                for qt in range(NT):
                    for kt in range(qt + 1):
                        mm(pe, bank[:, qt * DH:(qt + 1) * DH], lhsT=aa[:, kt, qt * P:(qt + 1) * P],
                           rhs=sv[:, kt, h * DH:(h + 1) * DH], start=(kt == 0), stop=(kt == qt),
                           done=("so", h) if (qt, kt) == (NT - 1, NT - 1) else None)

            scores(0)
            for h in range(8):
                sums(h)
                if h + 1 < 8:
                    scores(h + 1)
                values(h)

        def act_sb(act):
            act.wait_ge(*filled["nsa", "o", 63])
            for h in range(8):
                for kt in range(NT - 1, -1, -1):
                    b = kt % 2
                    z = banks["z", h, kt][:, kt * P:SEQ]
                    t = za[:, b, kt * P:SEQ]
                    act.wait_ge(*filled["z", h, kt])
                    if h or kt < NT - 2:
                        prev = (h, kt + 2) if kt + 2 < NT else (h - 1, kt - 2)
                        act.wait_ge(*dve_made["sp0", prev[0], prev[1]])
                    act.activation(t, z, ACT.Abs).then_inc(*act_made.mark(("z1", h, kt)))
                    act.wait_ge(*act_made["z1", h, kt])
                    act.activation(t, t, ACT.Exp, scale=-1.0).then_inc(*act_made.mark(("z2", h, kt)))
                    act.wait_ge(*act_made["z2", h, kt])
                    act.activation(t, t, ACT.Ln, bias=1.0).then_inc(*act_made.mark(("z3", h, kt)))
                for kt in range(NT - 1, -1, -1):
                    act.wait_ge(*filled["r", h, kt])
                    if h:
                        act.wait_ge(*filled["so", h - 1])
                    act.activation(aa[:, kt, kt * P:SEQ], banks["z", h, kt][:, kt * P:SEQ], ACT.Exp)\
                       .then_inc(*act_made.mark(("a", h, kt)))
                    banks.drain(("z", h, kt), "act_made")

        def dve_sb(dve):
            for h in range(8):
                for kt in range(NT - 1, -1, -1):
                    dve.wait_ge(*act_made["z3", h, kt])
                    if h >= 2:
                        dve.wait_ge(*filled["r", h - 2, 0])
                    dve.scalar_tensor_tensor(out=sp[:, h % 2, kt, kt * P:SEQ], in0=banks["z", h, kt][:, kt * P:SEQ],
                                             scalar=0.0, in1=za[:, kt % 2, kt * P:SEQ], op0=ALU.max, op1=ALU.add)\
                       .then_inc(*dve_made.mark(("sp0", h, kt)))
                dve.wait_ge(*filled["so", h])
                dve.tensor_copy(onat[:, :, h * DH:(h + 1) * DH],
                                banks["so", h][:, 0:NT * DH].rearrange("p (t c) -> p t c", t=NT))\
                   .then_inc(*dve_made.mark(("sbout", h)))
                banks.drain(("so", h), "dve_made")

        def pool_sb(pool):
            for h in range(8):
                for kt in range(NT - 1, -1, -1):
                    pool.wait_ge(*dve_made["sp0", h, kt])
                    d = sp[:, h % 2, kt, kt * P:(kt + 1) * P]
                    pool.tensor_tensor(d, d, cst("strict"), ALU.mult).then_inc(*pool_made.mark(("sp", h, kt)))

        then(pe=pe_sb, act=act_sb, dve=dve_sb, pool=pool_sb)

        A = Area(work)
        oT = A.take(KD, SEQ)
        free = [filled["so", 7]]
        then(turned("ot0", onat, oT, KD, [dve_made["sbout", 7], dve_made["nsa", "out", 63]], free))

        def out_linear(key, src, ready):
            def pe_part(pe):
                for n in range(KD):
                    pe_linear(pe, key, n, src, KD, ready)
            return pe_part

        then(pe=out_linear("mix0", oT, turned_at("ot0")), dve=lambda dve: dve_residual(dve, "mix0"))

        def ffn(layer, xkey, hfree, arena_free):
            key = f"f{layer}"
            then(norm(key, x_after(xkey), ("ffn_norm", layer), hT, hfree))
            A = Area()
            gT = A.take(FC, SEQ)
            cv = A.take(3, SEQ)
            sl = A.take(3, SEQ)

            def pe_part(pe):
                for n in range(FC):
                    pe_linear(pe, (key, "a"), n, hT, KD, h_at(key))
                    pe_linear(pe, (key, "b"), n, hT, KD, None)
                for n in range(KD):
                    pe_linear(pe, (key, "y"), n, gT, FC, lambda k: dve_made[key, "g", k])

            def act_part(act):
                act.wait_ge(*arena_free)
                for n in range(FC):
                    free = [act_made[(key, "a"), "silu", n - 3]] if n >= 3 else []
                    act_conv_start(act, (key, "a"), n, cv[:, n % 3, :], col("conv_w", (layer, 2), n),
                                   col("conv_b", layer, n), free)
                    act.wait_ge(*dve_made[(key, "a"), "taps", n, 1])
                    if n >= 3:
                        act.wait_ge(*dve_made[key, "g", n - 3])
                    act.activation(sl[:, n % 3, :], cv[:, n % 3, :], ACT.Silu)\
                       .then_inc(*act_made.mark(((key, "a"), "silu", n)))

            def dve_part(dve):
                for n in range(FC):
                    dve_conv_taps(dve, (key, "a"), n, cv[:, n % 3, :],
                                  [col("conv_w", (layer, 1), n), col("conv_w", (layer, 0), n)])
                    dve.wait_ge(*act_made[(key, "a"), "silu", n])
                    dve.wait_ge(*filled[(key, "b"), n])
                    dve.tensor_tensor(gT[:, n, :], sl[:, n % 3, :], banks[(key, "b"), n][:, :], ALU.mult)\
                       .then_inc(*dve_made.mark((key, "g", n)))
                    banks.drain(((key, "b"), n), "dve_made")
                dve_residual(dve, (key, "y"))

            then(pe=pe_part, act=act_part, dve=dve_part)
            return (key, "y")

        x1 = ffn(0, "mix0", filled["gates", 0], filled["mix0", KD - 1])

        then(norm("h1", x_after(x1), ("attn_norm", 1), hT, filled[("f0", "b"), FC - 1]))
        A = Area()
        q1, k1 = A.take(KD, SEQ), A.take(KD, SEQ)
        v1 = A.take(NT, D)
        onat1 = A.take(NT, D)
        Pb1, PT1 = A.take(3, SEQ), A.take(3, SEQ)
        ff, lf, cum = A.take(SEQ), A.take(SEQ), A.take(SEQ)
        parts3 = A.take16(SEQ)
        rest, rest2 = A.take(SEQ), A.take(SEQ)
        oT1 = A.take(KD, SEQ)

        def pe_odd_in(pe):
            pe_linear(pe, "f", 0, hT, KD, h_at("h1"), 16)
            for key in ("q1", "k1"):
                for n in range(KD):
                    pe_linear(pe, key, n, hT, KD, None)
            for n in range(KD):
                pe_natural(pe, "v1", n, hT)

        def act_odd_in(act):
            act.wait_ge(*filled[("f0", "y"), KD - 1])
            f16 = ff[0:16, :]
            act.wait_ge(*dve_made["f+b"])
            act.activation(lf[0:16, :], f16, ACT.Abs).then_inc(*act_made.mark("f1"))
            act.wait_ge(*act_made["f1"])
            act.activation(lf[0:16, :], lf[0:16, :], ACT.Exp, scale=-1.0).then_inc(*act_made.mark("f2"))
            act.wait_ge(*act_made["f2"])
            act.activation(lf[0:16, :], lf[0:16, :], ACT.Ln, bias=1.0).then_inc(*act_made.mark("f3"))
            for key, dst, s in (("q1", q1, SCALE), ("k1", k1, 1.0)):
                for n in range(KD):
                    act.wait_ge(*filled[key, n])
                    act.activation(dst[:, n, :], banks[key, n][:, :], ACT.Copy, scale=s)\
                       .then_inc(*act_made.mark((key, n)))
                    banks.drain((key, n), "act_made")
            for n in range(KD):
                act.wait_ge(*filled["v1", n])
                act.activation(v1[:, :, n * P:(n + 1) * P], banks["v1", n][:, :].rearrange("p (t w) -> p t w", t=NT),
                               ACT.Copy).then_inc(*act_made.mark(("v1", n)))
                banks.drain(("v1", n), "act_made")

        def dve_odd_in(dve):
            dve.wait_ge(*filled["f", 0])
            dve.wait_ge(*filled[("f0", "y"), KD - 1])
            dve.tensor_scalar(ff[0:16, :], banks["f", 0][0:16, :], col("b_f", 0, 0, 16), None, ALU.add)\
               .then_inc(*dve_made.mark("f+b"))
            banks.drain(("f", 0), "dve_made")
            dve.memset(parts3[0:96, :], 0.0).then_inc(*dve_made.mark("p0"))
            dve.wait_ge(*act_made["f3"])
            dve.scalar_tensor_tensor(out=lf[0:16, :], in0=ff[0:16, :], scalar=0.0, in1=lf[0:16, :], op0=ALU.min,
                                     op1=ALU.subtract).then_inc(*dve_made.mark("lf"))
            dve.wait_ge(*dve_made["lf"])
            dve.tensor_tensor_scan(cum[0:16, :], cst("ones")[0:16, :], lf[0:16, :], 0.0, ALU.mult, ALU.add)\
               .then_inc(*dve_made.mark("cum"))
            dve.wait_ge(*dve_made["cum"])
            dve.tensor_copy(parts3[0:16, :], cum[0:16, :]).then_inc(*dve_made.mark("hi"))
            dve.wait_ge(*dve_made["hi"])
            dve.tensor_tensor(rest[0:16, :], cum[0:16, :], parts3[0:16, :], ALU.subtract)\
               .then_inc(*dve_made.mark("rest"))
            dve.wait_ge(*dve_made["rest"])
            dve.tensor_copy(rest2[0:16, :].bitcast(BF16)[:, 0:SEQ], rest[0:16, :]).then_inc(*dve_made.mark("mid"))
            dve.wait_ge(*dve_made["mid"])
            dve.tensor_copy(parts3[32:48, :], rest2[0:16, :].bitcast(BF16)[:, 0:SEQ]).then_inc(*dve_made.mark("midp"))
            dve.tensor_tensor(rest[0:16, :], rest[0:16, :], rest2[0:16, :].bitcast(BF16)[:, 0:SEQ], ALU.subtract)\
               .then_inc(*dve_made.mark("rest2"))
            dve.wait_ge(*dve_made["rest2"])
            dve.tensor_copy(parts3[64:80, :], rest[0:16, :]).then_inc(*dve_made.mark("lo"))

        then(pe=pe_odd_in, act=act_odd_in, dve=dve_odd_in)

        maps = []
        for h in range(16):
            r = slice(DH * (h % 2), DH * (h % 2) + DH)
            for qt in range(NT):
                W = (qt + 1) * P
                maps.append(dict(
                    q=q1[r, h // 2, qt * P:W], k=k1[r, h // 2, 0:W], width=W,
                    masks=[(cstb("selneg")[0:96, h * P:(h + 1) * P], parts3[0:96, 0:W], 0, ()),
                           (identb, cstb("causal"), qt * P, ())],
                    v=lambda t, h=h: v1[:, t, h * DH:(h + 1) * DH],
                    out=onat1[:, qt, h * DH:(h + 1) * DH], gate=None, add=None))
        then(softmax_maps("fox", maps, Pb1, PT1, lambda i: small_cols(32, i), lambda i: small_cols(36, i, 6),
                          [act_made["v1", KD - 1], dve_made["lo"]]))
        then(turned("ot1", onat1, oT1, KD, [dve_made["fox", "out", 63]]))
        then(pe=out_linear("mix1", oT1, turned_at("ot1")), dve=lambda dve: dve_residual(dve, "mix1"))
        x2 = ffn(1, "mix1", filled["v1", KD - 1], filled["mix1", KD - 1])

        then(norm("xn", x_after(x2), ("final_norm", 0), xT, filled[("f1", "b"), FC - 1]))

        csil, mod, gsc = small[:, 64:72], small[:, 80:128], small[:, 128:144]

        def act_mod(act):
            act.activation(csil, vec[:, VEC["c", 0]:VEC["c", 0] + KD], ACT.Silu).then_inc(*act_made.mark("csil"))

        def pe_mod(pe):
            pe.wait_ge(*act_made["csil"])
            for l in range(LAYERS):
                bank = banks.take(pe, ("mod", l))
                for n in range(24):
                    for k in range(KD):
                        w = tile_of(pe)
                        mm(pe, bank[:, n:n + 1], lhsT=w, rhs=csil[:, k:k + 1], start=(k == 0), stop=(k == KD - 1),
                           done=("mod", l) if (n, k) == (23, KD - 1) else None)
                        tile_done()

        def dve_mod(dve):
            for l in range(LAYERS):
                dve.wait_ge(*filled["mod", l])
                o = VEC["b_ada", l]
                dve.tensor_tensor(mod[:, 24 * l:24 * l + 24], banks["mod", l][:, 0:24], vec[:, o:o + 24], ALU.add)\
                   .then_inc(*dve_made.mark(("mod", l)))
                banks.drain(("mod", l), "dve_made")
                dve.wait_ge(*dve_made["mod", l])
                o = VEC["norm_g", l]
                dve.scalar_tensor_tensor(out=gsc[:, 8 * l:8 * l + 8], in0=mod[:, 24 * l + 8:24 * l + 16], scalar=1.0,
                                         in1=vec[:, o:o + 8], op0=ALU.add, op1=ALU.mult)\
                   .then_inc(*dve_made.mark(("gsc", l)))
                dve.wait_ge(*dve_made["gsc", l])

        then(act=act_mod, pe=pe_mod, dve=dve_mod)

        ROPE32 = ("perm32", "cos32", "sin32")

        def block2(l, xkey, hfree, arena_free):
            K = f"L{l}"
            hk = K + "h"
            then(norm(hk, xkey, None, hT, hfree,
                      mod=(lambda k: gsc[:, 8 * l + k:8 * l + k + 1],
                           lambda k: mod[:, 24 * l + k:24 * l + k + 1])))
            A = Area()
            qi, ki = A.take(2, SEQ), A.take(SEQ)
            q, k_ = A.take(4, SEQ), A.take(SEQ)
            v = A.take(NT, DH)
            wi = A.take(NT, 4)
            xbc = A.take(12, SEQ)
            rtmp = A.take(2, SEQ)
            oT = A.take(4, SEQ)
            mask = A.take16(3 * SEQ)
            dts = A.take(4, SEQ)
            tops = A.take(16, 8)
            work = A.at
            score = A.take(3, SEQ)
            relu = A.take(2, SEQ)
            onat = A.take(NT, 512)
            Pb, PT = A.take(3, SEQ), A.take(3, SEQ)
            cvb = A.take(3, SEQ)

            roped = [(K + "qi", n, qi[:, n, :]) for n in range(2)] + [(K + "ki", 0, ki)] \
                + [(K + "q", n, q[:, n, :]) for n in range(4)] + [(K + "k", 0, k_)]
            ropes = [rope_parts(a, n, d, ROPE32) for a, n, d in roped]
            xw = lambda j, n: col("xconv_w", (l, j), n)

            def ready(k):
                return act_made[hk, k]

            def pe_in(pe):
                for i in range(3):
                    pe_linear(pe, roped[i][0], roped[i][1], hT, KD, ready)
                    if i:
                        ropes[i - 1][0](pe)
                pe_natural(pe, K + "wi", 0, hT, 4)
                ropes[2][0](pe)
                for i in range(3, 8):
                    pe_linear(pe, roped[i][0], roped[i][1], hT, KD, None)
                    if i > 3:
                        ropes[i - 1][0](pe)
                pe_natural(pe, K + "v", 0, hT, DH)
                ropes[7][0](pe)
                pe_linear(pe, K + "dt", 0, hT, KD, None, 16)
                for n in range(12):
                    pe_linear(pe, K + "xbc", n, hT, KD, None)

            def act_in(act):
                act.wait_ge(*arena_free)

                def raw(i):
                    a, n, d = roped[i]
                    act.wait_ge(*filled[a, n])
                    act.activation(d, banks[a, n][:, :], ACT.Copy, scale=SCALE if a == K + "q" else 1.0)\
                       .then_inc(*act_made.mark((a, "raw", n)))
                    banks.drain((a, n), "act_made")
                for i in range(3):
                    raw(i)
                act.wait_ge(*filled[K + "wi", 0])
                act.activation(wi, banks[K + "wi", 0][:, 0:16].rearrange("p (t w) -> p t w", t=NT), ACT.Copy,
                               scale=0.5).then_inc(*act_made.mark(K + "wi"))
                banks.drain((K + "wi", 0), "act_made")
                for i in range(3, 8):
                    raw(i)
                act.wait_ge(*filled[K + "v", 0])
                act.activation(v, banks[K + "v", 0][:, 0:NT * DH].rearrange("p (t w) -> p t w", t=NT), ACT.Copy)\
                   .then_inc(*act_made.mark(K + "v"))
                banks.drain((K + "v", 0), "act_made")
                t = dts[0:16, 1, :]
                act.wait_ge(*dve_made[K + "dtb"])
                act.activation(t, dts[0:16, 0, :], ACT.Abs).then_inc(*act_made.mark(K + "d1"))
                act.wait_ge(*act_made[K + "d1"])
                act.activation(t, t, ACT.Exp, scale=-1.0).then_inc(*act_made.mark(K + "d2"))
                act.wait_ge(*act_made[K + "d2"])
                act.activation(t, t, ACT.Ln, bias=1.0).then_inc(*act_made.mark(K + "d3"))
                act.activation(small[0:16, 160:161], col("a_log", l, 0, 16), ACT.Exp)\
                   .then_inc(*act_made.mark(K + "ea"))
                for n in range(12):
                    free = [act_made[K + "xbc", "silu", n - 3]] if n >= 3 else []
                    act_conv_start(act, K + "xbc", n, cvb[:, n % 3, :], xw(3, n), col("xconv_b", l, n), free)
                    act.wait_ge(*dve_made[K + "xbc", "taps", n, 2])
                    act.activation(xbc[:, n, :], cvb[:, n % 3, :], ACT.Silu)\
                       .then_inc(*act_made.mark((K + "xbc", "silu", n)))
                for t in range(NT):
                    s = slice(t * P, (t + 1) * P)
                    act.wait_ge(*dve_made[K + "acs", t])
                    act.activation(dts[0:16, 2, s], dts[0:16, 3, s], ACT.Exp, scale=-1.0,
                                   bias=dts[0:16, 3, t * P + P - 1:t * P + P]).then_inc(*act_made.mark((K + "ds", t)))

            def dve_in(dve):
                dve.wait_ge(*arena_free)
                for i in range(8):
                    ropes[i][1](dve, rtmp[:, i % 2, :])
                dve.wait_ge(*filled[K + "dt", 0])
                dt, t, acs = dts[0:16, 0, :], dts[0:16, 1, :], dts[0:16, 3, :]
                dve.tensor_scalar(dt, banks[K + "dt", 0][0:16, :], col("dt_bias", l, 0, 16), None, ALU.add)\
                   .then_inc(*dve_made.mark(K + "dtb"))
                banks.drain((K + "dt", 0), "dve_made")
                dve.wait_ge(*act_made[K + "ea"])
                dve.scalar_tensor_tensor(out=dt, in0=dt, scalar=0.0, in1=t, op0=ALU.max, op1=ALU.add)\
                   .then_inc(*dve_made.mark(K + "dt"))
                dve.wait_ge(*dve_made[K + "dt"])
                dve.tensor_scalar(t, dt, small[0:16, 160:161], -1.0, ALU.mult, ALU.mult)\
                   .then_inc(*dve_made.mark(K + "adt"))
                dve.wait_ge(*dve_made[K + "adt"])
                for c in range(NT):
                    s = slice(c * P, (c + 1) * P)
                    dve.tensor_tensor_scan(acs[:, s], cst("ones")[0:16, s], t[:, s], 0.0, ALU.mult, ALU.add)\
                       .then_inc(*dve_made.mark((K + "acs", c)))
                for n in range(12):
                    dve_conv_taps(dve, K + "xbc", n, cvb[:, n % 3, :], [xw(2, n), xw(1, n), xw(0, n)])

            then(pe=pe_in, act=act_in, dve=dve_in)

            def pe_index(pe):
                pe.wait_ge(*dve_made[K + "ki", "roped", 0])
                for qt in range(1, NT):
                    W = (qt + 1) * P
                    for h in range(4):
                        r = slice(DH * (h % 2), DH * (h % 2) + DH)
                        bank = banks.take(pe, (K + "ix", qt, h))
                        mm(pe, bank[:, 0:W], lhsT=qi[r, h // 2, qt * P:W], rhs=ki[r, 0:W], start=True, stop=True,
                           done=(K + "ix", qt, h))

            def act_index(act):
                for qt in range(1, NT):
                    W = (qt + 1) * P
                    for h in range(4):
                        i = (qt - 1) * 4 + h
                        act.wait_ge(*filled[K + "ix", qt, h])
                        if i >= 2:
                            act.wait_ge(*dve_made[K + "sc", (i - 2) // 4 + 1, (i - 2) % 4])
                        act.activation(relu[:, i % 2, 0:W], banks[K + "ix", qt, h][:, 0:W], ACT.Relu, scale=SCALE)\
                           .then_inc(*act_made.mark((K + "relu", qt, h)))
                        banks.drain((K + "ix", qt, h), "act_made")

            def dve_index(dve):
                for qt in range(1, NT):
                    W = (qt + 1) * P
                    sc = score[:, qt - 1, 0:W]
                    for h in range(4):
                        i = (qt - 1) * 4 + h
                        dve.wait_ge(*act_made[K + "relu", qt, h])
                        w = wi[:, qt, h:h + 1]
                        if h == 0:
                            j = dve.tensor_scalar(sc, relu[:, i % 2, 0:W], w, None, ALU.mult)
                        else:
                            dve.wait_ge(*dve_made[K + "sc", qt, h - 1])
                            j = dve.scalar_tensor_tensor(out=sc, in0=relu[:, i % 2, 0:W], scalar=w, in1=sc,
                                                         op0=ALU.mult, op1=ALU.add)
                        j.then_inc(*dve_made.mark((K + "sc", qt, h)))
                for qt in range(1, NT):
                    W = (qt + 1) * P
                    sc = score[:, qt - 1, 0:W]
                    dve.wait_ge(*pool_made[K + "adm", qt])
                    for r in range(TOPK // 8):
                        if r:
                            dve.wait_ge(*dve_made[K + "rep", qt, r - 1])
                        dve.max(tops[:, r, :], sc).then_inc(*dve_made.mark((K + "top", qt, r)))
                        dve.wait_ge(*dve_made[K + "top", qt, r])
                        dve.match_replace(sc, tops[:, r, :], sc, TAKEN).then_inc(*dve_made.mark((K + "rep", qt, r)))
                    dve.wait_ge(*dve_made[K + "rep", qt, TOPK // 8 - 1])
                    dve.tensor_scalar(mask[:, (qt - 1) * SEQ:(qt - 1) * SEQ + W], sc, TAKEN / 2, NEG, ALU.is_gt,
                                      ALU.mult).then_inc(*dve_made.mark((K + "mask", qt)))

            def pool_index(pool):
                for qt in range(1, NT):
                    d = score[:, qt - 1, qt * P:(qt + 1) * P]
                    pool.wait_ge(*dve_made[K + "sc", qt, 3])
                    pool.affine_select(out=d, in_=d, compare_op=ALU.is_ge, fill=NEG, base=0, pattern=[[-1, P]],
                                       channel_multiplier=1).then_inc(*pool_made.mark((K + "adm", qt)))

            then(pe=pe_index, act=act_index, dve=dve_index, pool=pool_index)

            maps = []
            for h in range(8):
                r = slice(DH * (h % 2), DH * (h % 2) + DH)
                for qt in range(NT):
                    W = (qt + 1) * P
                    if qt == 0:
                        ms = [(identb, cstb("causal"), 0, ())]
                    else:
                        ms = [(identb, mask[:, (qt - 1) * SEQ:(qt - 1) * SEQ + W], 0, (dve_made[K + "mask", qt],))]
                    maps.append(dict(q=q[r, h // 2, qt * P:W], k=k_[r, 0:W], width=W, masks=ms,
                                     v=lambda t: v[:, t, :], out=onat[:, qt, h * DH:(h + 1) * DH],
                                     gate=None, add=None))
            then(softmax_maps(K + "dsa", maps, Pb, PT, lambda i: small_cols(32, i), lambda i: small_cols(36, i, 6),
                              [act_made[K + "v"], dve_made[K + "k", "roped", 0]]))
            then(turned(K + "ot", onat, oT, 4, [dve_made[K + "dsa", "out", 31]]))

            A = Area(work)
            xd = A.take(NT, D)
            bn = A.take(NT, 256)
            cbt = A.take(2, SEQ)
            st = A.take(3, D)
            B = Area()
            xds, eb, dg, ce = (B.take(2, SEQ) for _ in range(4))
            natd = A.take(3, NT, 16)
            lastd = A.take(16, NT)
            cd = A.take(16, NT)
            after_att = [filled[K + "ot", 3]]
            gla, gls, mg = None, None, None

            def pe_ssd(pe):
                for n in range(12):
                    pe.wait_ge(*act_made[K + "xbc", "silu", n])
                for t in range(NT):
                    pe.wait_ge(*act_made[K + "ds", t])
                bank = banks.take(pe, (K + "nat", 0))
                for j, row in enumerate((0, 3, 2)):
                    for t in range(NT):
                        o = (j * NT + t) * 16
                        tp(pe, bank[:, o:o + 16], dts[0:16, row, t * P:(t + 1) * P], ident[0:16, 0:16],
                           done=(K + "nat", 0) if (j, t) == (2, NT - 1) else None)
                pe.wait_ge(*dve_made[K + "lastd"])
                bank = banks.take(pe, (K + "last", 0))
                mm(pe, bank[:, 0:16 * NT], lhsT=cst("ones")[0:16, 0:P], rhs=lastd[0:16, :, :].rearrange("p a b -> p (a b)"),
                   start=True, stop=True, done=(K + "last", 0))
                for g in range(2):
                    bank = banks.take(pe, (K + "cb", g))
                    for t in range(NT):
                        s = slice(t * P, (t + 1) * P)
                        mm(pe, bank[:, s], lhsT=xbc[:, 8 + g, s], rhs=xbc[:, 10 + g, s], start=True, stop=True,
                           done=(K + "cb", g) if t == NT - 1 else None)
                    bank = banks.take(pe, (K + "bn", g))
                    for t in range(NT):
                        s = slice(t * P, (t + 1) * P)
                        tp(pe, bank[:, s], xbc[:, 8 + g, s], ident, done=(K + "bn", g) if t == NT - 1 else None)
                for t in range(NT):
                    for half in range(2):
                        bank = banks.take(pe, (K + "xt", t, half))
                        for j in range(4):
                            tp(pe, bank[:, j * P:(j + 1) * P], xbc[:, half * 4 + j, t * P:(t + 1) * P], ident,
                               done=(K + "xt", t, half) if j == 3 else None)
                for g in range(2):
                    pe.wait_ge(*act_made[K + "bn", g])
                for t in range(NT - 1):
                    for g in range(2):
                        pe.wait_ge(*dve_made[K + "xds", t, g])
                        bank = banks.take(pe, (K + "st", t, g))
                        mm(pe, bank[:, :], lhsT=bn[:, t, g * P:(g + 1) * P], rhs=xds[:, g, :], start=True, stop=True,
                           done=(K + "st", t, g))

                def spread(h):
                    bank = banks.take(pe, (K + "bc", h))
                    mm(pe, bank[:, :], lhsT=cst("sel")[0:16, h * P:(h + 1) * P], rhs=dts[0:16, 3, :], start=True,
                       stop=True, done=(K + "bc", h))

                spread(0)
                spread(1)
                pe.wait_ge(*dve_made[K + "st", NT - 2, 1])
                for h in range(16):
                    if h + 2 < 16:
                        spread(h + 2)
                    r = slice(DH * (h % 2), DH * (h % 2) + DH)
                    if h % 2 == 0:
                        bank = banks.take(pe, (K + "y", h // 2))
                    pe.wait_ge(*dve_made[K + "g", h])
                    pe.wait_ge(*pool_made[K + "ce", h])
                    for t in range(NT):
                        s = slice(t * P, (t + 1) * P)
                        last = t == NT - 1
                        mm(pe, bank[r, s], lhsT=xd[:, t, h * DH:(h + 1) * DH], rhs=dg[:, h % 2, s], start=True,
                           stop=(t == 0))
                        if t:
                            mm(pe, bank[r, s], lhsT=st[:, t - 1, h * DH:(h + 1) * DH], rhs=ce[:, h % 2, s],
                               start=False, stop=True,
                               done=((K + "y", h // 2) if h % 2 else (K + "yh", h)) if last else None)

            def act_ssd(act):
                act.wait_ge(*filled[K + "last", 0])
                act.activation(cd.rearrange("p a b -> p (a b)"), banks[K + "last", 0][:, 0:16 * NT], ACT.Exp)\
                   .then_inc(*act_made.mark(K + "cd"))
                banks.drain((K + "last", 0), "act_made")
                for g in range(2):
                    act.wait_ge(*filled[K + "cb", g])
                    act.activation(cbt[:, g, :], banks[K + "cb", g][:, :], ACT.Copy)\
                       .then_inc(*act_made.mark((K + "cb", g)))
                    banks.drain((K + "cb", g), "act_made")
                    act.wait_ge(*filled[K + "bn", g])
                    act.activation(bn[:, :, g * P:(g + 1) * P],
                                   banks[K + "bn", g][:, :].rearrange("p (t w) -> p t w", t=NT), ACT.Copy)\
                       .then_inc(*act_made.mark((K + "bn", g)))
                    banks.drain((K + "bn", g), "act_made")
                for h in range(16):
                    act.wait_ge(*filled[K + "bc", h])
                    if h >= 2:
                        act.wait_ge(*pool_made[K + "ce", h - 2])
                    act.wait_ge(*dve_made[K + "seg", h])
                    act.activation(eb[:, h % 2, :], banks[K + "bc", h][:, :], ACT.Exp)\
                       .then_inc(*act_made.mark((K + "eb", h)))
                    banks.drain((K + "bc", h), "act_made")
                    act.activation(dg[:, h % 2, :], dg[:, h % 2, :], ACT.Exp).then_inc(*act_made.mark((K + "dg", h)))

            def heads_of(a, t, g, row):
                return natd[:, row, t, 8 * g:8 * g + 8].rearrange("p (h c) -> p h c", c=1).to_broadcast([P, 8, DH])

            def dve_ssd(dve):
                for w in after_att:
                    dve.wait_ge(*w)
                for t in range(NT):
                    dve.wait_ge(*dve_made[K + "acs", t])
                last = dts[0:16, 3, P - 1:SEQ:P].rearrange("p (a t) -> p a t", a=1).to_broadcast([16, 16, NT])
                dve.tensor_tensor(lastd[0:16, :, :], last,
                                  ident[0:16, 0:16].rearrange("p (h c) -> p h c", c=1).to_broadcast([16, 16, NT]),
                                  ALU.mult).then_inc(*dve_made.mark(K + "lastd"))
                dve.wait_ge(*filled[K + "nat", 0])
                b = banks[K + "nat", 0]
                dve.tensor_copy(natd.rearrange("p a t c -> p (a t c)"), b[:, 0:192]).then_inc(*dve_made.mark(K + "nat0"))
                banks.drain((K + "nat", 0), "dve_made")
                dve.wait_ge(*dve_made[K + "nat0"])
                n1 = natd[:, 1, :, :].rearrange("p t c -> p (t c)")
                dve.tensor_scalar(n1, n1, -1.0, None, ALU.mult).then_inc(*dve_made.mark(K + "nat"))
                for g in range(2):
                    dve.wait_ge(*act_made[K + "cb", g])
                    c3 = cbt[:, g, :].rearrange("p (t w) -> p t w", t=NT)
                    tri = cst("causalT").rearrange("p (t w) -> p t w", t=1).to_broadcast([P, NT, P])
                    dve.tensor_tensor(c3, c3, tri, ALU.mult).then_inc(*dve_made.mark((K + "cbm", g)))
                for t in range(NT):
                    for g in range(2):
                        dve.wait_ge(*filled[K + "xt", t, g])
                        d = xd[:, t, g * 512:(g + 1) * 512].rearrange("p (h c) -> p h c", h=8)
                        dve.tensor_tensor(d, banks[K + "xt", t, g][:, :].rearrange("p (h c) -> p h c", h=8),
                                          heads_of(None, t, g, 0), ALU.mult).then_inc(*dve_made.mark((K + "xd", t, g)))
                        banks.drain((K + "xt", t, g), "dve_made")
                for t in range(NT - 1):
                    for g in range(2):
                        d = xd[:, t, g * 512:(g + 1) * 512].rearrange("p (h c) -> p h c", h=8)
                        dve.wait_ge(*dve_made[K + "xd", t, g])
                        if t:
                            dve.wait_ge(*filled[K + "st", t - 1, g])
                        dve.tensor_tensor(xds[:, g, :].rearrange("p (h c) -> p h c", h=8), d, heads_of(None, t, g, 2),
                                          ALU.mult).then_inc(*dve_made.mark((K + "xds", t, g)))
                    for g in range(2):
                        dst = st[:, t, g * 512:(g + 1) * 512]
                        bank = banks[K + "st", t, g][:, :]
                        if t == 0:
                            dve.wait_ge(*filled[K + "st", t, g])
                            dve.tensor_copy(dst, bank).then_inc(*dve_made.mark((K + "st", t, g)))
                        else:
                            dve.wait_ge(*act_made[K + "cd"])
                            dve.wait_ge(*dve_made[K + "st", t - 1, g])
                            prev = st[:, t - 1, g * 512:(g + 1) * 512].rearrange("p (h c) -> p h c", h=8)
                            decay = cd[:, 8 * g:8 * g + 8, t:t + 1].to_broadcast([P, 8, DH])
                            dve.tensor_tensor(dst.rearrange("p (h c) -> p h c", h=8), prev, decay, ALU.mult)\
                               .then_inc(*dve_made.mark((K + "std", t, g)))
                            dve.wait_ge(*dve_made[K + "std", t, g])
                            dve.wait_ge(*filled[K + "st", t, g])
                            dve.tensor_tensor(dst, dst, bank, ALU.add).then_inc(*dve_made.mark((K + "st", t, g)))
                        banks.drain((K + "st", t, g), "dve_made")

                def seg(h):
                    dve.wait_ge(*filled[K + "bc", h])
                    if h >= 2:
                        dve.wait_ge(*filled[(K + "y", (h - 2) // 2) if h % 2 else (K + "yh", h - 2)])
                    for t in range(NT):
                        s = slice(t * P, (t + 1) * P)
                        i = dve.tensor_scalar(dg[:, h % 2, s], banks[K + "bc", h][:, s], natd[:, 1, t, h:h + 1], 0.0,
                                              ALU.add, ALU.min)
                    i.then_inc(*dve_made.mark((K + "seg", h)))

                seg(0)
                for h in range(16):
                    if h + 1 < 16:
                        seg(h + 1)
                    dve.wait_ge(*act_made[K + "dg", h])
                    dve.tensor_tensor(dg[:, h % 2, :], dg[:, h % 2, :], cbt[:, h // 8, :], ALU.mult)\
                       .then_inc(*dve_made.mark((K + "g", h)))
                    if h % 2:
                        c = h // 2
                        if c:
                            drain_y(dve, c - 1)
                drain_y(dve, KD - 1)

            def drain_y(dve, c):
                dve.wait_ge(*filled[K + "y", c])
                dve.scalar_tensor_tensor(out=xbc[:, c, :], in0=xbc[:, c, :], scalar=col("d_skip", l, c),
                                         in1=banks[K + "y", c][:, :], op0=ALU.mult, op1=ALU.add)\
                   .then_inc(*dve_made.mark((K + "y", c)))
                banks.drain((K + "y", c), "dve_made")

            def pool_ssd(pool):
                for h in range(16):
                    pool.wait_ge(*act_made[K + "eb", h])
                    if h >= 2:
                        pool.wait_ge(*filled[(K + "y", (h - 2) // 2) if h % 2 else (K + "yh", h - 2)])
                    pool.tensor_tensor(ce[:, h % 2, :], eb[:, h % 2, :], xbc[:, 10 + h // 8, :], ALU.mult)\
                       .then_inc(*pool_made.mark((K + "ce", h)))

            then(pe=pe_ssd, act=act_ssd, dve=dve_ssd, pool=pool_ssd)

            A = Area(work)
            sil = A.take(3, SEQ)
            sg = A.take(2, 2, SEQ)
            tg = A.take(2, 2, SEQ)
            mg = A.take(KD, SEQ)

            def pe_gate(pe):
                for n in range(4):
                    pe_linear(pe, K + "ga", n, hT, KD, None)
                for n in range(KD):
                    pe_linear(pe, K + "z", n, hT, KD, None)

            def act_gate(act):
                act.wait_ge(*filled[K + "y", KD - 1])
                for i in range(12):
                    key = (K + "ga", i) if i < 4 else (K + "z", i - 4)
                    act.wait_ge(*filled[key])
                    if i >= 3:
                        act.wait_ge(*dve_made[K + "gated", i - 3])
                    act.activation(sil[:, i % 3, :], banks[key][:, :], ACT.Silu)\
                       .then_inc(*act_made.mark((K + "sil", i)))
                    banks.drain(key, "act_made")

            def dve_gate(dve):
                for i in range(12):
                    dve.wait_ge(*act_made[K + "sil", i])
                    if i < 4:
                        dve.wait_ge(*turned_at(K + "ot")(i))
                        d = oT[:, i, :]
                    else:
                        dve.wait_ge(*dve_made[K + "y", i - 4])
                        d = xbc[:, i - 4, :]
                    dve.tensor_tensor(d, d, sil[:, i % 3, :], ALU.mult).then_inc(*dve_made.mark((K + "gated", i)))

            then(pe=pe_gate, act=act_gate, dve=dve_gate)

            sq2 = Area().take(KD, SEQ)

            def act_gn(act):
                for k in range(KD):
                    act.wait_ge(*dve_made[K + "gated", 4 + k])
                    act.activation(sq2[:, k, :], xbc[:, k, :], ACT.Square).then_inc(*act_made.mark((K + "gn", "sq", k)))
                for g in range(2):
                    act_root(act, K + "gn", rstd[:, g, :], g)

            def pe_gn(pe):
                for g in range(2):
                    bank = banks.take(pe, (K + "gn", "mean", g))
                    for j in range(4):
                        pe.wait_ge(*act_made[K + "gn", "sq", 4 * g + j])
                        mm(pe, bank[:, :], lhsT=cst("mean_g"), rhs=sq2[:, 4 * g + j, :], start=(j == 0), stop=(j == 3),
                           done=(K + "gn", "mean", g) if j == 3 else None)

            def dve_gn(dve):
                for g in range(2):
                    dve_inverse(dve, K + "gn", rstd[:, g, :], g)
                for k in range(KD):
                    dve.wait_ge(*act_made[K + "gn", "rstd", k // 4])
                    dve.scalar_tensor_tensor(out=xbc[:, k, :], in0=xbc[:, k, :], scalar=col("ssm_g", l, k),
                                             in1=rstd[:, k // 4, :], op0=ALU.mult, op1=ALU.mult)\
                       .then_inc(*dve_made.mark((K + "gn", k)))

            then(pe=pe_gn, act=act_gn, dve=dve_gn)

            def pe_merge(pe):
                for k in range(4):
                    pe.wait_ge(*dve_made[K + "gated", k])
                for n in range(0, KD, 2):
                    for m in (n, n + 1):
                        pe_linear(pe, K + "ya", m, oT, 4, None)
                    for m in (n, n + 1):
                        pe_linear(pe, K + "gla", m, hT, KD, None)
                        pe_linear(pe, K + "gls", m, hT, KD, None)
                        pe_linear(pe, K + "ys", m, xbc, KD, lambda k: dve_made[K + "gn", k])
                for n in range(KD):
                    pe_linear(pe, K + "out", n, mg, KD, lambda k: pool_made[K + "mg", k])

            def act_merge(act):
                for n in range(KD):
                    for j, key in enumerate(("gla", "gls")):
                        act.wait_ge(*filled[K + key, n])
                        if n >= 2:
                            act.wait_ge(*dve_made[K + "tg", n - 2, j])
                        act.activation(sg[:, n % 2, j, :], banks[K + key, n][:, :], ACT.Sigmoid)\
                           .then_inc(*act_made.mark((K + "sg", n, j)))
                        banks.drain((K + key, n), "act_made")

            def dve_merge(dve):
                for n in range(KD):
                    for j, key in enumerate(("ya", "ys")):
                        dve.wait_ge(*act_made[K + "sg", n, j])
                        dve.wait_ge(*filled[K + key, n])
                        if n >= 2:
                            dve.wait_ge(*pool_made[K + "mg", n - 2])
                        dve.tensor_tensor(tg[:, n % 2, j, :], sg[:, n % 2, j, :], banks[K + key, n][:, :], ALU.mult)\
                           .then_inc(*dve_made.mark((K + "tg", n, j)))
                        banks.drain((K + key, n), "dve_made")
                dve_residual(dve, K + "out", lambda n: mod[:, 24 * l + 16 + n:24 * l + 17 + n])

            def pool_merge(pool):
                for n in range(KD):
                    for j in range(2):
                        pool.wait_ge(*dve_made[K + "tg", n, j])
                    pool.tensor_tensor(mg[:, n, :], tg[:, n % 2, 0, :], tg[:, n % 2, 1, :], ALU.add)\
                        .then_inc(*pool_made.mark((K + "mg", n)))

            then(pe=pe_merge, act=act_merge, dve=dve_merge, pool=pool_merge)
            return K + "out"

        x3 = block2(0, lambda k: [dve_made["xn", k], dve_made["gsc", LAYERS - 1]], filled["xn", "mean", 0],
                    filled[("f1", "y"), KD - 1])
        x4 = block2(1, x_after(x3), filled["L0gls", KD - 1], filled["L0out", KD - 1])
        then(norm("fin", x_after(x4), ("final_g", 0), xT, filled["L1gls", KD - 1]))

        A = Area()
        y_nat = A.take(NT, D)

        def pe_back(pe):
            for k in range(KD):
                pe.wait_ge(*dve_made["fin", k])
            for t in range(NT):
                for half in range(2):
                    bank = banks.take(pe, ("back", t, half))
                    for j in range(4):
                        tp(pe, bank[:, j * P:(j + 1) * P], xT[:, half * 4 + j, t * P:(t + 1) * P], ident,
                           done=("back", t, half) if j == 3 else None)

        def act_back(act):
            act.wait_ge(*filled["L1out", KD - 1])
            for t in range(NT):
                act.wait_ge(*filled["back", t, 0])
                act.activation(y_nat[:, t, 0:512], banks["back", t, 0][:, :], ACT.Copy)\
                   .then_inc(*act_made.mark(("back", t)))
                banks.drain(("back", t, 0), "act_made")
                act.wait_ge(*act_made["back", t])
                act.wait_ge(*dve_made["back", t])
                act.dma_start(out[t * P:(t + 1) * P, :], y_nat[:, t, :]).then_inc(out_stored, 16)
            act.wait_ge(out_stored, 16 * NT)

        def dve_back(dve):
            for t in range(NT):
                dve.wait_ge(*filled["back", t, 1])
                dve.tensor_copy(y_nat[:, t, 512:1024], banks["back", t, 1][:, :])\
                   .then_inc(*dve_made.mark(("back", t)))
                banks.drain(("back", t, 1), "dve_made")

        then(pe=pe_back, act=act_back, dve=dve_back)

        block = ctx.enter_context(nc.Block())
        n_panels = stream_of.shape[0]

        @block.sync
        def _(sp):
            for i in range(min(RING, n_panels)):
                sp.dma_start(ring[:, i, :, :].rearrange("p k w -> p (k w)"), stream_of[i]).then_inc(panel_landed[i], 16)
            for i in range(RING, n_panels):
                sp.wait_ge(panel_used, i - RING + 1)
                s = i % RING
                sp.dma_start(ring[:, s, :, :].rearrange("p k w -> p (k w)"), stream_of[i])\
                  .then_inc(panel_landed[s], 16)

        @block.scalar
        def _(act):
            act.dma_start(x_nat, x_in.rearrange("(t p) d -> p t d", p=P)).then_inc(x_landed, 16)
            act.dma_start(vec[:, :], vec_in).then_inc(const_landed, 16)
            act.dma_start(cf[:, :], cf_in).then_inc(const_landed, 16)
            act.dma_start(cb[:, :], cb_in).then_inc(const_landed, 16)
            for part in prog["act"]:
                part(act)

        @block.tensor
        def _(pe):
            for part in prog["pe"]:
                part(pe)

        @block.vector
        def _(dve):
            for part in prog["dve"]:
                part(dve)

        @block.gpsimd
        def _(pool):
            for part in prog["pool"]:
                part(pool)

    assert tile_no[0] == n_tiles, (tile_no[0], n_tiles)
    return {"signals": {n: dict(s.at) for n, s in signals.items()}, "order": list(banks.order),
            "drained": dict(banks.drained)}


def pack_stream(inputs):
    tiles = stream()
    assert len(tiles) % KD == 0
    a = np.zeros((len(tiles) // KD, P, KD, P), np.float32)
    for t, (name, layer, row, cols) in enumerate(tiles):
        w = inputs[name][layer]
        d = a[t // KD, :, t % KD, :]
        if isinstance(cols, str):
            d[0:DH, 0:DH] = w[row:row + DH]
            d[DH:P, DH:P] = w[row:row + DH]
        elif cols[-1] - cols[0] == len(cols) - 1:
            d[:, 0:len(cols)] = w[row:row + P, cols[0]:cols[-1] + 1]
        else:
            d[:, 0:len(cols)] = w[row:row + P][:, cols]
    return a.reshape(len(tiles) // KD, P, KD * P)


def pack_vec(inputs):
    a = np.zeros((P, NVEC), np.float32)

    def put(name, layer, v, chunks):
        a[:, VEC[name, layer]:VEC[name, layer] + chunks] = v.reshape(chunks, P).T

    for l in range(2):
        put("attn_norm", l, inputs["attn_norm"][l], KD)
        put("ffn_norm", l, inputs["ffn_norm"][l], KD)
        for j in range(3):
            put("conv_w", (l, j), inputs["ffn_conv_w"][l, j], FC)
        put("conv_b", l, inputs["ffn_conv_b"][l], FC)
        put("b_ada", l, inputs["b_ada_2"][l], 24)
        put("norm_g", l, inputs["norm_g_2"][l], KD)
        for j in range(4):
            put("xconv_w", (l, j), inputs["conv_w_2"][l, j], 12)
        put("xconv_b", l, inputs["conv_b_2"][l], 12)
        a[0:16, VEC["dt_bias", l]] = inputs["dt_bias_2"][l]
        a[0:16, VEC["a_log", l]] = inputs["a_log_2"][l]
        put("d_skip", l, np.repeat(inputs["d_skip_2"][l], DH), KD)
        put("ssm_g", l, inputs["ssm_norm_g_2"][l], KD)
    put("final_norm", 0, inputs["final_norm"], KD)
    put("final_g", 0, inputs["final_g_2"], KD)
    put("c", 0, inputs["c_2"][0], KD)
    for name, src in (("pos_k", "ev_cmp_pos_k"), ("pos_v", "ev_cmp_pos_v")):
        o = VEC[name, 0]
        a[0:DH, o:o + CMP_LEN] = inputs[src][0].T
        a[DH:P, o:o + CMP_LEN] = inputs[src][0].T
    a[0:16, VEC["b_f", 0]] = inputs["od_b_f"][0]
    return a


def kernel(**inputs):
    import ml_dtypes
    import concourse.bacc as bacc
    from concourse.bass_utils import run_bass_kernel_spmd as run

    inputs = {k: np.ascontiguousarray(v) for k, v in inputs.items()}
    cf, cb = constants()
    arrays = {"weights": pack_stream(inputs), "x": inputs["x"][0], "vec": pack_vec(inputs), "cf": cf,
              "cb": cb.astype(ml_dtypes.bfloat16)}

    def program(known):
        nc = bacc.Bacc("TRN2", target_bir_lowering=False, num_devices=1)
        ins = [nc.dram_tensor(n + "_dram", a.shape, mybir.dt.from_np(a.dtype), kind="ExternalInput").ap()
               for n, a in arrays.items()]
        out = nc.dram_tensor("out_dram", (SEQ, D), F32, kind="ExternalOutput").ap()
        return nc, build(nc, ins, out, known)

    _, known = program(None)
    nc, _ = program(known)
    r = run(nc, [{n + "_dram": a for n, a in arrays.items()}], core_ids=[0])
    return np.asarray(r.results[0]["out_dram"]).reshape(1, SEQ, D)
```

```python
from contextlib import ExitStack

import numpy as np

import concourse.bass as bass
from concourse import mybir

F32 = mybir.dt.float32
F32R = mybir.dt.float32r
BF16 = mybir.dt.bfloat16
ALU = mybir.AluOpType
ACT = mybir.ActivationFunctionType
AX = mybir.AxisListType

P = 128
D = 1024
KD = D // P
SEQ = 512
NT = SEQ // P
DH = 64
SCALE = DH ** -0.5
NEG = -1e30
TAKEN = -3e38
EPS = 1e-6
D_FF = 2816
FC = D_FF // P
FH = FC // 2
NCMP = 31
CMP_LEN = 32
CMP_STRIDE = 16
TOPK = 128
RAW = 5
PARTS = 3
ARENA = 22850
NBANK = 7
LAYERS = 2


def ada_steps(layer, n):
    first = 2 * n if n < 2 else n + 2
    return [(layer, j // KD, j % KD) for j in range(first, first + (2 if n < 2 else 1))]


def stream():
    tiles = []

    def full(name, layer, cols):
        for k in range(KD):
            tiles.append((name, layer, k * P, cols))

    def proj(name, layer, start, width):
        for i in range(0, width, P):
            full(name, layer, list(range(start + i, start + min(i + P, width))))

    def tall(name, layer, kt, first=0):
        for n in range(KD):
            for k in range(first, first + kt):
                tiles.append((name, layer, k * P, list(range(n * P, n * P + P))))

    def ffn(layer):
        for n in range(FC):
            proj("ffn_w_in", layer, n * P, P)
            proj("ffn_w_in", layer, D_FF + n * P, P)
            for l, b, k in ada_steps(layer, n):
                for i in range(KD):
                    tiles.append(("w_ada_2", l, k * P, list(range(b * D + i * P, b * D + i * P + P))))
            if n % FH == FH - 1:
                tall("ffn_w_out", layer, FH, n + 1 - FH)

    sq, sk, sv, nq, kc, vc, ksl, vsl, kwn, vwn, g = 0, 512, 1024, 1536, 2048, 2176, 2304, 2432, 2560, 2688, 2816
    proj("ev_w_in", 0, kc, P)
    proj("ev_w_in", 0, vc, P)
    proj("ev_w_in", 0, ksl, P)
    proj("ev_w_in", 0, kwn, P)
    for c in range(4):
        full("ev_w_in", 0, [nq + (gr * 4 + c) * DH + i for gr in range(2) for i in range(DH)])
    proj("ev_w_in", 0, vsl, P)
    proj("ev_w_in", 0, vwn, P)
    proj("ev_w_in", 0, g, 24)
    proj("ev_w_in", 0, sk, 512)
    proj("ev_w_in", 0, sq, 512)
    proj("ev_w_in", 0, sv, 512)
    for name in ("ev_cmp_w_k", "ev_cmp_w_v"):
        for l in range(CMP_LEN):
            tiles.append((name, 0, l * DH, "twice"))
    tall("ev_w_out", 0, KD)
    ffn(0)
    proj("od_w_in", 0, 3072, 16)
    for c in range(KD):
        for part in range(3):
            proj("od_w_in", 0, part * D + c * P, P)
    tall("od_w_out", 0, KD)
    ffn(1)
    for layer in range(LAYERS):
        w = "w_in_2"
        proj(w, layer, 1152, 256)
        full(w, layer, [1408 + i for _ in range(2) for i in range(DH)])
        proj(w, layer, 1472, 4)
        proj(w, layer, 0, 512)
        full(w, layer, [512 + i for _ in range(2) for i in range(DH)])
        proj(w, layer, 576, DH)
        proj(w, layer, 4036, 16)
        proj(w, layer, 2500, 1536)
        proj(w, layer, 640, 512)
        proj(w, layer, 1476, 1024)
        for n in range(KD):
            for k in range(4):
                tiles.append(("w_branch_a_2", layer, k * P, list(range(n * P, n * P + P))))
            if n % 2:
                for m in (n - 1, n):
                    proj(w, layer, 4052 + m * P, P)
                    proj(w, layer, 5076 + m * P, P)
                    for k in range(KD):
                        tiles.append(("w_branch_s_2", layer, k * P, list(range(m * P, m * P + P))))
        tall("w_out_2", layer, KD)
    return tiles


def vec_layout():
    at, n = {}, 0
    for name, layer, cols in (
        [("attn_norm", l, KD) for l in range(2)] + [("ffn_norm", l, KD) for l in range(2)]
        + [("conv_w", (l, j), FC) for l in range(2) for j in range(3)] + [("conv_b", l, FC) for l in range(2)]
        + [("final_norm", 0, KD), ("pos_k", 0, CMP_LEN), ("pos_v", 0, CMP_LEN), ("b_f", 0, 1), ("c", 0, KD)]
        + [("b_ada", l, 24) for l in range(2)] + [("norm_g", l, KD) for l in range(2)]
        + [("xconv_w", (l, j), 12) for l in range(2) for j in range(4)] + [("xconv_b", l, 12) for l in range(2)]
        + [("dt_bias", l, 1) for l in range(2)] + [("a_log", l, 1) for l in range(2)]
        + [("d_skip", l, KD) for l in range(2)] + [("ssm_g", l, KD) for l in range(2)] + [("final_g", 0, KD)]
    ):
        at[name, layer] = n
        n += cols
    return at, n


VEC, NVEC = vec_layout()

CF = {}
CB = {}
CR = {}


def _place(table, items):
    n = 0
    for name, w in items:
        table[name] = (n, w)
        n += w
    return n


NCF = _place(CF, [("ident", P), ("tri", P), ("nones", P), ("mean_d", P), ("mean_g", P), ("perm8", P), ("perm32", P),
                  ("cosc", 32), ("sinc", 32),
                  ("strict", P), ("causalT", P), ("cmp01", NT * 32), ("ones", P)])
NCR = _place(CR, [("cos8", SEQ), ("sin8", SEQ), ("cos32", SEQ), ("sin32", SEQ)])
NCB = _place(CB, [("ident", P), ("causal", P), ("strictT", P), ("cmp", NT * P), ("selneg", 16)])


def constants():
    f = np.zeros((P, NCF), np.float32)
    b = np.zeros((P, NCB), np.float32)
    rot = np.zeros((P, NCR), np.float32)

    def put(t, table, name, a):
        a = np.asarray(a, np.float32).reshape(a.shape[0], -1)
        o, w = table[name]
        assert a.shape[1] == w, name
        t[: a.shape[0], o:o + w] = a

    i = np.arange(P)
    put(f, CF, "ident", np.eye(P))
    put(f, CF, "tri", -(i[:, None] >= i[None, :]).astype(np.float32))
    put(f, CF, "nones", -np.ones((P, P)))
    put(f, CF, "mean_d", np.full((P, P), 1.0 / D))
    put(f, CF, "mean_g", np.full((P, P), 1.0 / 512))

    def rope(rot, theta, pos):
        half = rot // 2
        if rot == 16:
            inv = (np.float32(theta) ** (-(np.arange(half, dtype=np.float32) * np.float32(2.0) / np.float32(rot)))).astype(np.float32)
        else:
            inv = (np.float32(theta) ** (-np.arange(0, rot, 2, dtype=np.float32) / np.float32(rot))).astype(np.float32)
        ang = (pos.astype(np.float32)[:, None] * inv[None, :]).astype(np.float32)
        cos = np.ones((P, len(pos)), np.float32)
        sin = np.zeros((P, len(pos)), np.float32)
        perm = np.zeros((P, P), np.float32)
        for base in (0, DH):
            for j in range(DH):
                if j < half:
                    src, s = j + half, -1.0
                elif j < rot:
                    src, s = j - half, 1.0
                else:
                    perm[base + j, base + j] = 1.0
                    continue
                perm[base + src, base + j] = 1.0
                cos[base + j] = np.cos(ang[:, j % half])
                sin[base + j] = s * np.sin(ang[:, j % half])
        return cos, sin, perm

    pos = np.arange(SEQ)
    cmp_end = np.arange(32) * CMP_STRIDE + CMP_LEN - 1
    c, s, m = rope(16, 500000.0, pos)
    put(rot, CR, "cos8", c), put(rot, CR, "sin8", s), put(f, CF, "perm8", m)
    c, s, m = rope(16, 500000.0, cmp_end)
    put(f, CF, "cosc", c), put(f, CF, "sinc", s)
    c, s, m = rope(64, 10000.0, pos)
    put(rot, CR, "cos32", c), put(rot, CR, "sin32", s), put(f, CF, "perm32", m)
    put(f, CF, "strict", (i[:, None] < i[None, :]).astype(np.float32))
    put(f, CF, "causalT", (i[:, None] <= i[None, :]).astype(np.float32))
    seen = (cmp_end[None, None, :] <= (i[:, None, None] + P * np.arange(NT)[None, :, None])) & (np.arange(32) < NCMP)
    put(f, CF, "cmp01", seen.astype(np.float32))
    put(f, CF, "ones", np.ones((P, P)))
    put(b, CB, "ident", np.eye(P))
    put(b, CB, "causal", np.where(i[None, :] > i[:, None], NEG, 0.0))
    put(b, CB, "strictT", np.where(i[:, None] >= i[None, :], NEG, 0.0))
    put(b, CB, "cmp", np.repeat(np.where(seen, 0.0, NEG)[:, :, None, :], 4, axis=2))
    sn = np.zeros((96, 16), np.float32)
    for q in range(3):
        sn[32 * q + np.arange(16), np.arange(16)] = -1.0
    put(b, CB, "selneg", sn)
    return f, b, rot


class Pair:

    def __init__(self, hi, lo):
        self.parts = hi, lo

    def __getitem__(self, at):
        p, part, k, f = at
        return self.parts[part][p, k, f]


class Signal:

    def __init__(self, sem, known, final=False):
        self.sem, self.known, self.count, self.at = sem, known or {}, 0, {}
        self.final = final

    def mark(self, key=None, n=1):
        self.count += n
        assert key is None or key not in self.at, key
        self.at[key] = self.count
        return self.sem, n

    def __getitem__(self, key):
        return self.sem, self.known.get(key, 1) if not self.final else self.known[key]


class Banks:

    def __init__(self, aps, signals, order, drained, panel_of):
        self.aps, self.signals = aps, signals
        self.number = {key: n for n, key in enumerate(order or [])}
        self.known, self.order, self.drained = drained, [], {}
        self.last_panel, self.panel_of = panel_of, {}

    def take(self, pe, key):
        n = len(self.order)
        self.order.append(key)
        if n >= NBANK:
            name, count = self.known.get(self.order[n - NBANK]) if self.known else (next(iter(self.signals)), 1)
            pe.wait_ge(self.signals[name].sem, count)
        return self.aps[n % NBANK]

    def __getitem__(self, key):
        return self.aps[self.number[key] % NBANK if self.number else 0]

    def drain(self, key, name):
        self.drained[key] = (name, self.signals[name].count)


SIGNALS = ["bank_filled", "act_made", "dve_made", "pool_made"]


def build(nc, ins, out, known=None, final=False):
    stream_of, x_in, vec_in, cf_in, cb_in, rot_in = ins
    tiles = stream()
    kinds = ["PE" if t[0].startswith("ev_cmp") else "DVE" if t[0] == "w_ada_2" else "split" for t in tiles[::KD]]
    place = np.cumsum([k == "split" for k in kinds]) - 1
    splits = [p for p, k in enumerate(kinds) if k == "split"]
    ada_panel = dict(zip([st for l in range(2) for n in range(FC) for st in ada_steps(l, n)],
                         [p for p, k in enumerate(kinds) if k == "DVE"]))
    n_tiles = stream_of.shape[0] * KD
    with ExitStack() as ctx:
        def sb(name, shape, dt=F32):
            return ctx.enter_context(nc.sbuf_tensor(name, shape, dt))

        ring = sb("ring", [P, RAW, KD, P])
        wparts = sb("wparts", [P, PARTS, 2, KD, P], F32R)
        xT = sb("xT", [P, KD, SEQ])
        hT = sb("hT", [P, 2, KD, SEQ], F32R)
        hv = sb("hv", [P, 4, SEQ])
        rot = sb("rot", [P, 2, SEQ])
        vec = sb("vecs", [P, NVEC])
        cf = sb("cf_sb", [P, NCF])
        cb = sb("cb_sb", [P, NCB], BF16)
        small = sb("small", [P, 256])
        rstd = sb("rstd", [P, 2, SEQ])
        arena = sb("arena", [P, ARENA])
        arena_at = nc.sbuf_base - 4 * ARENA
        arena_r = nc.alloc_sbuf_tensor_at("arena_r", [P, ARENA], F32R, offset=arena_at)
        psum = [ctx.enter_context(nc.psum_tensor(f"bank{i}", [P, SEQ], F32)) for i in range(NBANK)]
        mean_bank = ctx.enter_context(nc.psum_tensor("mean_bank", [P, SEQ], F32))

        signals = {name: Signal(ctx.enter_context(nc.semaphore(name)), known and known["signals"][name], final)
                   for name in SIGNALS}
        filled, act_made, dve_made, pool_made = (signals[n] for n in SIGNALS)
        banks = Banks(psum, signals, known and known["order"], known and known["drained"],
                      known and known["panel_of"])
        panel_landed = [ctx.enter_context(nc.semaphore(f"panel_landed{i}")) for i in range(RAW)]
        rot_landed = ctx.enter_context(nc.semaphore("rot_landed"))
        x_landed = ctx.enter_context(nc.semaphore("x_landed"))
        const_landed = ctx.enter_context(nc.semaphore("const_landed"))
        out_stored = ctx.enter_context(nc.semaphore("out_stored"))

        def cst(name):
            o, w = CF[name]
            return cf[:, o:o + w]

        def cstb(name):
            o, w = CB[name]
            return cb[:, o:o + w]

        def col(name, layer, k=0, parts=P):
            o = VEC[name, layer] + k
            return vec[0:parts, o:o + 1]

        class Area:

            def __init__(self, base=0):
                self.at = base

            def take(self, *shape):
                n = int(np.prod(shape))
                a = arena[:, self.at:min(self.at + n, ARENA)]
                self.at += n
                assert self.at <= ARENA, self.at
                if len(shape) == 2:
                    a = a.rearrange("p (a b) -> p a b", a=shape[0])
                elif len(shape) == 3:
                    a = a.rearrange("p (a b c) -> p a b c", a=shape[0], b=shape[1])
                return a

            def take_r(self, *shape):
                at = self.at
                self.take(int(np.prod(shape)))
                a = arena_r[:, at:self.at]
                if len(shape) == 2:
                    return a.rearrange("p (a b) -> p a b", a=shape[0])
                return a.rearrange("p (a b c) -> p a b c", a=shape[0], b=shape[1])

            def take16(self, n):
                a = arena[:, self.at:self.at + n // 2].bitcast(BF16)
                self.at += n // 2
                return a

        ident = cst("ident")
        identb = cstb("ident")

        tile_no = [0]

        def mm(pe, *args, done=None, ends=None, **kw):
            i = pe.matmul(*args, **kw)
            if done is not None:
                i.then_inc(*filled.mark(done))
                if ends is not None:
                    filled.at["panel", ends] = filled.count
            elif ends is not None:
                i.then_inc(*filled.mark(("panel", ends)))
            return i

        def tp(pe, *args, done=None):
            i = pe.transpose(*args)
            if done is not None:
                i.then_inc(*filled.mark(done))
            return i

        def landed(eng, panel):
            eng.wait_ge(panel_landed[panel % RAW], 16 * (panel // RAW + 1))

        def tile_of(pe):
            t = tile_no[0]
            tile_no[0] += 1
            panel, j = divmod(t, KD)
            ends = panel if j == KD - 1 else None
            if kinds[panel] == "split":
                if j == 0:
                    pe.wait_ge(*dve_made["w_lo", panel])
                slot = place[panel] % PARTS
                return (wparts[:, slot, 0, j, :], wparts[:, slot, 1, j, :]), ends
            if j == 0:
                landed(pe, panel)
            return ring[:, panel % RAW, j, :], ends

        def pe_linear(pe, key, n, rhs, rows, ready):
            bank = banks.take(pe, (key, n))
            for k in range(rows):
                (hi, lo), ends = tile_of(pe)
                if ready:
                    pe.wait_ge(*ready(k))
                last = k == rows - 1
                mm(pe, bank[:, :], lhsT=hi, rhs=rhs[:, 0, k, :], start=(k == 0), stop=False)
                mm(pe, bank[:, :], lhsT=hi, rhs=rhs[:, 1, k, :], start=False, stop=False)
                mm(pe, bank[:, :], lhsT=lo, rhs=rhs[:, 0, k, :], start=False, stop=last,
                   done=(key, n) if last else None, ends=ends)
            banks.panel_of[key, n] = (tile_no[0] - 1) // KD

        def pe_turn(pe, key, n, src, width=P):
            pe.wait_ge(*act_made[key, "T", n])
            bank = banks.take(pe, (key, "nat", n))
            for t in range(NT):
                tp(pe, bank[:, t * width:(t + 1) * width], src[0:width, t * P:(t + 1) * P], ident[0:width, 0:width],
                   done=(key, "nat", n) if t == NT - 1 else None)

        def turned_bank(key, n, width=P):
            return banks[key, "nat", n][:, 0:NT * width].rearrange("p (t w) -> p t w", t=NT)

        split_at = {"act": 0, "dve": 0}

        def keep_up(eng, who, key):
            if banks.last_panel is None:
                return
            end = banks.last_panel[key]
            upto = place[end] + PARTS - 1
            while split_at[who] <= min(upto, len(splits) - 1):
                i = split_at[who]
                p = splits[i]
                if any(k != "split" for k in kinds[end + 1:max(end, p - RAW) + 1]):
                    return
                split_at[who] += 1
                slot = i % PARTS
                if who == "act":
                    landed(eng, p)
                    if i >= PARTS:
                        eng.wait_ge(*filled["panel", splits[i - PARTS]])
                    eng.activation(wparts[:, slot, 0, :, :], ring[:, p % RAW, :, :], ACT.Copy)\
                       .then_inc(*act_made.mark(("w_hi", p)))
                else:
                    eng.wait_ge(*act_made["w_hi", p])
                    eng.tensor_tensor(wparts[:, slot, 1, :, :], ring[:, p % RAW, :, :],
                                      wparts[:, slot, 0, :, :].bitcast(F32), ALU.subtract)\
                       .then_inc(*dve_made.mark(("w_lo", p)))

        def act_bank(act, key):
            keep_up(act, "act", key)
            act.wait_ge(*filled[key])

        def dve_bank(dve, key):
            keep_up(dve, "dve", key)
            dve.wait_ge(*filled[key])

        def act_hi(act, dst, src, key):
            act.activation(dst, src, ACT.Copy).then_inc(*act_made.mark((key, "hi")))

        def dve_lo(dve, hi, lo, src, key):
            dve.wait_ge(*act_made[key, "hi"])
            dve.tensor_tensor(lo, src, hi.bitcast(F32), ALU.subtract).then_inc(*dve_made.mark((key, "lo")))

        def act_square(act, key, src, k, waits):
            for w in waits:
                act.wait_ge(*w)
            if k >= 4:
                act.wait_ge(*filled[key, "m", k - 4])
            act.activation(hv[:, k % 4, :], src[:, k, :], ACT.Square).then_inc(*act_made.mark((key, "sq", k)))

        def pe_mean(pe, key, k):
            pe.wait_ge(*act_made[key, "sq", k])
            mm(pe, mean_bank[:, :], lhsT=cst("mean_d"), rhs=hv[:, k % 4, :], start=(k == 0), stop=(k == KD - 1),
               done=(key, "m", k))

        def dve_inverse(dve, key, r, bank, last):
            dve.wait_ge(*filled[last])
            dve.tensor_scalar(r, bank, EPS, None, ALU.add).then_inc(*dve_made.mark((key, "eps")))
            dve.wait_ge(*dve_made[key, "eps"])
            dve.reciprocal(r, r).then_inc(*dve_made.mark((key, "inv")))

        def act_root(act, key, r):
            act.wait_ge(*dve_made[key, "inv"])
            act.activation(r, r, ACT.Sqrt).then_inc(*act_made.mark((key, "rstd")))

        def norm(key, gain, free=None, mod=None, to_x=False):
            def act_part(act):
                act_root(act, key, rstd[:, 0, :])
                if to_x:
                    return
                if free is not None:
                    act.wait_ge(*free)
                for k in range(KD):
                    act.wait_ge(*dve_made[key, "scaled", k])
                    if mod is not None:
                        act.activation(hT[:, 0, k, :], hv[:, k % 4, :], ACT.Identity, bias=mod[1](k))\
                           .then_inc(*act_made.mark(((key, k), "hi")))
                    else:
                        act_hi(act, hT[:, 0, k, :], hv[:, k % 4, :], (key, k))

            def pe_part(pe):
                pass

            def dve_part(dve):
                dve_inverse(dve, key, rstd[:, 0, :], mean_bank[:, :], (key, "m", KD - 1))
                dve.wait_ge(*act_made[key, "rstd"])
                if free is not None:
                    dve.wait_ge(*free)
                for k in range(KD + 1):
                    if k < KD:
                        g = col(*gain, k) if mod is None else mod[0](k)
                        if k >= 4 and not to_x:
                            dve.wait_ge(*dve_made[(key, k - 4), "lo"])
                        dst = xT[:, k, :] if to_x else hv[:, k % 4, :]
                        dve.scalar_tensor_tensor(out=dst, in0=xT[:, k, :], scalar=g, in1=rstd[:, 0, :],
                                                 op0=ALU.mult, op1=ALU.mult)\
                           .then_inc(*dve_made.mark((key, "scaled", k)))
                    if k and not to_x:
                        j = k - 1
                        hi, lo = hT[:, 0, j, :], hT[:, 1, j, :]
                        if mod is None:
                            dve_lo(dve, hi, lo, hv[:, j % 4, :], (key, j))
                        else:
                            dve.wait_ge(*act_made[(key, j), "hi"])
                            dve.scalar_tensor_tensor(out=lo, in0=hv[:, j % 4, :], scalar=mod[1](j),
                                                     in1=hi.bitcast(F32), op0=ALU.add, op1=ALU.subtract)\
                               .then_inc(*dve_made.mark(((key, j), "lo")))
            return act_part, pe_part, dve_part

        def h_at(key):
            return lambda k: dve_made[(key, k), "lo"]

        def softmax_maps(key, maps, Pb, PT, mx, sm, ready, deferred=None):
            M = len(maps)
            on_act = [i % 2 == 0 for i in range(M)]

            def pe_part(pe):
                for w in ready:
                    pe.wait_ge(*w)
                for i in range(M + 3):
                    if i < M:
                        m = maps[i]
                        bank = banks.take(pe, (key, "s", i))
                        W = m["width"]
                        extra = m["masks"]
                        mm(pe, bank[:, 0:W], lhsT=m["q"], rhs=m["k"], start=True, stop=not extra,
                           done=None if extra else (key, "s", i))
                        for j, (a, b, c, w) in enumerate(extra):
                            for wt in w:
                                pe.wait_ge(*wt)
                            mm(pe, bank[:, c:c + b.shape[-1]], lhsT=a, rhs=b, start=False, stop=j == len(extra) - 1,
                               done=(key, "s", i) if j == len(extra) - 1 else None)
                    if 2 <= i < M + 2:
                        j = i - 2
                        m = maps[j]
                        n = m["width"] // P
                        pe.wait_ge(*act_made[key, "p", j])
                        bank = banks.take(pe, (key, "t", j))
                        for t in range(n):
                            tp(pe, bank[:, t * P:(t + 1) * P], Pb[:, j % 3, t * P:(t + 1) * P], ident,
                               done=(key, "t", j) if t == n - 1 else None)
                    if i >= 3:
                        j = i - 3
                        m = maps[j]
                        n = m["width"] // P
                        pe.wait_ge(*(act_made if on_act[j] else dve_made)[key, "pt", j])
                        bank = banks.take(pe, (key, "o", j))
                        for t in range(n):
                            mm(pe, bank[:, 0:DH], lhsT=PT[:, j % 3, t * P:(t + 1) * P], rhs=m["v"](t), start=(t == 0),
                               stop=(t == n - 1), done=(key, "o", j) if t == n - 1 else None)

            def act_part(act):
                for i in range(M + 2):
                    if i < M:
                        W = maps[i]["width"]
                        act.wait_ge(*dve_made[key, "max", i])
                        if i >= 3:
                            act.wait_ge(*filled[key, "t", i - 3])
                        act.activation(Pb[:, i % 3, 0:W], banks[key, "s", i][:, 0:W], ACT.Exp, bias=mx(i),
                                       accum_out=sm(i)).then_inc(*act_made.mark((key, "p", i)))
                        banks.drain((key, "s", i), "act_made")
                    if i >= 2 and on_act[i - 2]:
                        j = i - 2
                        W = maps[j]["width"]
                        act.wait_ge(*filled[key, "t", j])
                        if j >= 3:
                            act.wait_ge(*filled[key, "o", j - 3])
                        act.activation(PT[:, j % 3, 0:W], banks[key, "t", j][:, 0:W], ACT.Copy)\
                           .then_inc(*act_made.mark((key, "pt", j)))
                        banks.drain((key, "t", j), "act_made")

            def dve_part(dve):
                for i in range(M + 3):
                    if i < M:
                        W = maps[i]["width"]
                        dve.wait_ge(*filled[key, "s", i])
                        if i >= 3:
                            dve.wait_ge(*act_made[key, "p", i - 3])
                        dve.tensor_reduce(mx(i), banks[key, "s", i][:, 0:W], AX.X, ALU.max, negate=True)\
                           .then_inc(*dve_made.mark((key, "max", i)))
                    if 1 <= i < M + 1:
                        j = i - 1
                        dve.wait_ge(*act_made[key, "p", j])
                        dve.reciprocal(sm(j), sm(j)).then_inc(*dve_made.mark((key, "inv", j)))
                        if maps[j]["gate"] is not None:
                            dve.wait_ge(*dve_made[key, "inv", j])
                            dve.tensor_tensor(sm(j), sm(j), maps[j]["gate"], ALU.mult)\
                               .then_inc(*dve_made.mark((key, "gated", j)))
                    if 2 <= i < M + 2 and not on_act[i - 2]:
                        j = i - 2
                        W = maps[j]["width"]
                        dve.wait_ge(*filled[key, "t", j])
                        if j >= 3:
                            dve.wait_ge(*filled[key, "o", j - 3])
                        dve.tensor_copy(PT[:, j % 3, 0:W], banks[key, "t", j][:, 0:W])\
                           .then_inc(*dve_made.mark((key, "pt", j)))
                        banks.drain((key, "t", j), "dve_made")
                    if i >= 3:
                        j = i - 3
                        m = maps[j]
                        dve.wait_ge(*filled[key, "o", j])
                        dve.wait_ge(*dve_made[key, "gated" if m["gate"] is not None else "inv", j])
                        o = banks[key, "o", j][:, 0:DH]
                        if m["add"] is not None:
                            dve.wait_ge(*m["add"])
                            dve.scalar_tensor_tensor(out=m["out"], in0=o, scalar=sm(j), in1=m["out"], op0=ALU.mult,
                                                     op1=ALU.add).then_inc(*dve_made.mark((key, "out", j)))
                        else:
                            dve.tensor_scalar(m["out"], o, sm(j), None, ALU.mult)\
                               .then_inc(*dve_made.mark((key, "out", j)))
                        banks.drain((key, "o", j), "dve_made")
            return act_part, pe_part, dve_part

        def turned(key, src, dst, n, waits, free=()):
            def pe_part(pe):
                for w in waits:
                    pe.wait_ge(*w)
                for k in range(n):
                    bank = banks.take(pe, (key, k))
                    for t in range(NT):
                        tp(pe, bank[:, t * P:(t + 1) * P], src[:, t, k * P:(k + 1) * P], ident,
                           done=(key, k) if t == NT - 1 else None)

            def act_part(act):
                for w in free:
                    act.wait_ge(*w)
                for k in range(0, n, 2):
                    act.wait_ge(*filled[key, k])
                    act.activation(dst[:, k, :], banks[key, k][:, :], ACT.Copy).then_inc(*act_made.mark((key, k)))
                    banks.drain((key, k), "act_made")

            def dve_part(dve):
                for w in free:
                    dve.wait_ge(*w)
                for k in range(1, n, 2):
                    dve.wait_ge(*filled[key, k])
                    dve.tensor_copy(dst[:, k, :], banks[key, k][:, :]).then_inc(*dve_made.mark((key, k)))
                    banks.drain((key, k), "dve_made")
            return act_part, pe_part, dve_part

        def turned_at(key):
            return lambda k: (act_made if k % 2 == 0 else dve_made)[key, k]

        def turned_parts(key, src, dst, waits):
            def pe_part(pe):
                for w in waits:
                    pe.wait_ge(*w)
                for k in range(KD):
                    bank = banks.take(pe, (key, k))
                    for t in range(NT):
                        tp(pe, bank[:, t * P:(t + 1) * P], src[:, t, k * P:(k + 1) * P], ident,
                           done=(key, k) if t == NT - 1 else None)

            def act_part(act):
                for k in range(KD):
                    act.wait_ge(*filled[key, k])
                    act_hi(act, dst[:, 0, k, :], banks[key, k][:, :], (key, k))

            def dve_part(dve):
                for k in range(KD):
                    dve_lo(dve, dst[:, 0, k, :], dst[:, 1, k, :], banks[key, k][:, :], (key, k))
                    banks.drain((key, k), "dve_made")
            return act_part, pe_part, dve_part

        def lo_of(key):
            return lambda k: dve_made[(key, k), "lo"]

        def project(items, ready, rtmp, vt, table=None):
            turns = [i for i, it in enumerate(items) if it["kind"] == "turn"]
            slot = {i: j % 2 for j, i in enumerate(turns)}
            ropes = [i for i, it in enumerate(items) if it["kind"] == "rope"]

            def pe_after(pe, i):
                it = items[i]
                if it["kind"] == "rope":
                    rope_parts(it["key"], it["n"], it["dst"], table)[0](pe)
                elif it["kind"] == "turn":
                    pe_turn(pe, it["key"], it["n"], vt[:, slot[i], :], it.get("width", P))

            def pe_part(pe):
                for i, it in enumerate(items):
                    pe_linear(pe, it["key"], it["n"], hT, KD, ready if i == 0 else None)
                    if i:
                        pe_after(pe, i - 1)
                pe_after(pe, len(items) - 1)

            def act_after(act, i):
                it = items[i]
                if it["kind"] == "turn" and "func" in it:
                    w = it.get("width", P)
                    act.wait_ge(*filled[it["key"], "nat", it["n"]])
                    act.activation(it["dst"], turned_bank(it["key"], it["n"], w), it["func"])\
                       .then_inc(*act_made.mark((it["key"], "turned", it["n"])))
                    banks.drain((it["key"], "nat", it["n"]), "act_made")

            def act_part(act):
                for i, it in enumerate(items):
                    key, n, kind = it["key"], it["n"], it["kind"]
                    if kind == "own":
                        keep_up(act, "act", (key, n))
                    else:
                        act_bank(act, (key, n))
                        mark = {"copy": (key, n), "rope": (key, "raw", n), "turn": (key, "T", n)}[kind]
                        w = it.get("width", P)
                        if kind == "turn":
                            j = turns.index(i)
                            if j >= 2:
                                prev = items[turns[j - 2]]
                                act.wait_ge(*filled[prev["key"], "nat", prev["n"]])
                            dst, src = vt[0:w, slot[i], :], banks[key, n][0:w, :]
                        else:
                            dst, src = it["dst"], banks[key, n][:, :]
                        act.activation(dst, src, ACT.Copy, scale=it.get("scale", 1.0)).then_inc(*act_made.mark(mark))
                        banks.drain((key, n), "act_made")
                    if i:
                        act_after(act, i - 1)
                act_after(act, len(items) - 1)

            def dve_after(dve, i):
                it = items[i]
                key, n = it["key"], it["n"]
                if it["kind"] == "rope":
                    rope_parts(key, n, it["dst"], table)[1](dve, rtmp[:, ropes.index(i) % 2, :])
                elif it["kind"] == "turn" and "func" not in it:
                    dve.wait_ge(*filled[key, "nat", n])
                    dve.tensor_copy(it["dst"], turned_bank(key, n, it.get("width", P)))\
                       .then_inc(*dve_made.mark((key, "turned", n)))
                    banks.drain((key, "nat", n), "dve_made")
                elif it["kind"] == "own":
                    it["do"](dve)

            def dve_part(dve):
                for i, it in enumerate(items):
                    keep_up(dve, "dve", (it["key"], it["n"]))
                    if i:
                        dve_after(dve, i - 1)
                dve_after(dve, len(items) - 1)
            return act_part, pe_part, dve_part

        def item(key, n, kind, dst=None, **kw):
            return dict(key=key, n=n, kind=kind, dst=dst, **kw)

        def back_to_x(key, src, rows, ready, nxt, gate=None):
            def pe_part(pe):
                for n in range(KD):
                    pe_linear(pe, key, n, src, rows, ready if n == 0 else None)
                    if n >= 2 and nxt:
                        pe_mean(pe, nxt, n - 2)
                for k in (KD - 2, KD - 1) if nxt else ():
                    pe_mean(pe, nxt, k)

            def act_part(act):
                for n in range(KD):
                    keep_up(act, "act", (key, n))
                    if nxt:
                        act_square(act, nxt, xT, n, [dve_made[key, "x", n]])

            return act_part, pe_part, lambda dve: dve_residual(dve, key, gate)

        def dve_residual(dve, key, gate=None):
            for n in range(KD):
                dve_bank(dve, (key, n))
                bank = banks[key, n][:, :]
                if gate is None:
                    i = dve.tensor_tensor(xT[:, n, :], xT[:, n, :], bank, ALU.add)
                else:
                    i = dve.scalar_tensor_tensor(out=xT[:, n, :], in0=bank, scalar=gate(n), in1=xT[:, n, :],
                                                 op0=ALU.mult, op1=ALU.add)
                i.then_inc(*dve_made.mark((key, "x", n)))
                banks.drain((key, n), "dve_made")

        def x_after(key):
            return lambda k: [dve_made[key, "x", k]]

        def act_conv_start(act, key, n, cv, w, b, free):
            act_bank(act, (key, n))
            for f in free:
                act.wait_ge(*f)
            act.activation(cv, banks[key, n][:, :], ACT.Identity, bias=b, scale=w)\
               .then_inc(*act_made.mark((key, "tap", n)))

        def dve_conv_taps(dve, key, n, cv, ws):
            keep_up(dve, "dve", (key, n))
            dve.wait_ge(*act_made[key, "tap", n])
            for j, w in enumerate(ws):
                s = j + 1
                if j:
                    dve.wait_ge(*dve_made[key, "taps", n, j - 1])
                dve.scalar_tensor_tensor(out=cv[:, s:SEQ], in0=banks[key, n][:, 0:SEQ - s], scalar=w,
                                         in1=cv[:, s:SEQ], op0=ALU.mult, op1=ALU.add)\
                   .then_inc(*dve_made.mark((key, "taps", n, j)))
            banks.drain((key, n), "dve_made")

        def rope_parts(key, n, dst, table, width=SEQ):
            perm, cos, sin = table
            cos, sin = cos[:, 0:width], sin[:, 0:width]

            def pe_part(pe):
                pe.wait_ge(*act_made[key, "raw", n])
                bank = banks.take(pe, (key, "rot", n))
                mm(pe, bank[:, 0:width], lhsT=cst(perm), rhs=dst, start=True, stop=True, done=(key, "rot", n))

            def dve_part(dve, tmp):
                dve.wait_ge(*filled[key, "rot", n])
                dve.tensor_tensor(tmp, banks[key, "rot", n][:, 0:width], sin, ALU.mult)\
                   .then_inc(*dve_made.mark((key, "sin", n)))
                banks.drain((key, "rot", n), "dve_made")
                dve.tensor_tensor(dst, dst, cos, ALU.mult).then_inc(*dve_made.mark((key, "cos", n)))
                dve.wait_ge(*dve_made[key, "cos", n])
                dve.tensor_tensor(dst, dst, tmp, ALU.add).then_inc(*dve_made.mark((key, "roped", n)))
            return pe_part, dve_part

        prog = {"act": [], "pe": [], "dve": [], "pool": []}

        def then(parts=None, **kw):
            if parts is not None:
                prog["act"].append(parts[0])
                prog["pe"].append(parts[1])
                prog["dve"].append(parts[2])
            for e, f in kw.items():
                prog[e].append(f)

        A = Area()
        x_nat = A.take(NT, D)

        def pe_start(pe):
            pe.wait_ge(x_landed, 16)
            pe.wait_ge(const_landed, 48)

        def all_consts(eng):
            eng.wait_ge(const_landed, 48)

        then(pe=pe_start, act=all_consts, dve=all_consts, pool=all_consts)
        then(turned("x", x_nat, xT, KD, []))
        prog["pe"].append(lambda pe: [pe_mean(pe, "h0", k) for k in range(KD)])
        prog["act"].append(lambda act: [act_square(act, "h0", xT, k, [turned_at("x")(k)]) for k in range(KD)])
        prog["act"].append(lambda act: keep_up(act, "act", ("kvc", 0)))
        prog["dve"].append(lambda dve: keep_up(dve, "dve", ("kvc", 0)))

        then(norm("h0", ("attn_norm", 0)))
        A = Area()
        sq, sk = A.take(4, SEQ), A.take(4, SEQ)
        sv = A.take(NT, 512)
        nq = A.take(4, SEQ)
        onat = A.take(NT, D)
        nsa_at = A.at
        kvc = A.take(2, SEQ)
        ksw = A.take(2, SEQ)
        vsw = A.take(2, NT, P)
        gates = A.take(NT, 24)
        kcr = A.take(32)
        vcn = A.take(P)
        rtmp = A.take(2, SEQ)
        cpx, cpt = A.take(256), A.take(2, SEQ)
        vt = A.take(2, SEQ)
        kin = Area(A.at).take(2, CMP_LEN, NCMP)
        Pb, PT = A.take(3, SEQ), A.take(3, SEQ)
        ROPE8 = ("perm8", rot[:, 0, :], rot[:, 1, :])
        items = [item("kvc", n, "copy", kvc[:, n, :]) for n in range(2)]
        items += [item("ksw", n, "rope", ksw[:, n, :]) for n in range(2)]
        items += [item("nq", n, "rope", nq[:, n, :], scale=SCALE) for n in range(4)]
        items += [item("vsw", n, "turn", vsw[:, n, :, :]) for n in range(2)]
        items += [item("gates", 0, "turn", gates, width=24, func=ACT.Sigmoid)]
        items += [item("sk", n, "copy", sk[:, n, :]) for n in range(4)]
        items += [item("sq", n, "copy", sq[:, n, :], scale=SCALE) for n in range(4)]
        items += [item("sv", n, "turn", sv[:, :, n * P:(n + 1) * P]) for n in range(4)]

        def dve_rot(dve):
            dve.wait_ge(rot_landed, 16)

        then(dve=dve_rot)
        then(project(items, h_at("h0"), rtmp, vt, ROPE8))

        def dve_kin(dve):
            for n, name in enumerate(("pos_k", "pos_v")):
                dve.wait_ge(*act_made["kvc", n])
                o = VEC[name, 0]
                pos = vec[:, o:o + CMP_LEN].rearrange("p (l c) -> p l c", c=1).to_broadcast([P, CMP_LEN, NCMP])
                for half in range(2):
                    ls = slice(half * CMP_STRIDE, (half + 1) * CMP_STRIDE)
                    first = half * CMP_STRIDE
                    src = kvc[:, n, first:first + NCMP * CMP_STRIDE].rearrange("p (c l) -> p l c", l=CMP_STRIDE)
                    dve.tensor_tensor(kin[:, n, ls, :], src, pos[:, ls, :], ALU.add)\
                       .then_inc(*dve_made.mark(("kin", n, half)))

        then(dve=dve_kin)

        rope_c = rope_parts("kcr", 0, kcr[:, 0:NCMP], ("perm8", cst("cosc"), cst("sinc")), NCMP)

        def pe_compress(pe):
            for n in range(2):
                for half in range(2):
                    pe.wait_ge(*dve_made["kin", n, half])
                bank = banks.take(pe, ("cmp", n))
                for l in range(CMP_LEN):
                    w, ends = tile_of(pe)
                    a, b = (w, kin[:, n, l, :]) if n == 0 else (kin[:, n, l, :], w)
                    mm(pe, bank[:, 0:NCMP] if n == 0 else bank[0:NCMP, 0:P], lhsT=a, rhs=b, start=(l == 0),
                       stop=(l == CMP_LEN - 1), done=("cmp", n) if l == CMP_LEN - 1 else None, ends=ends)
            rope_c[0](pe)

        def act_compress(act):
            act.wait_ge(*filled["cmp", 0])
            act.activation(kcr[:, 0:NCMP], banks["cmp", 0][:, 0:NCMP], ACT.Copy)\
               .then_inc(*act_made.mark(("kcr", "raw", 0)))
            banks.drain(("cmp", 0), "act_made")
            act.wait_ge(*filled["cmp", 1])
            act.activation(vcn[0:NCMP, :], banks["cmp", 1][0:NCMP, 0:P], ACT.Copy).then_inc(*act_made.mark("vcn"))
            banks.drain(("cmp", 1), "act_made")

        def dve_compress(dve):
            rope_c[1](dve, rtmp[:, 0, 0:NCMP])

        then(pe=pe_compress, act=act_compress, dve=dve_compress)

        nmax, den, dzero = small[:, 0:8], small[:, 8:16], small[:, 16:24]

        def by_head(a, w=32):
            return a.rearrange("p (h c) -> p h c", h=8)

        def pe_cmp(pe):
            pe.wait_ge(*dve_made["kcr", "roped", 0])
            pe.wait_ge(*dve_made["nq", "roped", 3])
            pe.wait_ge(*act_made["vcn"])
            for qt in range(NT):
                for g in range(2):
                    r = slice(DH * g, DH * g + DH)
                    bank = banks.take(pe, ("cs", qt, g))
                    mm(pe, bank[:, 0:P], lhsT=identb, rhs=cstb("cmp")[:, qt * P:(qt + 1) * P], start=True, stop=False)
                    for c in range(4):
                        mm(pe, bank[:, 32 * c:32 * c + NCMP], lhsT=nq[r, c, qt * P:(qt + 1) * P], rhs=kcr[r, 0:NCMP],
                           start=False, stop=(c == 3), done=("cs", qt, g) if c == 3 else None)
                pe.wait_ge(*dve_made["c01", qt])
                for half in range(2):
                    bank = banks.take(pe, ("ct", qt, half))
                    for j in range(4):
                        h = 4 * half + j
                        tp(pe, bank[0:32, j * P:(j + 1) * P], cpx[:, 32 * h:32 * h + 32], ident,
                           done=("ct", qt, half) if j == 3 else None)
                bank = banks.take(pe, ("co", qt))
                for h in range(8):
                    if h % 4 == 0:
                        pe.wait_ge(*act_made["cpt", qt, h // 4])
                    g = h // 4
                    mm(pe, bank[:, h * DH:(h + 1) * DH], lhsT=cpt[0:NCMP, h // 4, (h % 4) * P:(h % 4 + 1) * P],
                       rhs=vcn[0:NCMP, g * DH:(g + 1) * DH], start=True, stop=True,
                       done=("co", qt) if h == 7 else None)

        def act_cmp(act):
            for qt in range(NT):
                act.wait_ge(*dve_made["csub", qt, 1])
                act.activation(cpx, cpx, ACT.Exp).then_inc(*act_made.mark(("cexp", qt)))
                for half in range(2):
                    act.wait_ge(*filled["ct", qt, half])
                    if qt:
                        act.wait_ge(*filled["co", qt - 1])
                    act.activation(cpt[0:32, half, :], banks["ct", qt, half][0:32, :], ACT.Copy)\
                       .then_inc(*act_made.mark(("cpt", qt, half)))
                    banks.drain(("ct", qt, half), "act_made")

        def dve_cmp(dve):
            for qt in range(NT):
                if qt:
                    dve.wait_ge(*filled["ct", qt - 1, 1])
                for g in range(2):
                    dve.wait_ge(*filled["cs", qt, g])
                    bank = banks["cs", qt, g][:, 0:P].rearrange("p (h c) -> p h c", h=4)
                    mine = nmax[:, 4 * g:4 * g + 4]
                    dve.tensor_reduce(mine, bank, AX.X, ALU.max, negate=True)\
                       .then_inc(*dve_made.mark(("cmax", qt, g)))
                    dve.wait_ge(*dve_made["cmax", qt, g])
                    dve.tensor_tensor(cpx[:, P * g:P * g + P].rearrange("p (h c) -> p h c", h=4), bank,
                                      mine.rearrange("p (h c) -> p h c", c=1).to_broadcast([P, 4, 32]), ALU.add)\
                       .then_inc(*dve_made.mark(("csub", qt, g)))
                    banks.drain(("cs", qt, g), "dve_made")
                dve.wait_ge(*act_made["cexp", qt])
                o = CF["cmp01"][0] + 32 * qt
                seen = cf[:, o:o + 32].rearrange("p (h c) -> p h c", h=1).to_broadcast([P, 8, 32])
                dve.tensor_tensor(by_head(cpx), by_head(cpx), seen, ALU.mult).then_inc(*dve_made.mark(("c01", qt)))
                dve.wait_ge(*dve_made["c01", qt])
                dve.tensor_reduce(den, by_head(cpx), AX.X, ALU.add).then_inc(*dve_made.mark(("cden", qt)))
                dve.wait_ge(*dve_made["cden", qt])
                dve.tensor_scalar(dzero, den, 0.0, None, ALU.is_equal).then_inc(*dve_made.mark(("cz", qt)))
                dve.wait_ge(*dve_made["cz", qt])
                dve.tensor_tensor(den, den, dzero, ALU.add).then_inc(*dve_made.mark(("cd1", qt)))
                dve.wait_ge(*dve_made["cd1", qt])
                dve.reciprocal(den, den).then_inc(*dve_made.mark(("cinv", qt)))
                dve.wait_ge(*dve_made["cinv", qt])
                if qt == 0:
                    dve.wait_ge(*act_made["gates", "turned", 0])
                dve.tensor_tensor(den, den, gates[:, qt, 0:24:3], ALU.mult).then_inc(*dve_made.mark(("cg", qt)))
                dve.wait_ge(*dve_made["cg", qt])
                dve.wait_ge(*filled["co", qt])
                dve.tensor_tensor(onat[:, qt, 512:1024].rearrange("p (h c) -> p h c", h=8),
                                  by_head(banks["co", qt][:, :]),
                                  den.rearrange("p (h c) -> p h c", c=1).to_broadcast([P, 8, DH]), ALU.mult)\
                   .then_inc(*dve_made.mark(("cout", qt)))
                banks.drain(("co", qt), "dve_made")

        then(pe=pe_cmp, act=act_cmp, dve=dve_cmp)

        def small_cols(base, i, n=3):
            return small[:, base + i % n:base + i % n + 1]

        maps = []
        for b in range(2):
            for h in range(8):
                g, c = divmod(h, 4)
                r = slice(DH * g, DH * g + DH)
                for qt in range(NT):
                    W = (qt + 1) * P
                    maps.append(dict(
                        q=nq[r, c, qt * P:W], k=ksw[r, b, 0:W], width=W,
                        masks=[(identb, cstb("causal"), qt * P, ())],
                        v=lambda t, b=b, g=g: vsw[:, b, t, g * DH:(g + 1) * DH],
                        out=onat[:, qt, 512 + h * DH:512 + (h + 1) * DH],
                        gate=gates[:, qt, 3 * h + 1 + b:3 * h + 2 + b],
                        add=dve_made["cout", qt] if b == 0 else dve_made["nsa", "out", h * NT + qt]))
        then(softmax_maps("nsa", maps, Pb, PT, lambda i: small_cols(32, i), lambda i: small_cols(36, i, 6),
                          [dve_made["vsw", "turned", 1], dve_made["nq", "roped", 3]]))

        A = Area(nsa_at)
        za = A.take(2, SEQ)
        sp = A.take(2, NT, SEQ)
        aa = A.take(NT, SEQ)

        def pe_sb(pe):
            pe.wait_ge(*dve_made["sv", "turned", 3])

            def scores(h):
                r = slice(DH * (h % 2), DH * (h % 2) + DH)
                for kt in range(NT - 1, -1, -1):
                    bank = banks.take(pe, ("z", h, kt))
                    mm(pe, bank[:, kt * P:SEQ], lhsT=sk[r, h // 2, kt * P:(kt + 1) * P], rhs=sq[r, h // 2, kt * P:SEQ],
                       start=True, stop=True, done=("z", h, kt))

            def sums(h):
                for kt in range(NT - 1, -1, -1):
                    bank = banks["z", h, kt]
                    pe.wait_ge(*pool_made["sp", h, kt])
                    mm(pe, bank[:, kt * P:(kt + 1) * P], lhsT=identb, rhs=cstb("strictT"), start=False, stop=False,
                       skip_group_check=True)
                    mm(pe, bank[:, kt * P:SEQ], lhsT=cst("tri"), rhs=sp[:, h % 2, kt, kt * P:SEQ], start=False,
                       stop=(kt == NT - 1), skip_group_check=True, done=("r", h, kt) if kt == NT - 1 else None)
                    for jt in range(kt + 1, NT):
                        mm(pe, bank[:, jt * P:SEQ], lhsT=cst("nones"), rhs=sp[:, h % 2, jt, jt * P:SEQ], start=False,
                           stop=(jt == NT - 1), skip_group_check=True, done=("r", h, kt) if jt == NT - 1 else None)

            def values(h):
                for kt in range(NT):
                    pe.wait_ge(*act_made["a", h, kt])
                bank = banks.take(pe, ("so", h))
                for qt in range(NT):
                    for kt in range(qt + 1):
                        mm(pe, bank[:, qt * DH:(qt + 1) * DH], lhsT=aa[:, kt, qt * P:(qt + 1) * P],
                           rhs=sv[:, kt, h * DH:(h + 1) * DH], start=(kt == 0), stop=(kt == qt),
                           done=("so", h) if (qt, kt) == (NT - 1, NT - 1) else None)

            scores(0)
            for h in range(8):
                sums(h)
                if h + 1 < 8:
                    scores(h + 1)
                values(h)

        def act_sb(act):
            act.wait_ge(*filled["nsa", "o", 63])
            for h in range(8):
                for kt in range(NT - 1, -1, -1):
                    b = kt % 2
                    z = banks["z", h, kt][:, kt * P:SEQ]
                    t = za[:, b, kt * P:SEQ]
                    act.wait_ge(*filled["z", h, kt])
                    if h or kt < NT - 2:
                        prev = (h, kt + 2) if kt + 2 < NT else (h - 1, kt - 2)
                        act.wait_ge(*dve_made["sp0", prev[0], prev[1]])
                    act.activation(t, z, ACT.Abs).then_inc(*act_made.mark(("z1", h, kt)))
                    act.wait_ge(*act_made["z1", h, kt])
                    act.activation(t, t, ACT.Exp, scale=-1.0).then_inc(*act_made.mark(("z2", h, kt)))
                    act.wait_ge(*act_made["z2", h, kt])
                    act.activation(t, t, ACT.Ln, bias=1.0).then_inc(*act_made.mark(("z3", h, kt)))
                for kt in range(NT - 1, -1, -1):
                    act.wait_ge(*filled["r", h, kt])
                    if h:
                        act.wait_ge(*filled["so", h - 1])
                    act.activation(aa[:, kt, kt * P:SEQ], banks["z", h, kt][:, kt * P:SEQ], ACT.Exp)\
                       .then_inc(*act_made.mark(("a", h, kt)))
                    banks.drain(("z", h, kt), "act_made")

        def dve_sb(dve):
            for h in range(8):
                for kt in range(NT - 1, -1, -1):
                    dve.wait_ge(*act_made["z3", h, kt])
                    if h >= 2:
                        dve.wait_ge(*filled["r", h - 2, 0])
                    dve.scalar_tensor_tensor(out=sp[:, h % 2, kt, kt * P:SEQ], in0=banks["z", h, kt][:, kt * P:SEQ],
                                             scalar=0.0, in1=za[:, kt % 2, kt * P:SEQ], op0=ALU.max, op1=ALU.add)\
                       .then_inc(*dve_made.mark(("sp0", h, kt)))
                dve.wait_ge(*filled["so", h])
                dve.tensor_copy(onat[:, :, h * DH:(h + 1) * DH],
                                banks["so", h][:, 0:NT * DH].rearrange("p (t c) -> p t c", t=NT))\
                   .then_inc(*dve_made.mark(("sbout", h)))
                banks.drain(("so", h), "dve_made")

        def pool_sb(pool):
            for h in range(8):
                for kt in range(NT - 1, -1, -1):
                    pool.wait_ge(*dve_made["sp0", h, kt])
                    d = sp[:, h % 2, kt, kt * P:(kt + 1) * P]
                    pool.tensor_tensor(d, d, cst("strict"), ALU.mult).then_inc(*pool_made.mark(("sp", h, kt)))

        then(pe=pe_sb, act=act_sb, dve=dve_sb, pool=pool_sb)

        oT = Area().take_r(2, KD, SEQ)
        then(act=lambda act: keep_up(act, "act", ("mix0", 0)), dve=lambda dve: keep_up(dve, "dve", ("mix0", 0)))
        then(turned_parts("ot0", onat, oT, [dve_made["sbout", 7], dve_made["nsa", "out", 63]]))
        then(back_to_x("mix0", oT, KD, lo_of("ot0"), "f0"))

        csil, mod, gsc = small[:, 64:72], small[:, 80:128], small[:, 128:144]
        prog["act"].insert(1, lambda act: act.activation(csil, vec[:, VEC["c", 0]:VEC["c", 0] + KD], ACT.Silu)
                           .then_inc(*act_made.mark("csil")))

        def ffn(layer, nxt, hfree, arena_free):
            key = f"f{layer}"
            then(norm(key, ("ffn_norm", layer), hfree))
            A = Area()
            gT = A.take_r(2, FH, SEQ)
            cv = A.take(3, SEQ)
            sl = A.take(3, SEQ)
            acc = A.take(D)

            def dve_ada(dve, step):
                l, b, k = step
                panel = ada_panel[step]
                landed(dve, panel)
                w = ring[:, panel % RAW, :, :].rearrange("p a b -> p (a b)")
                if k == 0:
                    dve.wait_ge(*act_made["csil"])
                    if b:
                        dve.wait_ge(*filled["mod", l, b - 1])
                    i = dve.tensor_scalar(acc, w, csil[:, 0:1], None, ALU.mult)
                else:
                    dve.wait_ge(*dve_made["ada", l, b, k - 1])
                    i = dve.scalar_tensor_tensor(out=acc, in0=w, scalar=csil[:, k:k + 1], in1=acc, op0=ALU.mult,
                                                 op1=ALU.add)
                i.then_inc(*dve_made.mark(("ada", l, b, k)))
                dve_made.at["ada panel", panel] = dve_made.count

            def pe_ada(pe, l, b):
                pe.wait_ge(*dve_made["ada", l, b, KD - 1])
                bank = banks.take(pe, ("mod", l, b))
                for i in range(KD):
                    mm(pe, bank[:, i:i + 1], lhsT=acc[:, i * P:(i + 1) * P], rhs=cst("ones")[:, 0:1], start=True,
                       stop=True, done=("mod", l, b) if i == KD - 1 else None)

            def dve_mod(dve, l, b):
                dve.wait_ge(*filled["mod", l, b])
                o = VEC["b_ada", l] + KD * b
                m = 24 * l + KD * b
                dve.tensor_tensor(mod[:, m:m + KD], banks["mod", l, b][:, 0:KD], vec[:, o:o + KD], ALU.add)\
                   .then_inc(*dve_made.mark(("mod", l, b)))
                banks.drain(("mod", l, b), "dve_made")
                if b == 1:
                    dve.wait_ge(*dve_made["mod", l, b])
                    o = VEC["norm_g", l]
                    dve.scalar_tensor_tensor(out=gsc[:, 8 * l:8 * l + 8], in0=mod[:, m:m + KD], scalar=1.0,
                                             in1=vec[:, o:o + 8], op0=ALU.add, op1=ALU.mult)\
                       .then_inc(*dve_made.mark(("gsc", l)))
                    dve.wait_ge(*dve_made["gsc", l])

            complete = {n: b for n in range(FC) for _, b, k in ada_steps(layer, n) if k == KD - 1}
            final = max(complete)

            def parts(first):
                chunks = range(first, first + FH)

                def pe_part(pe):
                    for n in chunks:
                        pe_linear(pe, (key, "a"), n, hT, KD, h_at(key) if n == 0 else None)
                        pe_linear(pe, (key, "b"), n, hT, KD, None)
                        for _ in ada_steps(layer, n):
                            tile_no[0] += KD
                        if n - 1 in complete:
                            pe_ada(pe, layer, complete[n - 1])

                def act_g(act, n):
                    act.wait_ge(*dve_made[key, "g", n])
                    act_hi(act, gT[:, 0, n % FH, :], sl[:, n % 3, :], (key, "g", n))

                def act_part(act):
                    if first == 0:
                        act.wait_ge(*arena_free)
                    for n in chunks:
                        if n > first:
                            act_g(act, n - 1)
                        free = [act_made[(key, "a"), "silu", n - 3]] if n >= 3 else []
                        act_conv_start(act, (key, "a"), n, cv[:, n % 3, :], col("conv_w", (layer, 2), n),
                                       col("conv_b", layer, n), free)
                        act.wait_ge(*dve_made[(key, "a"), "taps", n, 1])
                        if n >= 3:
                            act.wait_ge(*dve_made[(key, "g", n - 3), "lo"])
                        act.activation(sl[:, n % 3, :], cv[:, n % 3, :], ACT.Silu)\
                           .then_inc(*act_made.mark(((key, "a"), "silu", n)))
                        keep_up(act, "act", ((key, "b"), n))
                    act_g(act, chunks[-1])

                def dve_part(dve):
                    def lo(n):
                        dve_lo(dve, gT[:, 0, n % FH, :], gT[:, 1, n % FH, :], sl[:, n % 3, :], (key, "g", n))
                    for n in chunks:
                        if n > first:
                            lo(n - 1)
                        dve_conv_taps(dve, (key, "a"), n, cv[:, n % 3, :],
                                      [col("conv_w", (layer, 1), n), col("conv_w", (layer, 0), n)])
                        dve.wait_ge(*act_made[(key, "a"), "silu", n])
                        dve_bank(dve, ((key, "b"), n))
                        dve.tensor_tensor(sl[:, n % 3, :], sl[:, n % 3, :], banks[(key, "b"), n][:, :], ALU.mult)\
                           .then_inc(*dve_made.mark((key, "g", n)))
                        banks.drain(((key, "b"), n), "dve_made")
                        if n - 1 in complete:
                            dve_mod(dve, layer, complete[n - 1])
                        for step in ada_steps(layer, n):
                            dve_ada(dve, step)
                    lo(chunks[-1])
                return act_part, pe_part, dve_part

            then(parts(0))
            then(back_to_x((key, "y0"), gT, FH, lambda k: dve_made[(key, "g", k), "lo"], None))
            then(parts(FH))
            if final == FC - 1:
                then(pe=lambda pe: pe_ada(pe, layer, complete[final]), dve=lambda dve: dve_mod(dve, layer, complete[final]))
            then(back_to_x((key, "y"), gT, FH, lambda k: dve_made[(key, "g", FH + k), "lo"], nxt))

        ffn(0, "h1", filled["sv", 3], filled["mix0", KD - 1])

        def act_rot(act):
            act.wait_ge(*dve_made["nq", "roped", 3])
            act.dma_start(rot[:, :, :].rearrange("p a b -> p (a b)"), rot_in[:, 2 * SEQ:4 * SEQ]).then_inc(rot_landed, 16)

        then(act=act_rot)

        then(norm("h1", ("attn_norm", 1), filled[("f0", "b"), FC - 1]))
        A = Area()
        q1, k1 = A.take(KD, SEQ), A.take(KD, SEQ)
        v1 = A.take(NT, D)
        onat1 = A.take(NT, D)
        Pb1, PT1 = A.take(3, SEQ), A.take(3, SEQ)
        rest, rest2 = PT1[:, 0, :], PT1[:, 1, :]
        ff, lf, cum = A.take(SEQ), A.take(SEQ), A.take(SEQ)
        parts3 = A.take16(SEQ)
        vt1 = A.take(2, SEQ)
        oT1 = Area().take_r(2, KD, SEQ)

        def act_f(act):
            act.wait_ge(*dve_made["f+b"])
            act.activation(lf[0:16, :], ff[0:16, :], ACT.Abs).then_inc(*act_made.mark("f1"))
            act.wait_ge(*act_made["f1"])
            act.activation(lf[0:16, :], lf[0:16, :], ACT.Exp, scale=-1.0).then_inc(*act_made.mark("f2"))
            act.wait_ge(*act_made["f2"])
            act.activation(lf[0:16, :], lf[0:16, :], ACT.Ln, bias=1.0).then_inc(*act_made.mark("f3"))

        def dve_f(dve):
            dve.wait_ge(*filled["f", 0])
            dve.tensor_scalar(ff[0:16, :], banks["f", 0][0:16, :], col("b_f", 0, 0, 16), None, ALU.add)\
               .then_inc(*dve_made.mark("f+b"))
            banks.drain(("f", 0), "dve_made")
            dve.memset(parts3[0:96, :], 0.0).then_inc(*dve_made.mark("p0"))

        def dve_cum(dve):
            dve.wait_ge(*act_made["f3"])
            dve.scalar_tensor_tensor(out=lf[0:16, :], in0=ff[0:16, :], scalar=0.0, in1=lf[0:16, :], op0=ALU.min,
                                     op1=ALU.subtract).then_inc(*dve_made.mark("lf"))
            dve.wait_ge(*dve_made["lf"])
            dve.tensor_tensor_scan(cum[0:16, :], cst("ones")[0:16, 0:1].to_broadcast([16, SEQ]), lf[0:16, :], 0.0, ALU.mult, ALU.add)\
               .then_inc(*dve_made.mark("cum"))
            dve.wait_ge(*dve_made["cum"])
            dve.tensor_copy(parts3[0:16, :], cum[0:16, :]).then_inc(*dve_made.mark("hi"))
            dve.wait_ge(*dve_made["hi"])
            dve.tensor_tensor(rest[0:16, :], cum[0:16, :], parts3[0:16, :], ALU.subtract)\
               .then_inc(*dve_made.mark("rest"))
            dve.wait_ge(*dve_made["rest"])
            dve.tensor_copy(rest2[0:16, :].bitcast(BF16)[:, 0:SEQ], rest[0:16, :]).then_inc(*dve_made.mark("mid"))
            dve.wait_ge(*dve_made["mid"])
            dve.tensor_copy(parts3[32:48, :], rest2[0:16, :].bitcast(BF16)[:, 0:SEQ]).then_inc(*dve_made.mark("midp"))
            dve.tensor_tensor(rest[0:16, :], rest[0:16, :], rest2[0:16, :].bitcast(BF16)[:, 0:SEQ], ALU.subtract)\
               .then_inc(*dve_made.mark("rest2"))
            dve.wait_ge(*dve_made["rest2"])
            dve.tensor_copy(parts3[64:80, :], rest[0:16, :]).then_inc(*dve_made.mark("lo"))

        items = [item("f", 0, "own", do=dve_f)]
        for c in range(KD):
            items += [item("q1", c, "copy", q1[:, c, :], scale=SCALE), item("k1", c, "copy", k1[:, c, :]),
                      item("v1", c, "turn", v1[:, :, c * P:(c + 1) * P])]
        then(act=lambda act: act.wait_ge(*filled[("f0", "y"), KD - 1]), dve=lambda dve: dve.wait_ge(*filled[("f0", "y"), KD - 1]))
        then(project(items, h_at("h1"), None, vt1))
        then(act=act_f, dve=dve_cum)

        maps = []
        for h in range(16):
            r = slice(DH * (h % 2), DH * (h % 2) + DH)
            for qt in range(NT):
                W = (qt + 1) * P
                maps.append(dict(
                    q=q1[r, h // 2, qt * P:W], k=k1[r, h // 2, 0:W], width=W,
                    masks=[(cstb("selneg")[0:96, h:h + 1].to_broadcast([96, P]), parts3[0:96, 0:W], 0, ()),
                           (identb, cstb("causal"), qt * P, ())],
                    v=lambda t, h=h: v1[:, t, h * DH:(h + 1) * DH],
                    out=onat1[:, qt, h * DH:(h + 1) * DH], gate=None, add=None))
        then(softmax_maps("fox", maps, Pb1, PT1, lambda i: small_cols(32, i), lambda i: small_cols(36, i, 6),
                          [dve_made["v1", "turned", KD - 1], dve_made["lo"]]))
        then(turned_parts("ot1", onat1, oT1, [dve_made["fox", "out", 63]]))
        then(back_to_x("mix1", oT1, KD, lo_of("ot1"), "f1"))
        ffn(1, "xn", filled["v1", KD - 1], filled["mix1", KD - 1])

        then(norm("xn", ("final_norm", 0), to_x=True))
        then(act=lambda act: [act_square(act, "L0h", xT, k, [dve_made["xn", "scaled", k]]) for k in range(KD)],
             pe=lambda pe: [pe_mean(pe, "L0h", k) for k in range(KD)])

        ROPE32 = ("perm32", rot[:, 0, :], rot[:, 1, :])

        def block2(l, nxt, hfree, arena_free):
            K = f"L{l}"
            hk = K + "h"
            then(norm(hk, None, hfree,
                      mod=(lambda k: gsc[:, 8 * l + k:8 * l + k + 1],
                           lambda k: mod[:, 24 * l + k:24 * l + k + 1])))
            A = Area()
            qi, ki = A.take(2, SEQ), A.take(SEQ)
            q, k_ = A.take(4, SEQ), A.take(SEQ)
            v = A.take(NT, DH)
            wi = A.take(NT, 4)
            xbc_at = A.at
            xbc = A.take(12, SEQ)
            oT_at = A.at
            oT = A.take(4, SEQ)
            gate_at = A.at
            mask = A.take16(3 * SEQ)
            dts = A.take(4, SEQ)
            tops = A.take(16, 8)
            work = A.at
            score = A.take(3, SEQ)
            cvb = Area(A.at).take(3, SEQ)
            onat = A.take(NT, 512)
            Pb = A.take(3, SEQ)
            rtmp = relu = Area(A.at).take(2, SEQ)
            PT = A.take(3, SEQ)

            xw = lambda j, n: col("xconv_w", (l, j), n)

            def dve_dt(dve):
                dve.wait_ge(*filled[K + "dt", 0])
                dve.tensor_scalar(dts[0:16, 0, :], banks[K + "dt", 0][0:16, :], col("dt_bias", l, 0, 16), None,
                                  ALU.add).then_inc(*dve_made.mark(K + "dtb"))
                banks.drain((K + "dt", 0), "dve_made")

            items = [item(K + "qi", n, "rope", qi[:, n, :]) for n in range(2)]
            items += [item(K + "ki", 0, "rope", ki), item(K + "wi", 0, "turn", wi, width=4, scale=0.5)]
            items += [item(K + "q", n, "rope", q[:, n, :], scale=SCALE) for n in range(4)]
            items += [item(K + "k", 0, "rope", k_), item(K + "v", 0, "turn", v, width=DH)]
            items += [item(K + "dt", 0, "own", do=dve_dt)]
            then(act=lambda act: act.wait_ge(*arena_free), dve=lambda dve: dve.wait_ge(*arena_free))
            if l == 0:
                then(dve=lambda dve: dve.wait_ge(rot_landed, 32))
            then(project(items, h_at(hk), rtmp, cvb, ROPE32))

            def pe_in(pe):
                for n in range(12):
                    pe_linear(pe, K + "xbc", n, hT, KD, None)

            def act_in(act):
                t = dts[0:16, 1, :]
                act.wait_ge(*dve_made[K + "dtb"])
                act.activation(t, dts[0:16, 0, :], ACT.Abs).then_inc(*act_made.mark(K + "d1"))
                act.wait_ge(*act_made[K + "d1"])
                act.activation(t, t, ACT.Exp, scale=-1.0).then_inc(*act_made.mark(K + "d2"))
                act.wait_ge(*act_made[K + "d2"])
                act.activation(t, t, ACT.Ln, bias=1.0).then_inc(*act_made.mark(K + "d3"))
                act.activation(small[0:16, 160:161], col("a_log", l, 0, 16), ACT.Exp)\
                   .then_inc(*act_made.mark(K + "ea"))
                for n in range(12):
                    free = [act_made[K + "xbc", "silu", n - 3]] if n >= 3 else [filled[K + "v", "nat", 0]]
                    act_conv_start(act, K + "xbc", n, cvb[:, n % 3, :], xw(3, n), col("xconv_b", l, n), free)
                    act.wait_ge(*dve_made[K + "xbc", "taps", n, 2])
                    act.activation(xbc[:, n, :], cvb[:, n % 3, :], ACT.Silu)\
                       .then_inc(*act_made.mark((K + "xbc", "silu", n)))
                for t in range(NT):
                    s = slice(t * P, (t + 1) * P)
                    act.wait_ge(*dve_made[K + "acs", t])
                    act.activation(dts[0:16, 2, s], dts[0:16, 3, s], ACT.Exp, scale=-1.0,
                                   bias=dts[0:16, 3, t * P + P - 1:t * P + P]).then_inc(*act_made.mark((K + "ds", t)))

            def dve_in(dve):
                dt, t, acs = dts[0:16, 0, :], dts[0:16, 1, :], dts[0:16, 3, :]
                dve.wait_ge(*act_made[K + "ea"])
                dve.scalar_tensor_tensor(out=dt, in0=dt, scalar=0.0, in1=t, op0=ALU.max, op1=ALU.add)\
                   .then_inc(*dve_made.mark(K + "dt"))
                dve.wait_ge(*dve_made[K + "dt"])
                dve.tensor_scalar(t, dt, small[0:16, 160:161], -1.0, ALU.mult, ALU.mult)\
                   .then_inc(*dve_made.mark(K + "adt"))
                dve.wait_ge(*dve_made[K + "adt"])
                for c in range(NT):
                    s = slice(c * P, (c + 1) * P)
                    dve.tensor_tensor_scan(acs[:, s], cst("ones")[0:16, :], t[:, s], 0.0, ALU.mult, ALU.add)\
                       .then_inc(*dve_made.mark((K + "acs", c)))
                for n in range(12):
                    dve_conv_taps(dve, K + "xbc", n, cvb[:, n % 3, :], [xw(2, n), xw(1, n), xw(0, n)])

            then(pe=pe_in, act=act_in, dve=dve_in)

            def pe_index(pe):
                pe.wait_ge(*dve_made[K + "ki", "roped", 0])
                for qt in range(1, NT):
                    W = (qt + 1) * P
                    for h in range(4):
                        r = slice(DH * (h % 2), DH * (h % 2) + DH)
                        bank = banks.take(pe, (K + "ix", qt, h))
                        mm(pe, bank[:, 0:W], lhsT=qi[r, h // 2, qt * P:W], rhs=ki[r, 0:W], start=True, stop=True,
                           done=(K + "ix", qt, h))

            def act_index(act):
                for qt in range(1, NT):
                    W = (qt + 1) * P
                    for h in range(4):
                        i = (qt - 1) * 4 + h
                        act.wait_ge(*filled[K + "ix", qt, h])
                        if i >= 2:
                            act.wait_ge(*dve_made[K + "sc", (i - 2) // 4 + 1, (i - 2) % 4])
                        act.activation(relu[:, i % 2, 0:W], banks[K + "ix", qt, h][:, 0:W], ACT.Relu, scale=SCALE)\
                           .then_inc(*act_made.mark((K + "relu", qt, h)))
                        banks.drain((K + "ix", qt, h), "act_made")

            def dve_index(dve):
                for qt in range(1, NT):
                    W = (qt + 1) * P
                    sc = score[:, qt - 1, 0:W]
                    for h in range(4):
                        i = (qt - 1) * 4 + h
                        dve.wait_ge(*act_made[K + "relu", qt, h])
                        w = wi[:, qt, h:h + 1]
                        if h == 0:
                            j = dve.tensor_scalar(sc, relu[:, i % 2, 0:W], w, None, ALU.mult)
                        else:
                            dve.wait_ge(*dve_made[K + "sc", qt, h - 1])
                            j = dve.scalar_tensor_tensor(out=sc, in0=relu[:, i % 2, 0:W], scalar=w, in1=sc,
                                                         op0=ALU.mult, op1=ALU.add)
                        j.then_inc(*dve_made.mark((K + "sc", qt, h)))
                for qt in range(1, NT):
                    W = (qt + 1) * P
                    sc = score[:, qt - 1, 0:W]
                    dve.wait_ge(*pool_made[K + "adm", qt])
                    for r in range(TOPK // 8):
                        if r:
                            dve.wait_ge(*dve_made[K + "rep", qt, r - 1])
                        dve.max(tops[:, r, :], sc).then_inc(*dve_made.mark((K + "top", qt, r)))
                        dve.wait_ge(*dve_made[K + "top", qt, r])
                        dve.match_replace(sc, tops[:, r, :], sc, TAKEN).then_inc(*dve_made.mark((K + "rep", qt, r)))
                    dve.wait_ge(*dve_made[K + "rep", qt, TOPK // 8 - 1])
                    dve.tensor_scalar(mask[:, (qt - 1) * SEQ:(qt - 1) * SEQ + W], sc, TAKEN / 2, NEG, ALU.is_gt,
                                      ALU.mult).then_inc(*dve_made.mark((K + "mask", qt)))

            def pool_index(pool):
                for qt in range(1, NT):
                    d = score[:, qt - 1, qt * P:(qt + 1) * P]
                    pool.wait_ge(*dve_made[K + "sc", qt, 3])
                    pool.affine_select(out=d, in_=d, compare_op=ALU.is_ge, fill=NEG, base=0, pattern=[[-1, P]],
                                       channel_multiplier=1).then_inc(*pool_made.mark((K + "adm", qt)))

            then(pe=pe_index, act=act_index, dve=dve_index, pool=pool_index)

            maps = []
            for h in range(8):
                r = slice(DH * (h % 2), DH * (h % 2) + DH)
                for qt in range(NT):
                    W = (qt + 1) * P
                    if qt == 0:
                        ms = [(identb, cstb("causal"), 0, ())]
                    else:
                        ms = [(identb, mask[:, (qt - 1) * SEQ:(qt - 1) * SEQ + W], 0, (dve_made[K + "mask", qt],))]
                    maps.append(dict(q=q[r, h // 2, qt * P:W], k=k_[r, 0:W], width=W, masks=ms,
                                     v=lambda t: v[:, t, :], out=onat[:, qt, h * DH:(h + 1) * DH],
                                     gate=None, add=None))
            then(softmax_maps(K + "dsa", maps, Pb, PT, lambda i: small_cols(32, i), lambda i: small_cols(36, i, 6),
                              [dve_made[K + "v", "turned", 0], dve_made[K + "k", "roped", 0]]))
            then(turned(K + "ot", onat, oT, 4, [dve_made[K + "dsa", "out", 31]]))

            A = Area(work)
            xd = A.take(NT, D)
            st = A.take(3, D)
            bn = hv[:, 0:2, :].rearrange("p a (t w) -> p (a t) w", t=2)
            cbt = hv[:, 2:4, :]
            B = Area()
            xds, eb, dg, ce = (B.take(2, SEQ) for _ in range(4))
            natd = B.take(3, NT, 16)
            lastd = B.take(16, NT)
            cd = small[:, 168:232].rearrange("p (h t) -> p h t", h=16)
            after_att = [filled[K + "ot", 3]]

            def pe_ssd(pe):
                for n in range(12):
                    pe.wait_ge(*act_made[K + "xbc", "silu", n])
                for t in range(NT):
                    pe.wait_ge(*act_made[K + "ds", t])
                bank = banks.take(pe, (K + "nat", 0))
                for j, row in enumerate((0, 3, 2)):
                    for t in range(NT):
                        o = (j * NT + t) * 16
                        tp(pe, bank[:, o:o + 16], dts[0:16, row, t * P:(t + 1) * P], ident[0:16, 0:16],
                           done=(K + "nat", 0) if (j, t) == (2, NT - 1) else None)
                pe.wait_ge(*dve_made[K + "lastd"])
                bank = banks.take(pe, (K + "last", 0))
                mm(pe, bank[:, 0:16 * NT], lhsT=cst("ones")[0:16, 0:P], rhs=lastd[0:16, :, :].rearrange("p a b -> p (a b)"),
                   start=True, stop=True, done=(K + "last", 0))
                for g in range(2):
                    bank = banks.take(pe, (K + "cb", g))
                    for t in range(NT):
                        s = slice(t * P, (t + 1) * P)
                        mm(pe, bank[:, s], lhsT=xbc[:, 8 + g, s], rhs=xbc[:, 10 + g, s], start=True, stop=True,
                           done=(K + "cb", g) if t == NT - 1 else None)
                    bank = banks.take(pe, (K + "bn", g))
                    for t in range(NT):
                        s = slice(t * P, (t + 1) * P)
                        tp(pe, bank[:, s], xbc[:, 8 + g, s], ident, done=(K + "bn", g) if t == NT - 1 else None)
                for t in range(NT):
                    for half in range(2):
                        bank = banks.take(pe, (K + "xt", t, half))
                        for j in range(4):
                            tp(pe, bank[:, j * P:(j + 1) * P], xbc[:, half * 4 + j, t * P:(t + 1) * P], ident,
                               done=(K + "xt", t, half) if j == 3 else None)
                for g in range(2):
                    pe.wait_ge(*act_made[K + "bn", g])
                for t in range(NT - 1):
                    for g in range(2):
                        pe.wait_ge(*dve_made[K + "xds", t, g])
                        bank = banks.take(pe, (K + "st", t, g))
                        mm(pe, bank[:, :], lhsT=bn[:, t, g * P:(g + 1) * P], rhs=xds[:, g, :], start=True, stop=True,
                           done=(K + "st", t, g))

                def spread(h):
                    bank = banks.take(pe, (K + "bc", h))
                    mm(pe, bank[:, :], lhsT=ident[0:16, h:h + 1].to_broadcast([16, P]), rhs=dts[0:16, 3, :], start=True,
                       stop=True, done=(K + "bc", h))

                spread(0)
                spread(1)
                pe.wait_ge(*dve_made[K + "st", NT - 2, 1])
                for h in range(16):
                    if h + 2 < 16:
                        spread(h + 2)
                    r = slice(DH * (h % 2), DH * (h % 2) + DH)
                    if h % 2 == 0:
                        bank = banks.take(pe, (K + "y", h // 2))
                    pe.wait_ge(*dve_made[K + "g", h])
                    pe.wait_ge(*pool_made[K + "ce", h])
                    for t in range(NT):
                        s = slice(t * P, (t + 1) * P)
                        last = t == NT - 1
                        mm(pe, bank[r, s], lhsT=xd[:, t, h * DH:(h + 1) * DH], rhs=dg[:, h % 2, s], start=True,
                           stop=(t == 0))
                        if t:
                            mm(pe, bank[r, s], lhsT=st[:, t - 1, h * DH:(h + 1) * DH], rhs=ce[:, h % 2, s],
                               start=False, stop=True,
                               done=((K + "y", h // 2) if h % 2 else (K + "yh", h)) if last else None)

            def act_ssd(act):
                act.wait_ge(*filled[K + "last", 0])
                act.activation(cd.rearrange("p a b -> p (a b)"), banks[K + "last", 0][:, 0:16 * NT], ACT.Exp)\
                   .then_inc(*act_made.mark(K + "cd"))
                banks.drain((K + "last", 0), "act_made")
                for g in range(2):
                    act.wait_ge(*filled[K + "cb", g])
                    act.activation(cbt[:, g, :], banks[K + "cb", g][:, :], ACT.Copy)\
                       .then_inc(*act_made.mark((K + "cb", g)))
                    banks.drain((K + "cb", g), "act_made")
                    act.wait_ge(*filled[K + "bn", g])
                    act.activation(bn[:, :, g * P:(g + 1) * P],
                                   banks[K + "bn", g][:, :].rearrange("p (t w) -> p t w", t=NT), ACT.Copy)\
                       .then_inc(*act_made.mark((K + "bn", g)))
                    banks.drain((K + "bn", g), "act_made")
                for h in range(16):
                    act.wait_ge(*filled[K + "bc", h])
                    if h >= 2:
                        act.wait_ge(*pool_made[K + "ce", h - 2])
                    act.wait_ge(*dve_made[K + "seg", h])
                    act.activation(eb[:, h % 2, :], banks[K + "bc", h][:, :], ACT.Exp)\
                       .then_inc(*act_made.mark((K + "eb", h)))
                    banks.drain((K + "bc", h), "act_made")
                    act.activation(dg[:, h % 2, :], dg[:, h % 2, :], ACT.Exp).then_inc(*act_made.mark((K + "dg", h)))

            def heads_of(a, t, g, row):
                return natd[:, row, t, 8 * g:8 * g + 8].rearrange("p (h c) -> p h c", c=1).to_broadcast([P, 8, DH])

            def dve_ssd(dve):
                for w in after_att:
                    dve.wait_ge(*w)
                for t in range(NT):
                    dve.wait_ge(*dve_made[K + "acs", t])
                last = dts[0:16, 3, P - 1:SEQ:P].rearrange("p (a t) -> p a t", a=1).to_broadcast([16, 16, NT])
                dve.tensor_tensor(lastd[0:16, :, :], last,
                                  ident[0:16, 0:16].rearrange("p (h c) -> p h c", c=1).to_broadcast([16, 16, NT]),
                                  ALU.mult).then_inc(*dve_made.mark(K + "lastd"))
                dve.wait_ge(*filled[K + "nat", 0])
                b = banks[K + "nat", 0]
                dve.tensor_copy(natd.rearrange("p a t c -> p (a t c)"), b[:, 0:192]).then_inc(*dve_made.mark(K + "nat0"))
                banks.drain((K + "nat", 0), "dve_made")
                dve.wait_ge(*dve_made[K + "nat0"])
                n1 = natd[:, 1, :, :].rearrange("p t c -> p (t c)")
                dve.tensor_scalar(n1, n1, -1.0, None, ALU.mult).then_inc(*dve_made.mark(K + "nat"))
                for g in range(2):
                    dve.wait_ge(*act_made[K + "cb", g])
                    c3 = cbt[:, g, :].rearrange("p (t w) -> p t w", t=NT)
                    tri = cst("causalT").rearrange("p (t w) -> p t w", t=1).to_broadcast([P, NT, P])
                    dve.tensor_tensor(c3, c3, tri, ALU.mult).then_inc(*dve_made.mark((K + "cbm", g)))
                for t in range(NT):
                    for g in range(2):
                        dve.wait_ge(*filled[K + "xt", t, g])
                        d = xd[:, t, g * 512:(g + 1) * 512].rearrange("p (h c) -> p h c", h=8)
                        dve.tensor_tensor(d, banks[K + "xt", t, g][:, :].rearrange("p (h c) -> p h c", h=8),
                                          heads_of(None, t, g, 0), ALU.mult).then_inc(*dve_made.mark((K + "xd", t, g)))
                        banks.drain((K + "xt", t, g), "dve_made")
                for t in range(NT - 1):
                    for g in range(2):
                        d = xd[:, t, g * 512:(g + 1) * 512].rearrange("p (h c) -> p h c", h=8)
                        dve.wait_ge(*dve_made[K + "xd", t, g])
                        if t:
                            dve.wait_ge(*filled[K + "st", t - 1, g])
                        dve.tensor_tensor(xds[:, g, :].rearrange("p (h c) -> p h c", h=8), d, heads_of(None, t, g, 2),
                                          ALU.mult).then_inc(*dve_made.mark((K + "xds", t, g)))
                    for g in range(2):
                        dst = st[:, t, g * 512:(g + 1) * 512]
                        bank = banks[K + "st", t, g][:, :]
                        if t == 0:
                            dve.wait_ge(*filled[K + "st", t, g])
                            dve.tensor_copy(dst, bank).then_inc(*dve_made.mark((K + "st", t, g)))
                        else:
                            dve.wait_ge(*act_made[K + "cd"])
                            dve.wait_ge(*dve_made[K + "st", t - 1, g])
                            prev = st[:, t - 1, g * 512:(g + 1) * 512].rearrange("p (h c) -> p h c", h=8)
                            decay = cd[:, 8 * g:8 * g + 8, t:t + 1].to_broadcast([P, 8, DH])
                            dve.tensor_tensor(dst.rearrange("p (h c) -> p h c", h=8), prev, decay, ALU.mult)\
                               .then_inc(*dve_made.mark((K + "std", t, g)))
                            dve.wait_ge(*dve_made[K + "std", t, g])
                            dve.wait_ge(*filled[K + "st", t, g])
                            dve.tensor_tensor(dst, dst, bank, ALU.add).then_inc(*dve_made.mark((K + "st", t, g)))
                        banks.drain((K + "st", t, g), "dve_made")

                def seg(h):
                    dve.wait_ge(*filled[K + "bc", h])
                    if h >= 2:
                        dve.wait_ge(*filled[(K + "y", (h - 2) // 2) if h % 2 else (K + "yh", h - 2)])
                    for t in range(NT):
                        s = slice(t * P, (t + 1) * P)
                        i = dve.tensor_scalar(dg[:, h % 2, s], banks[K + "bc", h][:, s], natd[:, 1, t, h:h + 1], 0.0,
                                              ALU.add, ALU.min)
                    i.then_inc(*dve_made.mark((K + "seg", h)))

                seg(0)
                for h in range(16):
                    if h + 1 < 16:
                        seg(h + 1)
                    dve.wait_ge(*act_made[K + "dg", h])
                    dve.tensor_tensor(dg[:, h % 2, :], dg[:, h % 2, :], cbt[:, h // 8, :], ALU.mult)\
                       .then_inc(*dve_made.mark((K + "g", h)))
                    if h % 2:
                        c = h // 2
                        if c:
                            drain_y(dve, c - 1)
                drain_y(dve, KD - 1)

            def drain_y(dve, c):
                dve.wait_ge(*filled[K + "y", c])
                dve.scalar_tensor_tensor(out=xbc[:, c, :], in0=xbc[:, c, :], scalar=col("d_skip", l, c),
                                         in1=banks[K + "y", c][:, :], op0=ALU.mult, op1=ALU.add)\
                   .then_inc(*dve_made.mark((K + "y", c)))
                banks.drain((K + "y", c), "dve_made")

            def pool_ssd(pool):
                for h in range(16):
                    pool.wait_ge(*act_made[K + "eb", h])
                    if h >= 2:
                        pool.wait_ge(*filled[(K + "y", (h - 2) // 2) if h % 2 else (K + "yh", h - 2)])
                    pool.tensor_tensor(ce[:, h % 2, :], eb[:, h % 2, :], xbc[:, 10 + h // 8, :], ALU.mult)\
                       .then_inc(*pool_made.mark((K + "ce", h)))

            then(pe=pe_ssd, act=act_ssd, dve=dve_ssd, pool=pool_ssd)

            A = Area(gate_at)
            sg = A.take(2, 2, SEQ)
            at = A.at
            sil = A.take(3, SEQ)
            A.at = at
            mg = A.take_r(2, KD, SEQ)
            sq2 = Area().take(KD, SEQ)
            ys_hi = Area(xbc_at).take_r(KD, SEQ)
            ys_lo = Area().take_r(KD, SEQ)
            oa = Area(oT_at).take_r(4, SEQ), Area(xbc_at + KD * SEQ).take_r(4, SEQ)

            def pe_gate(pe):
                for n in range(4):
                    pe_linear(pe, K + "ga", n, hT, KD, None)
                for n in range(KD):
                    pe_linear(pe, K + "z", n, hT, KD, None)

            def act_gate(act):
                act.wait_ge(*filled[K + "y", KD - 1])
                for i in range(12):
                    key = (K + "ga", i) if i < 4 else (K + "z", i - 4)
                    act_bank(act, key)
                    if i >= 3:
                        act.wait_ge(*(dve_made[(K + "oa", i - 3), "lo"] if i < 7 else dve_made[K + "gated", i - 3]))
                    act.activation(sil[:, i % 3, :], banks[key][:, :], ACT.Silu)\
                       .then_inc(*act_made.mark((K + "sil", i)))
                    banks.drain(key, "act_made")
                    if i < 4:
                        act.wait_ge(*dve_made[K + "gated", i])
                        act_hi(act, oa[0][:, i, :], sil[:, i % 3, :], (K + "oa", i))
                    else:
                        act.wait_ge(*dve_made[K + "gated", i])
                        act.activation(sq2[:, i - 4, :], xbc[:, i - 4, :], ACT.Square)\
                           .then_inc(*act_made.mark((K + "gn", "sq", i - 4)))

            def dve_gate(dve):
                dve.wait_ge(*filled[K + "y", KD - 1])
                for i in range(12):
                    key = (K + "ga", i) if i < 4 else (K + "z", i - 4)
                    keep_up(dve, "dve", key)
                    dve.wait_ge(*act_made[K + "sil", i])
                    if i < 4:
                        dve.wait_ge(*turned_at(K + "ot")(i))
                        dve.tensor_tensor(sil[:, i % 3, :], oT[:, i, :], sil[:, i % 3, :], ALU.mult)\
                           .then_inc(*dve_made.mark((K + "gated", i)))
                        dve_lo(dve, oa[0][:, i, :], oa[1][:, i, :], sil[:, i % 3, :], (K + "oa", i))
                    else:
                        dve.wait_ge(*dve_made[K + "y", i - 4])
                        d = xbc[:, i - 4, :]
                        dve.tensor_tensor(d, d, sil[:, i % 3, :], ALU.mult).then_inc(*dve_made.mark((K + "gated", i)))

            then(pe=pe_gate, act=act_gate, dve=dve_gate)

            def act_gn(act):
                for g in range(2):
                    act_root(act, (K + "gn", g), rstd[:, g, :])
                    for k in range(4 * g, 4 * g + 4):
                        act.wait_ge(*dve_made[K + "gn", "scaled", k])
                        act_hi(act, ys_hi[:, k, :], hv[:, k % 4, :], (K + "ys in", k))

            def pe_gn(pe):
                for g in range(2):
                    bank = banks.take(pe, (K + "gn", "mean", g))
                    for j in range(4):
                        pe.wait_ge(*act_made[K + "gn", "sq", 4 * g + j])
                        mm(pe, bank[:, :], lhsT=cst("mean_g"), rhs=sq2[:, 4 * g + j, :], start=(j == 0), stop=(j == 3),
                           done=(K + "gn", "mean", g) if j == 3 else None)

            def dve_gn(dve):
                for g in range(2):
                    dve_inverse(dve, (K + "gn", g), rstd[:, g, :], banks[K + "gn", "mean", g][:, :],
                                (K + "gn", "mean", g))
                    banks.drain((K + "gn", "mean", g), "dve_made")
                dve.wait_ge(*filled[K + "gn", "mean", 1])
                for k in range(KD):
                    dve.wait_ge(*act_made[(K + "gn", k // 4), "rstd"])
                    if k >= 4:
                        dve.wait_ge(*dve_made[(K + "ys in", k - 4), "lo"])
                    dve.scalar_tensor_tensor(out=hv[:, k % 4, :], in0=xbc[:, k, :], scalar=col("ssm_g", l, k),
                                             in1=rstd[:, k // 4, :], op0=ALU.mult, op1=ALU.mult)\
                       .then_inc(*dve_made.mark((K + "gn", "scaled", k)))
                    dve_lo(dve, ys_hi[:, k, :], ys_lo[:, k, :], hv[:, k % 4, :], (K + "ys in", k))

            then(pe=pe_gn, act=act_gn, dve=dve_gn)

            def pe_merge(pe):
                for k in range(4):
                    pe.wait_ge(*dve_made[(K + "oa", k), "lo"])
                oa_in, ys_in = Pair(*oa), Pair(ys_hi, ys_lo)
                for n in range(0, KD, 2):
                    for m in (n, n + 1):
                        pe_linear(pe, K + "ya", m, oa_in, 4, None)
                    for m in (n, n + 1):
                        pe_linear(pe, K + "gla", m, hT, KD, None)
                        pe_linear(pe, K + "gls", m, hT, KD, None)
                        pe_linear(pe, K + "ys", m, ys_in, KD, lo_of(K + "ys in") if m == 0 else None)

            def act_merge(act):
                for n in range(0, KD, 2):
                    for m in (n, n + 1):
                        keep_up(act, "act", (K + "ya", m))
                    for m in (n, n + 1):
                        for j, key in enumerate(("gla", "gls")):
                            act_bank(act, (K + key, m))
                            if m >= 2:
                                act.wait_ge(*dve_made[(K + "mg", m - 2), "lo"])
                            act.activation(sg[:, m % 2, j, :], banks[K + key, m][:, :], ACT.Sigmoid)\
                               .then_inc(*act_made.mark((K + "sg", m, j)))
                            banks.drain((K + key, m), "act_made")
                        keep_up(act, "act", (K + "ys", m))
                        act.wait_ge(*pool_made[K + "mg", m])
                        act_hi(act, mg[:, 0, m, :], sg[:, m % 2, 0, :], (K + "mg", m))

            def dve_merge(dve):
                for n in range(0, KD, 2):
                    for m in (n, n + 1):
                        keep_up(dve, "dve", (K + "ya", m))
                    for m in (n, n + 1):
                        keep_up(dve, "dve", (K + "gls", m))
                        for j, key in enumerate(("ya", "ys")):
                            dve.wait_ge(*act_made[K + "sg", m, j])
                            dve_bank(dve, (K + key, m))
                            dve.tensor_tensor(sg[:, m % 2, j, :], sg[:, m % 2, j, :], banks[K + key, m][:, :],
                                              ALU.mult).then_inc(*dve_made.mark((K + "tg", m, j)))
                            banks.drain((K + key, m), "dve_made")
                        dve.wait_ge(*pool_made[K + "mg", m])
                        dve_lo(dve, mg[:, 0, m, :], mg[:, 1, m, :], sg[:, m % 2, 0, :], (K + "mg", m))

            def pool_merge(pool):
                for n in range(KD):
                    for j in range(2):
                        pool.wait_ge(*dve_made[K + "tg", n, j])
                    pool.tensor_tensor(sg[:, n % 2, 0, :], sg[:, n % 2, 0, :], sg[:, n % 2, 1, :], ALU.add)\
                        .then_inc(*pool_made.mark((K + "mg", n)))

            then(pe=pe_merge, act=act_merge, dve=dve_merge, pool=pool_merge)
            then(back_to_x(K + "out", mg, KD, lo_of(K + "mg"), nxt, lambda n: mod[:, 24 * l + 16 + n:24 * l + 17 + n]))

        block2(0, "L1h", filled[("f1", "b"), FC - 1], filled[("f1", "y"), KD - 1])
        block2(1, "fin", filled["L0gls", KD - 1], filled["L0out", KD - 1])
        then(norm("fin", ("final_g", 0), to_x=True))

        A = Area()
        y_nat = A.take(NT, D)

        def pe_back(pe):
            for k in range(KD):
                pe.wait_ge(*dve_made["fin", "scaled", k])
            for t in range(NT):
                for half in range(2):
                    bank = banks.take(pe, ("back", t, half))
                    for j in range(4):
                        tp(pe, bank[:, j * P:(j + 1) * P], xT[:, half * 4 + j, t * P:(t + 1) * P], ident,
                           done=("back", t, half) if j == 3 else None)

        def act_back(act):
            act.wait_ge(*filled["L1out", KD - 1])
            for t in range(NT):
                act.wait_ge(*filled["back", t, 0])
                act.activation(y_nat[:, t, 0:512], banks["back", t, 0][:, :], ACT.Copy)\
                   .then_inc(*act_made.mark(("back", t)))
                banks.drain(("back", t, 0), "act_made")
                act.wait_ge(*act_made["back", t])
                act.wait_ge(*dve_made["back", t])
                act.dma_start(out[t * P:(t + 1) * P, :], y_nat[:, t, :]).then_inc(out_stored, 16)
            act.wait_ge(out_stored, 16 * NT)

        def dve_back(dve):
            for t in range(NT):
                dve.wait_ge(*filled["back", t, 1])
                dve.tensor_copy(y_nat[:, t, 512:1024], banks["back", t, 1][:, :])\
                   .then_inc(*dve_made.mark(("back", t)))
                banks.drain(("back", t, 1), "dve_made")

        then(pe=pe_back, act=act_back, dve=dve_back)

        block = ctx.enter_context(nc.Block())
        n_panels = stream_of.shape[0]

        @block.sync
        def _(sp):
            for i in range(n_panels):
                if i >= RAW:
                    old = i - RAW
                    kind = kinds[old]
                    sp.wait_ge(*(dve_made["w_lo", old] if kind == "split" else filled["panel", old] if kind == "PE"
                                 else dve_made["ada panel", old]))
                sp.dma_start(ring[:, i % RAW, :, :].rearrange("p k w -> p (k w)"), stream_of[i])\
                  .then_inc(panel_landed[i % RAW], 16)

        @block.scalar
        def _(act):
            act.dma_start(x_nat, x_in.rearrange("(t p) d -> p t d", p=P)).then_inc(x_landed, 16)
            act.dma_start(vec[:, :], vec_in).then_inc(const_landed, 16)
            act.dma_start(cf[:, :], cf_in).then_inc(const_landed, 16)
            act.dma_start(cb[:, :], cb_in).then_inc(const_landed, 16)
            act.dma_start(rot[:, :, :].rearrange("p a b -> p (a b)"), rot_in[:, 0:2 * SEQ]).then_inc(rot_landed, 16)
            for part in prog["act"]:
                part(act)

        @block.tensor
        def _(pe):
            for part in prog["pe"]:
                part(pe)

        @block.vector
        def _(dve):
            for part in prog["dve"]:
                part(dve)

        @block.gpsimd
        def _(pool):
            for part in prog["pool"]:
                part(pool)

    assert tile_no[0] == n_tiles, (tile_no[0], n_tiles)
    return {"signals": {n: dict(s.at) for n, s in signals.items()}, "order": list(banks.order),
            "drained": dict(banks.drained), "panel_of": dict(banks.panel_of)}


def pack_stream(inputs):
    tiles = stream()
    assert len(tiles) % KD == 0
    a = np.zeros((len(tiles) // KD, P, KD, P), np.float32)
    for t, (name, layer, row, cols) in enumerate(tiles):
        w = inputs[name][layer]
        d = a[t // KD, :, t % KD, :]
        if isinstance(cols, str):
            d[0:DH, 0:DH] = w[row:row + DH]
            d[DH:P, DH:P] = w[row:row + DH]
        elif cols[-1] - cols[0] == len(cols) - 1:
            d[:, 0:len(cols)] = w[row:row + P, cols[0]:cols[-1] + 1]
        else:
            d[:, 0:len(cols)] = w[row:row + P][:, cols]
    return a.reshape(len(tiles) // KD, P, KD * P)


def pack_vec(inputs):
    a = np.zeros((P, NVEC), np.float32)

    def put(name, layer, v, chunks):
        a[:, VEC[name, layer]:VEC[name, layer] + chunks] = v.reshape(chunks, P).T

    for l in range(2):
        put("attn_norm", l, inputs["attn_norm"][l], KD)
        put("ffn_norm", l, inputs["ffn_norm"][l], KD)
        for j in range(3):
            put("conv_w", (l, j), inputs["ffn_conv_w"][l, j], FC)
        put("conv_b", l, inputs["ffn_conv_b"][l], FC)
        put("b_ada", l, inputs["b_ada_2"][l], 24)
        put("norm_g", l, inputs["norm_g_2"][l], KD)
        for j in range(4):
            put("xconv_w", (l, j), inputs["conv_w_2"][l, j], 12)
        put("xconv_b", l, inputs["conv_b_2"][l], 12)
        a[0:16, VEC["dt_bias", l]] = inputs["dt_bias_2"][l]
        a[0:16, VEC["a_log", l]] = inputs["a_log_2"][l]
        put("d_skip", l, np.repeat(inputs["d_skip_2"][l], DH), KD)
        put("ssm_g", l, inputs["ssm_norm_g_2"][l], KD)
    put("final_norm", 0, inputs["final_norm"], KD)
    put("final_g", 0, inputs["final_g_2"], KD)
    put("c", 0, inputs["c_2"][0], KD)
    for name, src in (("pos_k", "ev_cmp_pos_k"), ("pos_v", "ev_cmp_pos_v")):
        o = VEC[name, 0]
        a[0:DH, o:o + CMP_LEN] = inputs[src][0].T
        a[DH:P, o:o + CMP_LEN] = inputs[src][0].T
    a[0:16, VEC["b_f", 0]] = inputs["od_b_f"][0]
    return a


def kernel(**inputs):
    import ml_dtypes
    import concourse.bacc as bacc
    from concourse.bass_utils import run_bass_kernel_spmd as run

    inputs = {k: np.ascontiguousarray(v) for k, v in inputs.items()}
    cf, cb, rot = constants()
    arrays = {"weights": pack_stream(inputs), "x": inputs["x"][0], "vec": pack_vec(inputs), "cf": cf,
              "cb": cb.astype(ml_dtypes.bfloat16), "rot": rot}

    def program(known, final=False):
        nc = bacc.Bacc("TRN2", target_bir_lowering=False, num_devices=1)
        ins = [nc.dram_tensor(n + "_dram", a.shape, mybir.dt.from_np(a.dtype), kind="ExternalInput").ap()
               for n, a in arrays.items()]
        out = nc.dram_tensor("out_dram", (SEQ, D), F32, kind="ExternalOutput").ap()
        return nc, build(nc, ins, out, known, final)

    _, known = program(None)
    _, known = program(known)
    nc, _ = program(known, final=True)
    r = run(nc, [{n + "_dram": a for n, a in arrays.items()}], core_ids=[0])
    return np.asarray(r.results[0]["out_dram"]).reshape(1, SEQ, D)
```

```python
from contextlib import ExitStack

import numpy as np

import concourse.bass as bass
from concourse import mybir

F32 = mybir.dt.float32
F32R = mybir.dt.float32r
BF16 = mybir.dt.bfloat16
ALU = mybir.AluOpType
ACT = mybir.ActivationFunctionType
AX = mybir.AxisListType

P = 128
D = 1024
KD = D // P
SEQ = 512
NT = SEQ // P
DH = 64
SCALE = DH ** -0.5
NEG = -1e30
TAKEN = -3e38
EPS = 1e-6
D_FF = 2816
FC = D_FF // P
FH = FC // 2
NCMP = 31
CMP_LEN = 32
CMP_STRIDE = 16
TOPK = 128
RAW = 5
PARTS = 3
ARENA = 22850
NBANK = 7
EARLY = 5
MIDDLE = 3
DSA_EVERY = 4
ALL_BANKS = tuple(range(NBANK))
POOLS = (0, 1, 2), (3, 4, 5), (6, 7)
LAYERS = 2


def ada_steps(layer, n):
    first = 2 * n if n < 2 else n + 2
    return [(layer, j // KD, j % KD) for j in range(first, first + (2 if n < 2 else 1))]


def stream():
    tiles = []

    def full(name, layer, cols):
        for k in range(KD):
            tiles.append((name, layer, k * P, cols))

    def proj(name, layer, start, width):
        for i in range(0, width, P):
            full(name, layer, list(range(start + i, start + min(i + P, width))))

    def tall(name, layer, kt, first=0):
        for n in range(KD):
            for k in range(first, first + kt):
                tiles.append((name, layer, k * P, list(range(n * P, n * P + P))))

    def ffn(layer):
        for n in range(FC):
            proj("ffn_w_in", layer, n * P, P)
            proj("ffn_w_in", layer, D_FF + n * P, P)
            for l, b, k in ada_steps(layer, n):
                for i in range(KD):
                    tiles.append(("w_ada_2", l, k * P, list(range(b * D + i * P, b * D + i * P + P))))
            if n % FH == FH - 1:
                tall("ffn_w_out", layer, FH, n + 1 - FH)

    sq, sk, sv, nq, kc, vc, ksl, vsl, kwn, vwn, g = 0, 512, 1024, 1536, 2048, 2176, 2304, 2432, 2560, 2688, 2816
    proj("ev_w_in", 0, kc, P)
    proj("ev_w_in", 0, vc, P)
    chunks = [list(range(at, at + P)) for at in (ksl, kwn)]
    chunks += [[nq + (gr * 4 + c) * DH + i for gr in range(2) for i in range(DH)] for c in range(4)]
    chunks += [list(range(at, at + P)) for at in (vsl, vwn)]
    compress = [(name, 0, l * DH, "twice") for name in ("ev_cmp_w_k", "ev_cmp_w_v") for l in range(CMP_LEN)]
    for i, cols in enumerate(chunks):
        full("ev_w_in", 0, cols)
        tiles += compress[i * KD:(i + 1) * KD]
    proj("ev_w_in", 0, g, 24)
    proj("ev_w_in", 0, sk, 512)
    proj("ev_w_in", 0, sq, 512)
    proj("ev_w_in", 0, sv, 512)
    tall("ev_w_out", 0, KD)
    ffn(0)
    proj("od_w_in", 0, 3072, 16)
    for c in range(KD):
        for part in range(3):
            proj("od_w_in", 0, part * D + c * P, P)
    tall("od_w_out", 0, KD)
    ffn(1)
    for layer in range(LAYERS):
        w = "w_in_2"
        proj(w, layer, 1152, 256)
        full(w, layer, [1408 + i for _ in range(2) for i in range(DH)])
        proj(w, layer, 1472, 4)
        proj(w, layer, 0, 512)
        full(w, layer, [512 + i for _ in range(2) for i in range(DH)])
        proj(w, layer, 576, DH)
        proj(w, layer, 4036, 16)
        proj(w, layer, 2500, 1536)
        proj(w, layer, 640, 512)
        proj(w, layer, 1476, 1024)
        for n in range(KD):
            for k in range(4):
                tiles.append(("w_branch_a_2", layer, k * P, list(range(n * P, n * P + P))))
            if n % 2:
                for m in (n - 1, n):
                    proj(w, layer, 4052 + m * P, P)
                    proj(w, layer, 5076 + m * P, P)
                    for k in range(KD):
                        tiles.append(("w_branch_s_2", layer, k * P, list(range(m * P, m * P + P))))
        tall("w_out_2", layer, KD)
    return tiles


def vec_layout():
    at, n = {}, 0
    for name, layer, cols in (
        [("attn_norm", l, KD) for l in range(2)] + [("ffn_norm", l, KD) for l in range(2)]
        + [("conv_w", (l, j), FC) for l in range(2) for j in range(3)] + [("conv_b", l, FC) for l in range(2)]
        + [("final_norm", 0, KD), ("pos_k", 0, CMP_LEN), ("pos_v", 0, CMP_LEN), ("b_f", 0, 1), ("c", 0, KD)]
        + [("b_ada", l, 24) for l in range(2)] + [("norm_g", l, KD) for l in range(2)]
        + [("xconv_w", (l, j), 12) for l in range(2) for j in range(4)] + [("xconv_b", l, 12) for l in range(2)]
        + [("dt_bias", l, 1) for l in range(2)] + [("a_log", l, 1) for l in range(2)]
        + [("d_skip", l, KD) for l in range(2)] + [("ssm_g", l, KD) for l in range(2)] + [("final_g", 0, KD)]
    ):
        at[name, layer] = n
        n += cols
    return at, n


VEC, NVEC = vec_layout()

CF = {}
CB = {}
CR = {}


def _place(table, items):
    n = 0
    for name, w in items:
        table[name] = (n, w)
        n += w
    return n


NCF = _place(CF, [("ident", P), ("tri", P), ("nones", P), ("mean_d", 8), ("mean_g", 8), ("perm8", P), ("perm32", P),
                  ("cosc", 32), ("sinc", 32),
                  ("strict", P), ("cmp01", NT * 32), ("ones", P)])
NCR = _place(CR, [("cos8", SEQ), ("sin8", SEQ), ("cos32", SEQ), ("sin32", SEQ)])
NCB = _place(CB, [("ident", P), ("causal", P), ("strictT", P), ("cmp", NT * P), ("selneg", 16), ("sel", 16), ("later", P)])


def constants():
    f = np.zeros((P, NCF), np.float32)
    b = np.zeros((P, NCB), np.float32)
    rot = np.zeros((P, NCR), np.float32)

    def put(t, table, name, a):
        a = np.asarray(a, np.float32).reshape(a.shape[0], -1)
        o, w = table[name]
        assert a.shape[1] == w, name
        t[: a.shape[0], o:o + w] = a

    i = np.arange(P)
    put(f, CF, "ident", np.eye(P))
    put(f, CF, "tri", -(i[:, None] >= i[None, :]).astype(np.float32))
    put(f, CF, "nones", -np.ones((P, P)))
    put(f, CF, "mean_d", np.eye(1, 8, dtype=np.float32).repeat(P, 0) / D)
    put(f, CF, "mean_g", np.eye(1, 8, dtype=np.float32).repeat(P, 0) / 512)

    def rope(rot, theta, pos):
        half = rot // 2
        if rot == 16:
            inv = (np.float32(theta) ** (-(np.arange(half, dtype=np.float32) * np.float32(2.0) / np.float32(rot)))).astype(np.float32)
        else:
            inv = (np.float32(theta) ** (-np.arange(0, rot, 2, dtype=np.float32) / np.float32(rot))).astype(np.float32)
        ang = (pos.astype(np.float32)[:, None] * inv[None, :]).astype(np.float32)
        cos = np.ones((P, len(pos)), np.float32)
        sin = np.zeros((P, len(pos)), np.float32)
        perm = np.zeros((P, P), np.float32)
        for base in (0, DH):
            for j in range(DH):
                if j < half:
                    src, s = j + half, -1.0
                elif j < rot:
                    src, s = j - half, 1.0
                else:
                    perm[base + j, base + j] = 1.0
                    continue
                perm[base + src, base + j] = 1.0
                cos[base + j] = np.cos(ang[:, j % half])
                sin[base + j] = s * np.sin(ang[:, j % half])
        return cos, sin, perm

    pos = np.arange(SEQ)
    cmp_end = np.arange(32) * CMP_STRIDE + CMP_LEN - 1
    c, s, m = rope(16, 500000.0, pos)
    put(rot, CR, "cos8", c), put(rot, CR, "sin8", s), put(f, CF, "perm8", m)
    c, s, m = rope(16, 500000.0, cmp_end)
    put(f, CF, "cosc", c), put(f, CF, "sinc", s)
    c, s, m = rope(64, 10000.0, pos)
    put(rot, CR, "cos32", c), put(rot, CR, "sin32", s), put(f, CF, "perm32", m)
    put(f, CF, "strict", (i[:, None] < i[None, :]).astype(np.float32))
    seen = (cmp_end[None, None, :] <= (i[:, None, None] + P * np.arange(NT)[None, :, None])) & (np.arange(32) < NCMP)
    put(f, CF, "cmp01", seen.astype(np.float32))
    put(f, CF, "ones", np.ones((P, P)))
    put(b, CB, "ident", np.eye(P))
    put(b, CB, "causal", np.where(i[None, :] > i[:, None], NEG, 0.0))
    put(b, CB, "strictT", np.where(i[:, None] >= i[None, :], NEG, 0.0))
    put(b, CB, "cmp", np.repeat(np.where(seen, 0.0, NEG)[:, :, None, :], 4, axis=2))
    sn = np.zeros((96, 16), np.float32)
    for q in range(3):
        sn[32 * q + np.arange(16), np.arange(16)] = -1.0
    put(b, CB, "selneg", sn)
    put(b, CB, "sel", -sn)
    put(b, CB, "later", np.where(i[:, None] > i[None, :], -NEG, 0.0))
    return f, b, rot


STEPS_TYPE = type(i for i in ())


def finish(steps):
    if isinstance(steps, STEPS_TYPE):
        for _ in steps:
            pass


def spread(*counts):
    return [i for _, i in sorted(((step + 0.5) / n, i) for i, n in enumerate(counts) for step in range(n))]


def alternate(order, *parts):
    def program(functions):
        def run(eng):
            steps = [f(eng) if f else (i for i in ()) for f in functions]
            for i in order:
                next(steps[i], None)
            for rest in steps:
                finish(rest)
        return run
    return [program([p[i] if i < len(p) else None for p in parts]) for i in range(4)]


def one_after_the_other(*parts):
    def program(functions):
        def run(eng):
            for f in functions:
                if f:
                    yield from f(eng)
        return run
    return [program([p[i] if i < len(p) else None for p in parts]) for i in range(4)]


class Pair:

    def __init__(self, hi, lo):
        self.parts = hi, lo

    def __getitem__(self, at):
        p, part, k, f = at
        return self.parts[part][p, k, f]


class Signal:

    def __init__(self, sem, known, final=False):
        self.sem, self.known, self.count, self.at = sem, known or {}, 0, {}
        self.final = final

    def mark(self, key=None, n=1):
        self.count += n
        assert key is None or key not in self.at, key
        self.at[key] = self.count
        return self.sem, n

    def __getitem__(self, key):
        return self.sem, self.known.get(key, 1) if not self.final else self.known[key]


class Banks:

    def __init__(self, places, signals, known):
        self.places, self.signals, self.known = places, signals, known or {}
        self.at, self.drained, self.last, self.turn, self.panel_of = {}, {}, {}, {}, {}
        self.last_panel = self.known.get("panel_of")

    def take(self, pe, key, pool=ALL_BANKS):
        n = self.turn.get(pool, 0)
        self.turn[pool] = n + 1
        place = pool[n % len(pool)]
        if place in self.last:
            name, count = self.known["drained"][self.last[place]] if self.known else (next(iter(self.signals)), 1)
            pe.wait_ge(self.signals[name].sem, count)
        self.last[place] = key
        self.at[key] = place
        return self.places[place]

    def __getitem__(self, key):
        return self.places[self.known["at"][key] if self.known else 0]

    def drain(self, key, name):
        self.drained[key] = (name, self.signals[name].count)


SIGNALS = ["bank_filled", "act_made", "dve_made", "pool_made"]


def build(nc, ins, out, known=None, final=False):
    stream_of, x_in, vec_in, cf_in, cb_in, rot_in = ins
    tiles = stream()
    kinds = ["PE" if t[0].startswith("ev_cmp") else "DVE" if t[0] == "w_ada_2" else "split" for t in tiles[::KD]]
    place = np.cumsum([k == "split" for k in kinds]) - 1
    splits = [p for p, k in enumerate(kinds) if k == "split"]
    ada_panel = dict(zip([st for l in range(2) for n in range(FC) for st in ada_steps(l, n)],
                         [p for p, k in enumerate(kinds) if k == "DVE"]))
    n_tiles = stream_of.shape[0] * KD
    with ExitStack() as ctx:
        def sb(name, shape, dt=F32):
            return ctx.enter_context(nc.sbuf_tensor(name, shape, dt))

        ring = sb("ring", [P, RAW, KD, P])
        wparts = sb("wparts", [P, PARTS, 2, KD, P], F32R)
        xT = sb("xT", [P, KD, SEQ])
        hT = sb("hT", [P, 2, KD, SEQ], F32R)
        hv = sb("hv", [P, 4, SEQ])
        rot = sb("rot", [P, 2, SEQ])
        vec = sb("vecs", [P, NVEC])
        cf = sb("cf_sb", [P, NCF])
        cb = sb("cb_sb", [P, NCB], BF16)
        small = sb("small", [P, 256])
        rstd = sb("rstd", [P, 2, SEQ])
        arena = sb("arena", [P, ARENA])
        arena_at = nc.sbuf_base - 4 * ARENA
        arena_r = nc.alloc_sbuf_tensor_at("arena_r", [P, ARENA], F32R, offset=arena_at)
        psum = [ctx.enter_context(nc.psum_tensor(f"bank{i}", [P, SEQ], F32)) for i in range(NBANK)]
        mean_bank = ctx.enter_context(nc.psum_tensor("mean_bank", [P, SEQ], F32))

        signals = {name: Signal(ctx.enter_context(nc.semaphore(name)), known and known["signals"][name], final)
                   for name in SIGNALS}
        filled, act_made, dve_made, pool_made = (signals[n] for n in SIGNALS)
        places = dict(enumerate(psum))
        places[NBANK] = mean_bank
        banks = Banks(places, signals, known)
        panel_landed = [ctx.enter_context(nc.semaphore(f"panel_landed{i}")) for i in range(RAW)]
        rot_landed = ctx.enter_context(nc.semaphore("rot_landed"))
        x_landed = [ctx.enter_context(nc.semaphore(f"x_landed{t}")) for t in range(NT)]
        cf_landed = ctx.enter_context(nc.semaphore("cf_landed"))
        const_landed = ctx.enter_context(nc.semaphore("const_landed"))
        out_stored = ctx.enter_context(nc.semaphore("out_stored"))

        def cst(name):
            o, w = CF[name]
            return cf[:, o:o + w]

        def cstb(name):
            o, w = CB[name]
            return cb[:, o:o + w]

        def col(name, layer, k=0, parts=P):
            o = VEC[name, layer] + k
            return vec[0:parts, o:o + 1]

        class Area:

            def __init__(self, base=0):
                self.at = base

            def take(self, *shape):
                n = int(np.prod(shape))
                a = arena[:, self.at:min(self.at + n, ARENA)]
                self.at += n
                assert self.at <= ARENA, self.at
                if len(shape) == 2:
                    a = a.rearrange("p (a b) -> p a b", a=shape[0])
                elif len(shape) == 3:
                    a = a.rearrange("p (a b c) -> p a b c", a=shape[0], b=shape[1])
                return a

            def take_r(self, *shape):
                at = self.at
                self.take(int(np.prod(shape)))
                a = arena_r[:, at:self.at]
                if len(shape) == 2:
                    return a.rearrange("p (a b) -> p a b", a=shape[0])
                return a.rearrange("p (a b c) -> p a b c", a=shape[0], b=shape[1])

            def take16(self, n):
                a = arena[:, self.at:self.at + n // 2].bitcast(BF16)
                self.at += n // 2
                return a

        ident = cst("ident")
        identb = cstb("ident")

        tile_no = [0]

        def mm(pe, *args, done=None, ends=None, **kw):
            i = pe.matmul(*args, **kw)
            if done is not None:
                i.then_inc(*filled.mark(done))
                if ends is not None:
                    filled.at["panel", ends] = filled.count
            elif ends is not None:
                i.then_inc(*filled.mark(("panel", ends)))
            return i

        def tp(pe, *args, done=None):
            i = pe.transpose(*args)
            if done is not None:
                i.then_inc(*filled.mark(done))
            return i

        def landed(eng, panel):
            eng.wait_ge(panel_landed[panel % RAW], 16 * (panel // RAW + 1))

        def tile_of(pe):
            t = tile_no[0]
            tile_no[0] += 1
            panel, j = divmod(t, KD)
            ends = panel if j == KD - 1 else None
            if kinds[panel] == "split":
                if j == 0:
                    pe.wait_ge(*dve_made["w_lo", panel])
                slot = place[panel] % PARTS
                return (wparts[:, slot, 0, j, :], wparts[:, slot, 1, j, :]), ends
            if j == 0:
                landed(pe, panel)
            return ring[:, panel % RAW, j, :], ends

        def pe_linear(pe, key, n, rhs, rows, ready):
            finish(pe_linear_steps(pe, key, n, rhs, rows, ready))

        def pe_linear_steps(pe, key, n, rhs, rows, ready, pool=ALL_BANKS):
            bank = banks.take(pe, (key, n), pool)
            for k in range(rows):
                (hi, lo), ends = tile_of(pe)
                if ready:
                    pe.wait_ge(*ready(k))
                last = k == rows - 1
                mm(pe, bank[:, :], lhsT=hi, rhs=rhs[:, 0, k, :], start=(k == 0), stop=False)
                mm(pe, bank[:, :], lhsT=hi, rhs=rhs[:, 1, k, :], start=False, stop=False)
                mm(pe, bank[:, :], lhsT=lo, rhs=rhs[:, 0, k, :], start=False, stop=last,
                   done=(key, n) if last else None, ends=ends)
                if k in (2, 5):
                    yield
            banks.panel_of[key, n] = (tile_no[0] - 1) // KD

        def pe_turn(pe, key, n, src, width=P, pool=ALL_BANKS):
            pe.wait_ge(*act_made[key, "T", n])
            bank = banks.take(pe, (key, "nat", n), pool)
            for t in range(NT):
                tp(pe, bank[:, t * width:(t + 1) * width], src[0:width, t * P:(t + 1) * P], ident[0:width, 0:width],
                   done=(key, "nat", n) if t == NT - 1 else None)

        def turned_bank(key, n, width=P):
            return banks[key, "nat", n][:, 0:NT * width].rearrange("p (t w) -> p t w", t=NT)

        split_at = {"act": 0, "dve": 0}

        def keep_up(eng, who, key):
            if banks.last_panel is None:
                return
            end = banks.last_panel[key]
            upto = place[end] + PARTS - 1
            while split_at[who] <= min(upto, len(splits) - 1):
                i = split_at[who]
                p = splits[i]
                if any(k != "split" for k in kinds[end + 1:max(end, p - RAW) + 1]):
                    return
                split_at[who] += 1
                slot = i % PARTS
                if who == "act":
                    landed(eng, p)
                    if i >= PARTS:
                        eng.wait_ge(*filled["panel", splits[i - PARTS]])
                    eng.activation(wparts[:, slot, 0, :, :], ring[:, p % RAW, :, :], ACT.Copy)\
                       .then_inc(*act_made.mark(("w_hi", p)))
                else:
                    eng.wait_ge(*act_made["w_hi", p])
                    eng.tensor_tensor(wparts[:, slot, 1, :, :], ring[:, p % RAW, :, :],
                                      wparts[:, slot, 0, :, :].bitcast(F32), ALU.subtract)\
                       .then_inc(*dve_made.mark(("w_lo", p)))

        def act_bank(act, key):
            keep_up(act, "act", key)
            act.wait_ge(*filled[key])

        def dve_bank(dve, key):
            keep_up(dve, "dve", key)
            dve.wait_ge(*filled[key])

        def act_hi(act, dst, src, key):
            act.activation(dst, src, ACT.Copy).then_inc(*act_made.mark((key, "hi")))

        def dve_lo(dve, hi, lo, src, key):
            dve.wait_ge(*act_made[key, "hi"])
            dve.tensor_tensor(lo, src, hi.bitcast(F32), ALU.subtract).then_inc(*dve_made.mark((key, "lo")))

        roots = small[:, 232:240]

        def act_square(act, key, src, k, waits):
            for w in waits:
                act.wait_ge(*w)
            if k >= 4:
                act.wait_ge(*filled[key, "m", k - 4])
            act.activation(hv[:, k % 4, :], src[:, k, :], ACT.Square).then_inc(*act_made.mark((key, "sq", k)))

        def pe_squares(pe, src, weight, at, first):
            for t in range(NT):
                alone = first and t == 0
                i = mm(pe, mean_bank[:, 0:8] if alone else mean_bank[:, at + t:at + t + 1],
                       lhsT=src[:, t * P:(t + 1) * P], rhs=weight if alone else weight[:, 0:1], start=alone, stop=False,
                       skip_group_check=True)
            return i

        def pe_mean(pe, key, k):
            pe.wait_ge(*act_made[key, "sq", k])
            pe_squares(pe, hv[:, k % 4, :], cst("mean_d"), 0, k == 0).then_inc(*filled.mark((key, "m", k)))

        def dve_inverse(dve, key, r, last):
            dve.wait_ge(*filled[last])
            dve.tensor_scalar(r, mean_bank[:, 0:r.shape[-1]], EPS, None, ALU.add).then_inc(*dve_made.mark((key, "eps")))
            dve.wait_ge(*dve_made[key, "eps"])
            dve.reciprocal(r, r).then_inc(*dve_made.mark((key, "inv")))

        def act_root(act, key, r):
            act.wait_ge(*dve_made[key, "inv"])
            act.activation(r, r, ACT.Sqrt).then_inc(*act_made.mark((key, "rstd")))

        def dve_diagonal(dve, key, r, dst, g=0):
            dve.wait_ge(*act_made[key, "rstd"])
            dve.tensor_tensor(dst.rearrange("p (t c) -> p t c", t=NT),
                              ident.rearrange("p (t c) -> p t c", t=1).to_broadcast([P, NT, P]),
                              r.rearrange("p (t c) -> p t c", c=1).to_broadcast([P, NT, P]), ALU.mult)\
               .then_inc(*dve_made.mark((key, "diagonal", g)))

        def pe_all_partitions(pe, key, diagonal, g=0):
            pe.wait_ge(*dve_made[key, "diagonal", g])
            bank = banks.take(pe, (key, "rep", g))
            mm(pe, bank[:, :], lhsT=cst("ones"), rhs=diagonal, start=True, stop=True, done=(key, "rep", g))

        def norm(key, gain, free=None, mod=None, to_x=False):
            def act_part(act):
                act_root(act, key, roots[:, 0:NT])
                if to_x:
                    return
                if free is not None:
                    act.wait_ge(*free)
                for k in range(KD):
                    act.wait_ge(*dve_made[key, "scaled", k])
                    if mod is not None:
                        act.activation(hT[:, 0, k, :], hv[:, k % 4, :], ACT.Identity, bias=mod[1](k))\
                           .then_inc(*act_made.mark(((key, k), "hi")))
                    else:
                        act_hi(act, hT[:, 0, k, :], hv[:, k % 4, :], (key, k))

            def pe_part(pe):
                pe_all_partitions(pe, key, rstd[:, 0, :])

            def dve_part(dve):
                dve_inverse(dve, key, roots[:, 0:NT], (key, "m", KD - 1))
                dve_diagonal(dve, key, roots[:, 0:NT], rstd[:, 0, :])
                dve.wait_ge(*filled[key, "rep", 0])
                if free is not None:
                    dve.wait_ge(*free)
                for k in range(KD + 1):
                    if k < KD:
                        g = col(*gain, k) if mod is None else mod[0](k)
                        if k >= 4 and not to_x:
                            dve.wait_ge(*dve_made[(key, k - 4), "lo"])
                        dst = xT[:, k, :] if to_x else hv[:, k % 4, :]
                        dve.scalar_tensor_tensor(out=dst, in0=xT[:, k, :], scalar=g,
                                                 in1=banks[key, "rep", 0][:, :], op0=ALU.mult, op1=ALU.mult)\
                           .then_inc(*dve_made.mark((key, "scaled", k)))
                        if k == KD - 1:
                            banks.drain((key, "rep", 0), "dve_made")
                    if k and not to_x:
                        j = k - 1
                        hi, lo = hT[:, 0, j, :], hT[:, 1, j, :]
                        if mod is None:
                            dve_lo(dve, hi, lo, hv[:, j % 4, :], (key, j))
                        else:
                            dve.wait_ge(*act_made[(key, j), "hi"])
                            dve.scalar_tensor_tensor(out=lo, in0=hv[:, j % 4, :], scalar=mod[1](j),
                                                     in1=hi.bitcast(F32), op0=ALU.add, op1=ALU.subtract)\
                               .then_inc(*dve_made.mark(((key, j), "lo")))
            return act_part, pe_part, dve_part

        def h_at(key):
            return lambda k: dve_made[(key, k), "lo"]

        def softmax_maps(key, maps, Pb, PT, mx, sm, ready, two=ALL_BANKS, out=ALL_BANKS, dve_every=2):
            M = len(maps)
            on_act = [i % dve_every != 1 for i in range(M)]

            def pe_part(pe):
                for w in ready:
                    pe.wait_ge(*w)
                for i in range(M + 3):
                    if i < M:
                        m = maps[i]
                        for w in m.get("before", ()):
                            pe.wait_ge(*w)
                        bank = banks.take(pe, (key, "s", i), two)
                        W = m["width"]
                        extra = m["masks"]
                        mm(pe, bank[:, 0:W], lhsT=m["q"], rhs=m["k"], start=True, stop=not extra,
                           done=None if extra else (key, "s", i))
                        for j, (a, b, c, w) in enumerate(extra):
                            for wt in w:
                                pe.wait_ge(*wt)
                            mm(pe, bank[:, c:c + b.shape[-1]], lhsT=a, rhs=b, start=False, stop=j == len(extra) - 1,
                               done=(key, "s", i) if j == len(extra) - 1 else None)
                    if 2 <= i < M + 2:
                        j = i - 2
                        m = maps[j]
                        n = m["width"] // P
                        pe.wait_ge(*act_made[key, "p", j])
                        bank = banks.take(pe, (key, "t", j), two)
                        for t in range(n):
                            tp(pe, bank[:, t * P:(t + 1) * P], Pb[:, j % 3, t * P:(t + 1) * P], ident,
                               done=(key, "t", j) if t == n - 1 else None)
                    if i >= 3:
                        j = i - 3
                        m = maps[j]
                        n = m["width"] // P
                        pe.wait_ge(*(act_made if on_act[j] else dve_made)[key, "pt", j])
                        if "value" in m:
                            pe.wait_ge(*m["value"])
                        bank = banks.take(pe, (key, "o", j), out)
                        for t in range(n):
                            mm(pe, bank[:, 0:DH], lhsT=PT[:, j % 3, t * P:(t + 1) * P], rhs=m["v"](t), start=(t == 0),
                               stop=(t == n - 1), done=(key, "o", j) if t == n - 1 else None)
                    yield

            def act_part(act):
                for i in range(M + 3):
                    if 2 <= i < M + 2 and on_act[i - 2]:
                        j = i - 2
                        W = maps[j]["width"]
                        act.wait_ge(*filled[key, "t", j])
                        if j >= 3:
                            act.wait_ge(*filled[key, "o", j - 3])
                        act.activation(PT[:, j % 3, 0:W], banks[key, "t", j][:, 0:W], ACT.Copy)\
                           .then_inc(*act_made.mark((key, "pt", j)))
                        banks.drain((key, "t", j), "act_made")
                    if i < M:
                        W = maps[i]["width"]
                        act.wait_ge(*dve_made[key, "max", i])
                        if i >= 3:
                            act.wait_ge(*filled[key, "t", i - 3])
                        act.activation(Pb[:, i % 3, 0:W], banks[key, "s", i][:, 0:W], ACT.Exp, bias=mx(i),
                                       accum_out=sm(i)).then_inc(*act_made.mark((key, "p", i)))
                        banks.drain((key, "s", i), "act_made")
                    yield

            def dve_part(dve):
                for i in range(M + 3):
                    if i < M:
                        W = maps[i]["width"]
                        dve.wait_ge(*filled[key, "s", i])
                        if i >= 3:
                            dve.wait_ge(*act_made[key, "p", i - 3])
                        dve.tensor_reduce(mx(i), banks[key, "s", i][:, 0:W], AX.X, ALU.max, negate=True)\
                           .then_inc(*dve_made.mark((key, "max", i)))
                    if 1 <= i < M + 1:
                        j = i - 1
                        dve.wait_ge(*act_made[key, "p", j])
                        dve.reciprocal(sm(j), sm(j)).then_inc(*dve_made.mark((key, "inv", j)))
                        if maps[j]["gate"] is not None:
                            dve.wait_ge(*dve_made[key, "inv", j])
                            dve.tensor_tensor(sm(j), sm(j), maps[j]["gate"], ALU.mult)\
                               .then_inc(*dve_made.mark((key, "gated", j)))
                    if 2 <= i < M + 2 and not on_act[i - 2]:
                        j = i - 2
                        W = maps[j]["width"]
                        dve.wait_ge(*filled[key, "t", j])
                        if j >= 3:
                            dve.wait_ge(*filled[key, "o", j - 3])
                        dve.tensor_copy(PT[:, j % 3, 0:W], banks[key, "t", j][:, 0:W])\
                           .then_inc(*dve_made.mark((key, "pt", j)))
                        banks.drain((key, "t", j), "dve_made")
                    if i >= 3:
                        j = i - 3
                        m = maps[j]
                        dve.wait_ge(*filled[key, "o", j])
                        dve.wait_ge(*dve_made[key, "gated" if m["gate"] is not None else "inv", j])
                        o = banks[key, "o", j][:, 0:DH]
                        if m["add"] is not None:
                            dve.wait_ge(*m["add"])
                            dve.scalar_tensor_tensor(out=m["out"], in0=o, scalar=sm(j), in1=m["out"], op0=ALU.mult,
                                                     op1=ALU.add).then_inc(*dve_made.mark((key, "out", j)))
                        else:
                            dve.tensor_scalar(m["out"], o, sm(j), None, ALU.mult)\
                               .then_inc(*dve_made.mark((key, "out", j)))
                        banks.drain((key, "o", j), "dve_made")
                    yield
            return act_part, pe_part, dve_part

        def turned(key, src, dst, n, waits, free=()):
            def pe_part(pe):
                for w in waits:
                    pe.wait_ge(*w)
                for k in range(n):
                    bank = banks.take(pe, (key, k))
                    for t in range(NT):
                        tp(pe, bank[:, t * P:(t + 1) * P], src[:, t, k * P:(k + 1) * P], ident,
                           done=(key, k) if t == NT - 1 else None)

            def act_part(act):
                for w in free:
                    act.wait_ge(*w)
                for k in range(0, n, 2):
                    act.wait_ge(*filled[key, k])
                    act.activation(dst[:, k, :], banks[key, k][:, :], ACT.Copy).then_inc(*act_made.mark((key, k)))
                    banks.drain((key, k), "act_made")

            def dve_part(dve):
                for w in free:
                    dve.wait_ge(*w)
                for k in range(1, n, 2):
                    dve.wait_ge(*filled[key, k])
                    dve.tensor_copy(dst[:, k, :], banks[key, k][:, :]).then_inc(*dve_made.mark((key, k)))
                    banks.drain((key, k), "dve_made")
            return act_part, pe_part, dve_part

        def turned_at(key):
            return lambda k: (act_made if k % 2 == 0 else dve_made)[key, k]

        def turned_parts(key, src, dst, waits):
            def pe_part(pe):
                for w in waits:
                    pe.wait_ge(*w)
                for k in range(KD):
                    bank = banks.take(pe, (key, k))
                    for t in range(NT):
                        tp(pe, bank[:, t * P:(t + 1) * P], src[:, t, k * P:(k + 1) * P], ident,
                           done=(key, k) if t == NT - 1 else None)

            def act_part(act):
                for k in range(KD):
                    act.wait_ge(*filled[key, k])
                    act_hi(act, dst[:, 0, k, :], banks[key, k][:, :], (key, k))

            def dve_part(dve):
                for k in range(KD):
                    dve_lo(dve, dst[:, 0, k, :], dst[:, 1, k, :], banks[key, k][:, :], (key, k))
                    banks.drain((key, k), "dve_made")
            return act_part, pe_part, dve_part

        def lo_of(key):
            return lambda k: dve_made[(key, k), "lo"]

        def project(items, ready, rtmp, vt, table=None, vt_free=None, pool=ALL_BANKS):
            turns = [i for i, it in enumerate(items) if it["kind"] == "turn"]
            slot = {i: j % 2 for j, i in enumerate(turns)}
            ropes = [i for i, it in enumerate(items) if it["kind"] == "rope"]

            def pe_after(pe, i):
                it = items[i]
                if it["kind"] == "rope":
                    rope_parts(it["key"], it["n"], it["dst"], table, pool=pool)[0](pe)
                elif it["kind"] == "turn":
                    pe_turn(pe, it["key"], it["n"], vt[:, slot[i], :], it.get("width", P), pool)

            def pe_part(pe):
                for i, it in enumerate(items):
                    linear = pe_linear_steps(pe, it["key"], it["n"], hT, KD, ready if i == 0 else None, pool)
                    for step in range(3):
                        next(linear, None)
                        if i and step == 0:
                            pe_after(pe, i - 1)
                        yield
                pe_after(pe, len(items) - 1)
                yield

            def act_after(act, i):
                it = items[i]
                if it["kind"] == "turn" and "func" in it:
                    w = it.get("width", P)
                    act.wait_ge(*filled[it["key"], "nat", it["n"]])
                    act.activation(it["dst"], turned_bank(it["key"], it["n"], w), it["func"])\
                       .then_inc(*act_made.mark((it["key"], "turned", it["n"])))
                    banks.drain((it["key"], "nat", it["n"]), "act_made")

            def act_part(act):
                for i, it in enumerate(items):
                    key, n, kind = it["key"], it["n"], it["kind"]
                    keep_up(act, "act", (key, n))
                    yield
                    if i:
                        act_after(act, i - 1)
                    yield
                    if kind != "own":
                        act.wait_ge(*filled[key, n])
                        mark = {"copy": (key, n), "rope": (key, "raw", n), "turn": (key, "T", n)}[kind]
                        w = it.get("width", P)
                        if kind == "turn":
                            j = turns.index(i)
                            if j >= 2:
                                prev = items[turns[j - 2]]
                                act.wait_ge(*filled[prev["key"], "nat", prev["n"]])
                            elif vt_free is not None:
                                act.wait_ge(*vt_free)
                            dst, src = vt[0:w, slot[i], :], banks[key, n][0:w, :]
                        else:
                            dst, src = it["dst"], banks[key, n][:, :]
                        act.activation(dst, src, ACT.Copy, scale=it.get("scale", 1.0)).then_inc(*act_made.mark(mark))
                        banks.drain((key, n), "act_made")
                    yield
                act_after(act, len(items) - 1)
                yield

            def dve_after(dve, i):
                it = items[i]
                key, n = it["key"], it["n"]
                if it["kind"] == "rope":
                    rope_parts(key, n, it["dst"], table)[1](dve, rtmp[:, ropes.index(i) % 2, :])
                elif it["kind"] == "turn" and "func" not in it:
                    dve.wait_ge(*filled[key, "nat", n])
                    dve.tensor_copy(it["dst"], turned_bank(key, n, it.get("width", P)))\
                       .then_inc(*dve_made.mark((key, "turned", n)))
                    banks.drain((key, "nat", n), "dve_made")
                elif it["kind"] == "own":
                    it["do"](dve)

            def dve_part(dve):
                for i, it in enumerate(items):
                    keep_up(dve, "dve", (it["key"], it["n"]))
                    yield
                    if i:
                        dve_after(dve, i - 1)
                    yield
                    yield
                dve_after(dve, len(items) - 1)
                yield
            return act_part, pe_part, dve_part

        def item(key, n, kind, dst=None, **kw):
            return dict(key=key, n=n, kind=kind, dst=dst, **kw)

        def back_to_x(key, src, rows, ready, nxt, gate=None):
            def pe_part(pe):
                for n in range(KD):
                    pe_linear(pe, key, n, src, rows, ready if n == 0 else None)
                    if n >= 2 and nxt:
                        pe_mean(pe, nxt, n - 2)
                for k in (KD - 2, KD - 1) if nxt else ():
                    pe_mean(pe, nxt, k)

            def act_part(act):
                for n in range(KD):
                    keep_up(act, "act", (key, n))
                    if nxt:
                        act_square(act, nxt, xT, n, [dve_made[key, "x", n]])

            return act_part, pe_part, lambda dve: dve_residual(dve, key, gate)

        def dve_residual(dve, key, gate=None):
            for n in range(KD):
                dve_bank(dve, (key, n))
                bank = banks[key, n][:, :]
                if gate is None:
                    i = dve.tensor_tensor(xT[:, n, :], xT[:, n, :], bank, ALU.add)
                else:
                    i = dve.scalar_tensor_tensor(out=xT[:, n, :], in0=bank, scalar=gate(n), in1=xT[:, n, :],
                                                 op0=ALU.mult, op1=ALU.add)
                i.then_inc(*dve_made.mark((key, "x", n)))
                banks.drain((key, n), "dve_made")

        def x_after(key):
            return lambda k: [dve_made[key, "x", k]]

        def act_conv_start(act, key, n, cv, w, b, free):
            act_bank(act, (key, n))
            for f in free:
                act.wait_ge(*f)
            act.activation(cv, banks[key, n][:, :], ACT.Identity, bias=b, scale=w)\
               .then_inc(*act_made.mark((key, "tap", n)))

        def dve_conv_taps(dve, key, n, cv, ws):
            keep_up(dve, "dve", (key, n))
            dve.wait_ge(*act_made[key, "tap", n])
            for j, w in enumerate(ws):
                s = j + 1
                if j:
                    dve.wait_ge(*dve_made[key, "taps", n, j - 1])
                dve.scalar_tensor_tensor(out=cv[:, s:SEQ], in0=banks[key, n][:, 0:SEQ - s], scalar=w,
                                         in1=cv[:, s:SEQ], op0=ALU.mult, op1=ALU.add)\
                   .then_inc(*dve_made.mark((key, "taps", n, j)))
            banks.drain((key, n), "dve_made")

        def rope_parts(key, n, dst, table, width=SEQ, pool=ALL_BANKS):
            perm, cos, sin = table
            cos, sin = cos[:, 0:width], sin[:, 0:width]

            def pe_part(pe):
                pe.wait_ge(*act_made[key, "raw", n])
                bank = banks.take(pe, (key, "rot", n), pool)
                mm(pe, bank[:, 0:width], lhsT=cst(perm), rhs=dst, start=True, stop=True, done=(key, "rot", n))

            def dve_part(dve, tmp):
                dve.wait_ge(*filled[key, "rot", n])
                dve.tensor_tensor(tmp, banks[key, "rot", n][:, 0:width], sin, ALU.mult)\
                   .then_inc(*dve_made.mark((key, "sin", n)))
                banks.drain((key, "rot", n), "dve_made")
                dve.tensor_tensor(dst, dst, cos, ALU.mult).then_inc(*dve_made.mark((key, "cos", n)))
                dve.wait_ge(*dve_made[key, "cos", n])
                dve.tensor_tensor(dst, dst, tmp, ALU.add).then_inc(*dve_made.mark((key, "roped", n)))
            return pe_part, dve_part

        prog = {"act": [], "pe": [], "dve": [], "pool": []}

        def then(parts=None, **kw):
            if parts is not None:
                for e, f in zip(("act", "pe", "dve", "pool"), parts):
                    prog[e].append(f)
            for e, f in kw.items():
                prog[e].append(f)

        A = Area()
        x_nat = A.take(NT, D)

        def pe_x(pe):
            pe.wait_ge(cf_landed, 16)
            for t in range(NT):
                pe.wait_ge(x_landed[t], 16)
                for k in range(NBANK):
                    bank = banks.take(pe, ("x", k), (k,)) if t == 0 else banks["x", k]
                    tp(pe, bank[:, t * P:(t + 1) * P], x_nat[:, t, k * P:(k + 1) * P], ident,
                       done=("x", k) if t == NT - 1 else None)
            for k in range(NBANK, KD):
                bank = banks.take(pe, ("x", k))
                for t in range(NT):
                    tp(pe, bank[:, t * P:(t + 1) * P], x_nat[:, t, k * P:(k + 1) * P], ident,
                       done=("x", k) if t == NT - 1 else None)

        def all_consts(eng):
            eng.wait_ge(cf_landed, 16)
            eng.wait_ge(const_landed, 32)

        drains = turned("x", x_nat, xT, KD, [])
        then(act=drains[0], pe=pe_x, dve=drains[2])
        then(pe=all_consts, act=all_consts, dve=all_consts, pool=all_consts)
        prog["pe"].append(lambda pe: [pe_mean(pe, "h0", k) for k in range(KD)])
        prog["act"].append(lambda act: [act_square(act, "h0", xT, k, [turned_at("x")(k)]) for k in range(KD)])
        prog["act"].append(lambda act: keep_up(act, "act", ("kvc", 0)))
        prog["dve"].append(lambda dve: keep_up(dve, "dve", ("kvc", 0)))

        then(norm("h0", ("attn_norm", 0)))
        A = Area()
        sq, sk = A.take(4, SEQ), A.take(4, SEQ)
        sv = A.take(NT, 512)
        nq = A.take(4, SEQ)
        onat = A.take(NT, D)
        ksw = A.take(2, SEQ)
        vsw = A.take(2, NT, P)
        gates = A.take(NT, 24)
        kcr = A.take(32)
        vcn = A.take(P)
        B = Area(A.at)
        kvc = B.take(2, SEQ)
        kin = B.take(2, CMP_LEN, NCMP)
        rtmp = B.take(2, SEQ)
        cpx, cpt = B.take(256), B.take(2, SEQ)
        vt = B.take(2, SEQ)
        Pb, PT = A.take(3, SEQ), A.take(3, SEQ)

        def lower(area):
            return [area.take((NT - kt) * P) for kt in range(NT)]

        za, sp, aa = lower(A), lower(A), lower(A)
        ROPE8 = ("perm8", rot[:, 0, :], rot[:, 1, :])
        items = [item("kvc", n, "copy", kvc[:, n, :]) for n in range(2)]
        items_kv, items = items, []
        items += [item("ksw", n, "rope", ksw[:, n, :]) for n in range(2)]
        items += [item("nq", n, "rope", nq[:, n, :], scale=SCALE) for n in range(4)]
        items += [item("vsw", n, "turn", vsw[:, n, :, :]) for n in range(2)]
        items += [item("gates", 0, "turn", gates, width=24, func=ACT.Sigmoid)]
        items_nsa, items = items, []
        items += [item("sk", n, "copy", sk[:, n, :]) for n in range(4)]
        items += [item("sq", n, "copy", sq[:, n, :], scale=SCALE) for n in range(4)]
        items += [item("sv", n, "turn", sv[:, :, n * P:(n + 1) * P]) for n in range(4)]

        def dve_rot(dve):
            dve.wait_ge(rot_landed, 16)

        then(dve=dve_rot)
        then(project(items_kv, h_at("h0"), rtmp, vt, ROPE8))

        def dve_kin(dve):
            for n, name in enumerate(("pos_k", "pos_v")):
                dve.wait_ge(*act_made["kvc", n])
                o = VEC[name, 0]
                pos = vec[:, o:o + CMP_LEN].rearrange("p (l c) -> p l c", c=1).to_broadcast([P, CMP_LEN, NCMP])
                for half in range(2):
                    ls = slice(half * CMP_STRIDE, (half + 1) * CMP_STRIDE)
                    first = half * CMP_STRIDE
                    src = kvc[:, n, first:first + NCMP * CMP_STRIDE].rearrange("p (c l) -> p l c", l=CMP_STRIDE)
                    dve.tensor_tensor(kin[:, n, ls, :], src, pos[:, ls, :], ALU.add)\
                       .then_inc(*dve_made.mark(("kin", n, half)))

        then(dve=dve_kin)

        rope_c = rope_parts("kcr", 0, kcr[:, 0:NCMP], ("perm8", cst("cosc"), cst("sinc")), NCMP)

        def pe_compress(pe):
            for step in range(2 * CMP_LEN // KD):
                n, first = divmod(step * KD, CMP_LEN)
                if first == 0:
                    for half in range(2):
                        pe.wait_ge(*dve_made["kin", n, half])
                    bank = banks.take(pe, ("cmp", n), (NBANK,))
                for l in range(first, first + KD):
                    w, ends = tile_of(pe)
                    a, b = (w, kin[:, n, l, :]) if n == 0 else (kin[:, n, l, :], w)
                    mm(pe, bank[:, 0:NCMP] if n == 0 else bank[0:NCMP, 0:P], lhsT=a, rhs=b, start=(l == 0),
                       stop=(l == CMP_LEN - 1), done=("cmp", n) if l == CMP_LEN - 1 else None, ends=ends)
                if step == 4:
                    rope_c[0](pe)
                yield

        def act_compress(act):
            for step in range(2 * CMP_LEN // KD):
                if step == 3:
                    act.wait_ge(*filled["cmp", 0])
                    act.activation(kcr[:, 0:NCMP], banks["cmp", 0][:, 0:NCMP], ACT.Copy)\
                       .then_inc(*act_made.mark(("kcr", "raw", 0)))
                    banks.drain(("cmp", 0), "act_made")
                if step == 7:
                    act.wait_ge(*filled["cmp", 1])
                    act.activation(vcn[0:NCMP, :], banks["cmp", 1][0:NCMP, 0:P], ACT.Copy)\
                       .then_inc(*act_made.mark("vcn"))
                    banks.drain(("cmp", 1), "act_made")
                yield

        def dve_compress(dve):
            for step in range(2 * CMP_LEN // KD):
                if step == 4:
                    rope_c[1](dve, cpx[:, 0:NCMP])
                yield

        then(alternate([0, 0, 0, 1] * (2 * CMP_LEN // KD), project(items_nsa, None, rtmp, vt, ROPE8),
                       (act_compress, pe_compress, dve_compress)))

        nmax, den, dzero = small[:, 0:8], small[:, 8:16], small[:, 16:24]

        CMP_POOL = (3, 4, 5, 6)

        def by_head(a, w=32):
            return a.rearrange("p (h c) -> p h c", h=8)

        def pe_cmp(pe):
            pe.wait_ge(*dve_made["kcr", "roped", 0])
            pe.wait_ge(*dve_made["nq", "roped", 3])
            pe.wait_ge(*act_made["vcn"])
            for qt in range(NT):
                for g in range(2):
                    r = slice(DH * g, DH * g + DH)
                    bank = banks.take(pe, ("cs", qt, g), CMP_POOL)
                    mm(pe, bank[:, 0:P], lhsT=identb, rhs=cstb("cmp")[:, qt * P:(qt + 1) * P], start=True, stop=False)
                    for c in range(4):
                        mm(pe, bank[:, 32 * c:32 * c + NCMP], lhsT=nq[r, c, qt * P:(qt + 1) * P], rhs=kcr[r, 0:NCMP],
                           start=False, stop=(c == 3), done=("cs", qt, g) if c == 3 else None)
                yield
                pe.wait_ge(*dve_made["c01", qt])
                for half in range(2):
                    bank = banks.take(pe, ("ct", qt, half), CMP_POOL)
                    for j in range(4):
                        h = 4 * half + j
                        tp(pe, bank[0:32, j * P:(j + 1) * P], cpx[:, 32 * h:32 * h + 32], ident,
                           done=("ct", qt, half) if j == 3 else None)
                yield
                bank = banks.take(pe, ("co", qt), CMP_POOL)
                for h in range(8):
                    if h % 4 == 0:
                        pe.wait_ge(*act_made["cpt", qt, h // 4])
                    g = h // 4
                    mm(pe, bank[:, h * DH:(h + 1) * DH], lhsT=cpt[0:NCMP, h // 4, (h % 4) * P:(h % 4 + 1) * P],
                       rhs=vcn[0:NCMP, g * DH:(g + 1) * DH], start=True, stop=True,
                       done=("co", qt) if h == 7 else None)
                yield

        def act_cmp(act):
            for qt in range(NT):
                act.wait_ge(*dve_made["csub", qt, 1])
                act.activation(cpx, cpx, ACT.Exp).then_inc(*act_made.mark(("cexp", qt)))
                yield
                for half in range(2):
                    act.wait_ge(*filled["ct", qt, half])
                    if qt:
                        act.wait_ge(*filled["co", qt - 1])
                    act.activation(cpt[0:32, half, :], banks["ct", qt, half][0:32, :], ACT.Copy)\
                       .then_inc(*act_made.mark(("cpt", qt, half)))
                    banks.drain(("ct", qt, half), "act_made")
                yield
                yield

        def dve_cmp(dve):
            for qt in range(NT):
                if qt:
                    dve.wait_ge(*filled["ct", qt - 1, 1])
                for g in range(2):
                    dve.wait_ge(*filled["cs", qt, g])
                    bank = banks["cs", qt, g][:, 0:P].rearrange("p (h c) -> p h c", h=4)
                    mine = nmax[:, 4 * g:4 * g + 4]
                    dve.tensor_reduce(mine, bank, AX.X, ALU.max, negate=True)\
                       .then_inc(*dve_made.mark(("cmax", qt, g)))
                    dve.wait_ge(*dve_made["cmax", qt, g])
                    dve.tensor_tensor(cpx[:, P * g:P * g + P].rearrange("p (h c) -> p h c", h=4), bank,
                                      mine.rearrange("p (h c) -> p h c", c=1).to_broadcast([P, 4, 32]), ALU.add)\
                       .then_inc(*dve_made.mark(("csub", qt, g)))
                    banks.drain(("cs", qt, g), "dve_made")
                yield
                dve.wait_ge(*act_made["cexp", qt])
                o = CF["cmp01"][0] + 32 * qt
                seen = cf[:, o:o + 32].rearrange("p (h c) -> p h c", h=1).to_broadcast([P, 8, 32])
                dve.tensor_tensor(by_head(cpx), by_head(cpx), seen, ALU.mult).then_inc(*dve_made.mark(("c01", qt)))
                dve.wait_ge(*dve_made["c01", qt])
                dve.tensor_reduce(den, by_head(cpx), AX.X, ALU.add).then_inc(*dve_made.mark(("cden", qt)))
                dve.wait_ge(*dve_made["cden", qt])
                dve.tensor_scalar(dzero, den, 0.0, None, ALU.is_equal).then_inc(*dve_made.mark(("cz", qt)))
                dve.wait_ge(*dve_made["cz", qt])
                dve.tensor_tensor(den, den, dzero, ALU.add).then_inc(*dve_made.mark(("cd1", qt)))
                dve.wait_ge(*dve_made["cd1", qt])
                dve.reciprocal(den, den).then_inc(*dve_made.mark(("cinv", qt)))
                dve.wait_ge(*dve_made["cinv", qt])
                if qt == 0:
                    dve.wait_ge(*act_made["gates", "turned", 0])
                dve.tensor_tensor(den, den, gates[:, qt, 0:24:3], ALU.mult).then_inc(*dve_made.mark(("cg", qt)))
                yield
                dve.wait_ge(*dve_made["cg", qt])
                dve.wait_ge(*filled["co", qt])
                dve.tensor_tensor(onat[:, qt, 512:1024].rearrange("p (h c) -> p h c", h=8),
                                  by_head(banks["co", qt][:, :]),
                                  den.rearrange("p (h c) -> p h c", c=1).to_broadcast([P, 8, DH]), ALU.mult)\
                   .then_inc(*dve_made.mark(("cout", qt)))
                banks.drain(("co", qt), "dve_made")
                yield

        then(alternate(spread(3 * len(items) + 1, 3 * NT),
                       project(items, None, rtmp, vt, pool=POOLS[0], vt_free=filled["gates", "nat", 0]),
                       (act_cmp, pe_cmp, dve_cmp)))

        def small_cols(base, i, n=3):
            return small[:, base + i % n:base + i % n + 1]

        maps = []
        for b in range(2):
            for h in range(8):
                g, c = divmod(h, 4)
                r = slice(DH * g, DH * g + DH)
                for qt in range(NT):
                    W = (qt + 1) * P
                    maps.append(dict(
                        q=nq[r, c, qt * P:W], k=ksw[r, b, 0:W], width=W,
                        masks=[(identb, cstb("causal"), qt * P, ())],
                        v=lambda t, b=b, g=g: vsw[:, b, t, g * DH:(g + 1) * DH],
                        out=onat[:, qt, 512 + h * DH:512 + (h + 1) * DH],
                        gate=gates[:, qt, 3 * h + 1 + b:3 * h + 2 + b],
                        add=dve_made["cout", qt] if b == 0 else dve_made["nsa", "out", h * NT + qt]))
        nsa = softmax_maps("nsa", maps, Pb, PT, lambda i: small_cols(32, i), lambda i: small_cols(36, i, 6),
                           [dve_made["vsw", "turned", 1], dve_made["nq", "roped", 3], dve_made["cout", NT - 1]],
                           (4, 5, 6), (NBANK,))

        SB, STEPS = 8, 8
        SCORED = {0: (3,), 1: (2,), 2: (1,), 3: (0,)}
        SUMMED = {5: (3, 2), 6: (1,), 7: (0,)}

        def from_kt(bank, kt):
            return bank[:, kt * P:SEQ]

        def pe_sb(pe):
            pe.wait_ge(*dve_made["sv", "turned", 3])

            def scores(h, kt):
                r = slice(DH * (h % 2), DH * (h % 2) + DH)
                bank = banks.take(pe, ("z", h, kt), (kt,))
                mm(pe, from_kt(bank, kt), lhsT=sk[r, h // 2, kt * P:(kt + 1) * P], rhs=sq[r, h // 2, kt * P:SEQ],
                   start=True, stop=True, done=("z", h, kt))

            def sums(h, kt):
                bank = banks["z", h, kt]
                pe.wait_ge(*pool_made["sp", h, kt])
                mm(pe, bank[:, kt * P:(kt + 1) * P], lhsT=identb, rhs=cstb("strictT"), start=False, stop=False,
                   skip_group_check=True)
                for jt in range(kt, NT):
                    mm(pe, from_kt(bank, jt), lhsT=cst("tri" if jt == kt else "nones"), rhs=sp[jt], start=False,
                       stop=(jt == NT - 1), skip_group_check=True, done=("r", h, kt) if jt == NT - 1 else None)

            def values(h):
                for kt in range(NT):
                    pe.wait_ge(*act_made["a", h, kt])
                bank = banks.take(pe, ("so", h), (NBANK,))
                for qt in range(NT):
                    for kt in range(qt + 1):
                        mm(pe, bank[:, qt * DH:(qt + 1) * DH], lhsT=aa[kt][:, (qt - kt) * P:(qt - kt + 1) * P],
                           rhs=sv[:, kt, h * DH:(h + 1) * DH], start=(kt == 0), stop=(kt == qt),
                           done=("so", h) if (qt, kt) == (NT - 1, NT - 1) else None)

            for step in range(SB * STEPS + 4):
                h, r = divmod(step, STEPS)
                for kt in SCORED.get(r, ()) if h < SB else ():
                    scores(h, kt)
                for kt in SUMMED.get(r, ()) if h < SB else ():
                    sums(h, kt)
                if h and r == 2:
                    values(h - 1)
                yield

        def act_sb(act):
            def head(h, kt):
                act.wait_ge(*filled["z", h, kt])
                if h:
                    act.wait_ge(*dve_made["sp0", h - 1, kt])
                act.activation(za[kt], from_kt(banks["z", h, kt], kt), ACT.Abs).then_inc(*act_made.mark(("z1", h, kt)))
                act.wait_ge(*act_made["z1", h, kt])
                act.activation(za[kt], za[kt], ACT.Exp, scale=-1.0).then_inc(*act_made.mark(("z2", h, kt)))

            def weights(h, kt):
                act.wait_ge(*filled["r", h, kt])
                if h:
                    act.wait_ge(*filled["so", h - 1])
                act.activation(aa[kt], from_kt(banks["z", h, kt], kt), ACT.Exp).then_inc(*act_made.mark(("a", h, kt)))
                banks.drain(("z", h, kt), "act_made")

            act.wait_ge(*dve_made["cout", NT - 1])
            for step in range(SB * STEPS + 4):
                h, r = divmod(step, STEPS)
                if h and r == 0:
                    weights(h - 1, 0)
                for kt in SCORED.get(r, ()) if h < SB else ():
                    head(h, kt)
                if h < SB and r == 4:
                    for kt in range(NT - 1, -1, -1):
                        act.wait_ge(*act_made["z2", h, kt])
                        act.activation(za[kt], za[kt], ACT.Ln, bias=1.0).then_inc(*act_made.mark(("z3", h, kt)))
                if h < SB and r >= 6:
                    for kt in ((3, 2), (1,))[r - 6]:
                        weights(h, kt)
                yield

        def dve_sb(dve):
            for step in range(SB * STEPS + 4):
                h, r = divmod(step, STEPS)
                if h < SB and r == 4:
                    for kt in range(NT - 1, -1, -1):
                        dve.wait_ge(*act_made["z3", h, kt])
                        if h:
                            dve.wait_ge(*filled["r", h - 1, 0])
                        dve.scalar_tensor_tensor(out=sp[kt], in0=from_kt(banks["z", h, kt], kt), scalar=0.0,
                                                 in1=za[kt], op0=ALU.max, op1=ALU.add)\
                           .then_inc(*dve_made.mark(("sp0", h, kt)))
                if h and r == 2:
                    o = h - 1
                    dve.wait_ge(*filled["so", o])
                    dve.tensor_copy(onat[:, :, o * DH:(o + 1) * DH],
                                    banks["so", o][:, 0:NT * DH].rearrange("p (t c) -> p t c", t=NT))\
                       .then_inc(*dve_made.mark(("sbout", o)))
                    banks.drain(("so", o), "dve_made")
                yield

        def pool_sb(pool):
            for step in range(SB * STEPS + 4):
                h, r = divmod(step, STEPS)
                if h < SB and r == 4:
                    for kt in range(NT - 1, -1, -1):
                        pool.wait_ge(*dve_made["sp0", h, kt])
                        d = sp[kt][:, 0:P]
                        pool.tensor_tensor(d, d, cst("strict"), ALU.mult).then_inc(*pool_made.mark(("sp", h, kt)))
                yield

        then(alternate([0, 1] * (SB * STEPS + 4), (act_sb, pe_sb, dve_sb, pool_sb), (*nsa, None)))

        oT = Area().take_r(2, KD, SEQ)
        then(act=lambda act: keep_up(act, "act", ("mix0", 0)), dve=lambda dve: keep_up(dve, "dve", ("mix0", 0)))
        then(turned_parts("ot0", onat, oT, [dve_made["sbout", 7], dve_made["nsa", "out", 63]]))
        then(back_to_x("mix0", oT, KD, lo_of("ot0"), "f0"))

        csil, mod, gsc = small[:, 64:72], small[:, 80:128], small[:, 128:144]
        prog["act"].insert(2, lambda act: act.activation(csil, vec[:, VEC["c", 0]:VEC["c", 0] + KD], ACT.Silu)
                           .then_inc(*act_made.mark("csil")))

        def ffn(layer, nxt, hfree, arena_free):
            key = f"f{layer}"
            then(norm(key, ("ffn_norm", layer), hfree))
            A = Area()
            gT = A.take_r(2, FH, SEQ)
            cv = A.take(3, SEQ)
            sl = A.take(3, SEQ)
            acc = A.take(D)

            def dve_ada(dve, step):
                l, b, k = step
                panel = ada_panel[step]
                landed(dve, panel)
                w = ring[:, panel % RAW, :, :].rearrange("p a b -> p (a b)")
                if k == 0:
                    dve.wait_ge(*act_made["csil"])
                    if b:
                        dve.wait_ge(*filled["mod", l, b - 1])
                    i = dve.tensor_scalar(acc, w, csil[:, 0:1], None, ALU.mult)
                else:
                    dve.wait_ge(*dve_made["ada", l, b, k - 1])
                    i = dve.scalar_tensor_tensor(out=acc, in0=w, scalar=csil[:, k:k + 1], in1=acc, op0=ALU.mult,
                                                 op1=ALU.add)
                i.then_inc(*dve_made.mark(("ada", l, b, k)))
                dve_made.at["ada panel", panel] = dve_made.count

            def pe_ada(pe, l, b):
                pe.wait_ge(*dve_made["ada", l, b, KD - 1])
                bank = banks.take(pe, ("mod", l, b))
                for i in range(KD):
                    mm(pe, bank[:, i:i + 1], lhsT=acc[:, i * P:(i + 1) * P], rhs=cst("ones")[:, 0:1], start=True,
                       stop=True, done=("mod", l, b) if i == KD - 1 else None)

            def dve_mod(dve, l, b):
                dve.wait_ge(*filled["mod", l, b])
                o = VEC["b_ada", l] + KD * b
                m = 24 * l + KD * b
                dve.tensor_tensor(mod[:, m:m + KD], banks["mod", l, b][:, 0:KD], vec[:, o:o + KD], ALU.add)\
                   .then_inc(*dve_made.mark(("mod", l, b)))
                banks.drain(("mod", l, b), "dve_made")
                if b == 1:
                    dve.wait_ge(*dve_made["mod", l, b])
                    o = VEC["norm_g", l]
                    dve.scalar_tensor_tensor(out=gsc[:, 8 * l:8 * l + 8], in0=mod[:, m:m + KD], scalar=1.0,
                                             in1=vec[:, o:o + 8], op0=ALU.add, op1=ALU.mult)\
                       .then_inc(*dve_made.mark(("gsc", l)))
                    dve.wait_ge(*dve_made["gsc", l])

            complete = {n: b for n in range(FC) for _, b, k in ada_steps(layer, n) if k == KD - 1}
            final = max(complete)

            def parts(first):
                chunks = range(first, first + FH)

                def pe_part(pe):
                    for n in chunks:
                        pe_linear(pe, (key, "a"), n, hT, KD, h_at(key) if n == 0 else None)
                        pe_linear(pe, (key, "b"), n, hT, KD, None)
                        for _ in ada_steps(layer, n):
                            tile_no[0] += KD
                        if n - 1 in complete:
                            pe_ada(pe, layer, complete[n - 1])

                def act_g(act, n):
                    act.wait_ge(*dve_made[key, "g", n])
                    act_hi(act, gT[:, 0, n % FH, :], sl[:, n % 3, :], (key, "g", n))

                def act_part(act):
                    if first == 0:
                        act.wait_ge(*arena_free)
                    for n in chunks:
                        if n > first:
                            act_g(act, n - 1)
                        free = [act_made[(key, "a"), "silu", n - 3]] if n >= 3 else []
                        act_conv_start(act, (key, "a"), n, cv[:, n % 3, :], col("conv_w", (layer, 2), n),
                                       col("conv_b", layer, n), free)
                        act.wait_ge(*dve_made[(key, "a"), "taps", n, 1])
                        if n >= 3:
                            act.wait_ge(*dve_made[(key, "g", n - 3), "lo"])
                        act.activation(sl[:, n % 3, :], cv[:, n % 3, :], ACT.Silu)\
                           .then_inc(*act_made.mark(((key, "a"), "silu", n)))
                        keep_up(act, "act", ((key, "b"), n))
                    act_g(act, chunks[-1])

                def dve_part(dve):
                    def lo(n):
                        dve_lo(dve, gT[:, 0, n % FH, :], gT[:, 1, n % FH, :], sl[:, n % 3, :], (key, "g", n))
                    for n in chunks:
                        if n > first:
                            lo(n - 1)
                        dve_conv_taps(dve, (key, "a"), n, cv[:, n % 3, :],
                                      [col("conv_w", (layer, 1), n), col("conv_w", (layer, 0), n)])
                        dve.wait_ge(*act_made[(key, "a"), "silu", n])
                        dve_bank(dve, ((key, "b"), n))
                        dve.tensor_tensor(sl[:, n % 3, :], sl[:, n % 3, :], banks[(key, "b"), n][:, :], ALU.mult)\
                           .then_inc(*dve_made.mark((key, "g", n)))
                        banks.drain(((key, "b"), n), "dve_made")
                        if n - 1 in complete:
                            dve_mod(dve, layer, complete[n - 1])
                        for step in ada_steps(layer, n):
                            dve_ada(dve, step)
                    lo(chunks[-1])
                return act_part, pe_part, dve_part

            then(parts(0))
            then(back_to_x((key, "y0"), gT, FH, lambda k: dve_made[(key, "g", k), "lo"], None))
            then(parts(FH))
            if final == FC - 1:
                then(pe=lambda pe: pe_ada(pe, layer, complete[final]), dve=lambda dve: dve_mod(dve, layer, complete[final]))
            then(back_to_x((key, "y"), gT, FH, lambda k: dve_made[(key, "g", FH + k), "lo"], nxt))

        ffn(0, "h1", filled["sv", 3], filled["mix0", KD - 1])

        def act_rot(act):
            act.wait_ge(*dve_made["nq", "roped", 3])
            act.dma_start(rot[:, :, :].rearrange("p a b -> p (a b)"), rot_in[:, 2 * SEQ:4 * SEQ]).then_inc(rot_landed, 16)

        then(act=act_rot)

        then(norm("h1", ("attn_norm", 1), filled[("f0", "b"), FC - 1]))
        A = Area()
        q1, k1 = A.take(KD, SEQ), A.take(KD, SEQ)
        v1 = A.take(NT, D)
        onat1 = A.take(NT, D)
        Pb1, PT1 = A.take(3, SEQ), A.take(3, SEQ)
        rest, rest2 = PT1[:, 0, :], PT1[:, 1, :]
        ff, lf, cum = A.take(SEQ), A.take(SEQ), A.take(SEQ)
        parts3 = A.take16(SEQ)
        vt1 = A.take(2, SEQ)
        oT1 = Area().take_r(2, KD, SEQ)

        def act_f(act):
            act.wait_ge(*dve_made["f+b"])
            act.activation(lf[0:16, :], ff[0:16, :], ACT.Abs).then_inc(*act_made.mark("f1"))
            act.wait_ge(*act_made["f1"])
            act.activation(lf[0:16, :], lf[0:16, :], ACT.Exp, scale=-1.0).then_inc(*act_made.mark("f2"))
            act.wait_ge(*act_made["f2"])
            act.activation(lf[0:16, :], lf[0:16, :], ACT.Ln, bias=1.0).then_inc(*act_made.mark("f3"))

        def dve_f(dve):
            dve.wait_ge(*filled["f", 0])
            dve.tensor_scalar(ff[0:16, :], banks["f", 0][0:16, :], col("b_f", 0, 0, 16), None, ALU.add)\
               .then_inc(*dve_made.mark("f+b"))
            banks.drain(("f", 0), "dve_made")
            dve.memset(parts3[0:96, :], 0.0).then_inc(*dve_made.mark("p0"))

        def dve_cum(dve):
            dve.wait_ge(*act_made["f3"])
            dve.scalar_tensor_tensor(out=lf[0:16, :], in0=ff[0:16, :], scalar=0.0, in1=lf[0:16, :], op0=ALU.min,
                                     op1=ALU.subtract).then_inc(*dve_made.mark("lf"))
            dve.wait_ge(*dve_made["lf"])
            dve.tensor_tensor_scan(cum[0:16, :], cst("ones")[0:16, 0:1].to_broadcast([16, SEQ]), lf[0:16, :], 0.0, ALU.mult, ALU.add)\
               .then_inc(*dve_made.mark("cum"))
            dve.wait_ge(*dve_made["cum"])
            dve.tensor_copy(parts3[0:16, :], cum[0:16, :]).then_inc(*dve_made.mark("hi"))
            dve.wait_ge(*dve_made["hi"])
            dve.tensor_tensor(rest[0:16, :], cum[0:16, :], parts3[0:16, :], ALU.subtract)\
               .then_inc(*dve_made.mark("rest"))
            dve.wait_ge(*dve_made["rest"])
            dve.tensor_copy(rest2[0:16, :].bitcast(BF16)[:, 0:SEQ], rest[0:16, :]).then_inc(*dve_made.mark("mid"))
            dve.wait_ge(*dve_made["mid"])
            dve.tensor_copy(parts3[32:48, :], rest2[0:16, :].bitcast(BF16)[:, 0:SEQ]).then_inc(*dve_made.mark("midp"))
            dve.tensor_tensor(rest[0:16, :], rest[0:16, :], rest2[0:16, :].bitcast(BF16)[:, 0:SEQ], ALU.subtract)\
               .then_inc(*dve_made.mark("rest2"))
            dve.wait_ge(*dve_made["rest2"])
            dve.tensor_copy(parts3[64:80, :], rest[0:16, :]).then_inc(*dve_made.mark("lo"))

        items = [item("f", 0, "own", do=dve_f)]
        for c in range(KD):
            items += [item("q1", c, "copy", q1[:, c, :], scale=SCALE), item("k1", c, "copy", k1[:, c, :]),
                      item("v1", c, "turn", v1[:, :, c * P:(c + 1) * P])]
        then(act=lambda act: act.wait_ge(*filled[("f0", "y"), KD - 1]), dve=lambda dve: dve.wait_ge(*filled[("f0", "y"), KD - 1]))
        then(project(items[:4], h_at("h1"), None, vt1))
        then(act=act_f, dve=dve_cum)

        maps = []
        for h in range(16):
            r = slice(DH * (h % 2), DH * (h % 2) + DH)
            for qt in range(NT):
                W = (qt + 1) * P
                maps.append(dict(
                    q=q1[r, h // 2, qt * P:W], k=k1[r, h // 2, 0:W], width=W,
                    masks=[(cstb("selneg")[0:96, h:h + 1].to_broadcast([96, P]), parts3[0:96, 0:W], 0, ()),
                           (identb, cstb("causal"), qt * P, ())],
                    v=lambda t, h=h: v1[:, t, h * DH:(h + 1) * DH],
                    out=onat1[:, qt, h * DH:(h + 1) * DH], gate=None, add=None,
                    before=(act_made["q1", h // 2], act_made["k1", h // 2]), value=dve_made["v1", "turned", h // 2]))
        fox = softmax_maps("fox", maps, Pb1, PT1, lambda i: small_cols(32, i), lambda i: small_cols(36, i, 6),
                           [dve_made["lo"]], *POOLS[1:])
        order = [0, 0, 0] + spread(6, 8) + spread(9, 8) * (KD - 2) + [0] + [1] * (len(maps) + 3)
        then(alternate(order, project(items[4:], None, None, vt1, vt_free=filled["v1", "nat", 0], pool=POOLS[0]), fox))
        then(turned_parts("ot1", onat1, oT1, [dve_made["fox", "out", 63]]))
        then(back_to_x("mix1", oT1, KD, lo_of("ot1"), "f1"))
        ffn(1, "xn", filled["v1", KD - 1], filled["mix1", KD - 1])

        then(norm("xn", ("final_norm", 0), to_x=True))
        then(act=lambda act: [act_square(act, "L0h", xT, k, [dve_made["xn", "scaled", k]]) for k in range(KD)],
             pe=lambda pe: [pe_mean(pe, "L0h", k) for k in range(KD)])

        ROPE32 = ("perm32", rot[:, 0, :], rot[:, 1, :])

        def block2(l, nxt, hfree, arena_free):
            K = f"L{l}"
            hk = K + "h"
            then(norm(hk, None, hfree,
                      mod=(lambda k: gsc[:, 8 * l + k:8 * l + k + 1],
                           lambda k: mod[:, 24 * l + k:24 * l + k + 1])))
            A = Area()
            qi, ki = A.take(2, SEQ), A.take(SEQ)
            q, k_ = A.take(4, SEQ), A.take(SEQ)
            v = A.take(NT, DH)
            wi = A.take(NT, 4)
            xbc_at = A.at
            xbc = A.take(12, SEQ)
            oT_at = A.at
            oT = A.take(4, SEQ)
            gate_at = A.at
            mask = A.take16(3 * SEQ)
            dts = A.take(4, SEQ)
            tops = A.take(16, 8)
            work = A.at
            score = A.take(3, SEQ)
            vt = Area(A.at).take(2, SEQ)
            onat = A.take(NT, 512)
            Pb = A.take(3, SEQ)
            rtmp = Area(A.at).take(2, SEQ)
            relu = hv[:, 0:2, :]
            PT = A.take(3, SEQ)

            xw = lambda j, n: col("xconv_w", (l, j), n)

            def dve_dt(dve):
                dve.wait_ge(*filled[K + "dt", 0])
                dve.tensor_scalar(dts[0:16, 0, :], banks[K + "dt", 0][0:16, :], col("dt_bias", l, 0, 16), None,
                                  ALU.add).then_inc(*dve_made.mark(K + "dtb"))
                banks.drain((K + "dt", 0), "dve_made")

            items = [item(K + "qi", n, "rope", qi[:, n, :]) for n in range(2)]
            items += [item(K + "ki", 0, "rope", ki), item(K + "wi", 0, "turn", wi, width=4, scale=0.5)]
            later = [item(K + "q", n, "rope", q[:, n, :], scale=SCALE) for n in range(4)]
            later += [item(K + "k", 0, "rope", k_), item(K + "v", 0, "turn", v, width=DH)]
            later += [item(K + "dt", 0, "own", do=dve_dt)]
            then(act=lambda act: act.wait_ge(*arena_free), dve=lambda dve: dve.wait_ge(*arena_free))
            if l == 0:
                then(dve=lambda dve: dve.wait_ge(rot_landed, 32))
            then(project(items, h_at(hk), rtmp, vt, ROPE32))

            def conv(first, end, silu_now, pool=ALL_BANKS):
                def pe_conv(pe):
                    for n in range(first, end):
                        linear = pe_linear_steps(pe, K + "xbc", n, hT, KD, None, pool)
                        for _ in range(3):
                            next(linear, None)
                            yield

                def silu(act, n):
                    act.wait_ge(*dve_made[K + "xbc", "taps", n, 2])
                    act.activation(xbc[:, n, :], xbc[:, n, :], ACT.Silu).then_inc(*act_made.mark((K + "xbc", "silu", n)))

                def act_conv(act):
                    for n in range(first, end):
                        keep_up(act, "act", (K + "xbc", n))
                        yield
                        if n > first and silu_now:
                            silu(act, n - 1)
                        yield
                        act_conv_start(act, K + "xbc", n, xbc[:, n, :], xw(3, n), col("xconv_b", l, n), ())
                        yield
                    for n in (end - 1,) if silu_now else reversed(range(first, end)):
                        silu(act, n)

                def dve_conv(dve):
                    for n in range(first, end):
                        keep_up(dve, "dve", (K + "xbc", n))
                        yield
                        yield
                        dve_conv_taps(dve, K + "xbc", n, xbc[:, n, :], [xw(2, n), xw(1, n), xw(0, n)])
                        yield
                return act_conv, pe_conv, dve_conv, None

            def act_dt(act):
                t = dts[0:16, 1, :]
                act.wait_ge(*dve_made[K + "dtb"])
                act.activation(t, dts[0:16, 0, :], ACT.Abs).then_inc(*act_made.mark(K + "d1"))
                act.wait_ge(*act_made[K + "d1"])
                act.activation(t, t, ACT.Exp, scale=-1.0).then_inc(*act_made.mark(K + "d2"))
                act.wait_ge(*act_made[K + "d2"])
                act.activation(t, t, ACT.Ln, bias=1.0).then_inc(*act_made.mark(K + "d3"))
                act.activation(small[0:16, 160:161], col("a_log", l, 0, 16), ACT.Exp)\
                   .then_inc(*act_made.mark(K + "ea"))
                for t in range(NT):
                    s = slice(t * P, (t + 1) * P)
                    act.wait_ge(*dve_made[K + "acs", t])
                    act.activation(dts[0:16, 2, s], dts[0:16, 3, s], ACT.Exp, scale=-1.0,
                                   bias=dts[0:16, 3, t * P + P - 1:t * P + P]).then_inc(*act_made.mark((K + "ds", t)))

            def dve_dt_sums(dve):
                dt, t, acs = dts[0:16, 0, :], dts[0:16, 1, :], dts[0:16, 3, :]
                dve.wait_ge(*act_made[K + "ea"])
                dve.scalar_tensor_tensor(out=dt, in0=dt, scalar=0.0, in1=t, op0=ALU.max, op1=ALU.add)\
                   .then_inc(*dve_made.mark(K + "dt"))
                dve.wait_ge(*dve_made[K + "dt"])
                dve.tensor_scalar(t, dt, small[0:16, 160:161], -1.0, ALU.mult, ALU.mult)\
                   .then_inc(*dve_made.mark(K + "adt"))
                dve.wait_ge(*dve_made[K + "adt"])
                for c in range(NT):
                    s = slice(c * P, (c + 1) * P)
                    dve.tensor_tensor_scan(acs[:, s], cst("ones")[0:16, :], t[:, s], 0.0, ALU.mult, ALU.add)\
                       .then_inc(*dve_made.mark((K + "acs", c)))

            def pe_index(pe):
                pe.wait_ge(*dve_made[K + "ki", "roped", 0])
                for qt in range(1, NT):
                    W = (qt + 1) * P
                    for h in range(4):
                        r = slice(DH * (h % 2), DH * (h % 2) + DH)
                        bank = banks.take(pe, (K + "ix", qt, h), POOLS[1])
                        mm(pe, bank[:, 0:W], lhsT=qi[r, h // 2, qt * P:W], rhs=ki[r, 0:W], start=True, stop=True,
                           done=(K + "ix", qt, h))
                        yield

            def act_index(act):
                for qt in range(1, NT):
                    W = (qt + 1) * P
                    for h in range(4):
                        i = (qt - 1) * 4 + h
                        act.wait_ge(*filled[K + "ix", qt, h])
                        if i >= 2:
                            act.wait_ge(*dve_made[K + "sc", (i - 2) // 4 + 1, (i - 2) % 4])
                        act.activation(relu[:, i % 2, 0:W], banks[K + "ix", qt, h][:, 0:W], ACT.Relu, scale=SCALE)\
                           .then_inc(*act_made.mark((K + "relu", qt, h)))
                        banks.drain((K + "ix", qt, h), "act_made")
                        yield

            def dve_index(dve):
                dve.wait_ge(*dve_made[K + "wi", "turned", 0])
                for qt in range(1, NT):
                    W = (qt + 1) * P
                    sc = score[:, qt - 1, 0:W]
                    for h in range(4):
                        i = (qt - 1) * 4 + h
                        dve.wait_ge(*act_made[K + "relu", qt, h])
                        w = wi[:, qt, h:h + 1]
                        if h == 0:
                            j = dve.tensor_scalar(sc, relu[:, i % 2, 0:W], w, None, ALU.mult)
                        else:
                            dve.wait_ge(*dve_made[K + "sc", qt, h - 1])
                            j = dve.scalar_tensor_tensor(out=sc, in0=relu[:, i % 2, 0:W], scalar=w, in1=sc,
                                                         op0=ALU.mult, op1=ALU.add)
                        j.then_inc(*dve_made.mark((K + "sc", qt, h)))
                        yield

            def dve_top(dve):
                dve.wait_ge(*dve_made[K + "sc", NT - 1, 3])
                for qt in range(1, NT):
                    W = (qt + 1) * P
                    sc = score[:, qt - 1, 0:W]
                    dve.wait_ge(*pool_made[K + "adm", qt])
                    for r in range(TOPK // 8):
                        if r:
                            dve.wait_ge(*dve_made[K + "rep", qt, r - 1])
                        dve.max(tops[:, r, :], sc).then_inc(*dve_made.mark((K + "top", qt, r)))
                        dve.wait_ge(*dve_made[K + "top", qt, r])
                        dve.match_replace(sc, tops[:, r, :], sc, TAKEN).then_inc(*dve_made.mark((K + "rep", qt, r)))
                        if r < TOPK // 8 - 1:
                            yield
                    dve.wait_ge(*dve_made[K + "rep", qt, TOPK // 8 - 1])
                    dve.tensor_scalar(mask[:, (qt - 1) * SEQ:(qt - 1) * SEQ + W], sc, TAKEN / 2, NEG, ALU.is_gt,
                                      ALU.mult).then_inc(*dve_made.mark((K + "mask", qt)))
                    yield

            def pool_index(pool):
                for qt in range(1, NT):
                    for h in range(4):
                        if h == 3:
                            d = score[:, qt - 1, qt * P:(qt + 1) * P]
                            pool.wait_ge(*dve_made[K + "sc", qt, 3])
                            pool.affine_select(out=d, in_=d, compare_op=ALU.is_ge, fill=NEG, base=0,
                                               pattern=[[-1, P]], channel_multiplier=1)\
                                .then_inc(*pool_made.mark((K + "adm", qt)))
                        yield

            maps = []
            for qt in range(NT):
                for h in range(8):
                    r = slice(DH * (h % 2), DH * (h % 2) + DH)
                    W = (qt + 1) * P
                    if qt == 0:
                        ms = [(identb, cstb("causal"), 0, ())]
                    else:
                        ms = [(identb, mask[:, (qt - 1) * SEQ:(qt - 1) * SEQ + W], 0, (dve_made[K + "mask", qt],))]
                    maps.append(dict(q=q[r, h // 2, qt * P:W], k=k_[r, 0:W], width=W, masks=ms,
                                     v=lambda t: v[:, t, :], out=onat[:, qt, h * DH:(h + 1) * DH],
                                     gate=None, add=None))
            dsa = softmax_maps(K + "dsa", maps, Pb, PT, lambda i: small_cols(32, i), lambda i: small_cols(36, i, 6),
                               [dve_made[K + "v", "turned", 0], dve_made[K + "k", "roped", 0]], *POOLS[1:], dve_every=DSA_EVERY)
            def one_step(f):
                def run(eng):
                    f(eng)
                    yield
                return run

            strands = (
                one_after_the_other(project(later, None, rtmp, vt, ROPE32, pool=POOLS[0]),
                                    (one_step(act_dt), one_step(lambda pe: None), one_step(dve_dt_sums)),
                                    conv(0, EARLY, True, POOLS[0]), conv(EARLY, 12, False, POOLS[0])),
                one_after_the_other((act_index, pe_index, dve_index, pool_index), (None, None, dve_top)),
                dsa)
            index_steps, rounds = 4 * (NT - 1), TOPK // 8
            before = 3 * len(later) + 2 + 3 * EARLY - index_steps
            order = [1, 0] * index_steps + spread(before, rounds)
            order += spread(3 * MIDDLE, rounds, 8) + spread(3 * MIDDLE, rounds, 8)
            order += spread(3 * (12 - EARLY - 2 * MIDDLE), 0, 19)
            then(alternate(order, *strands))
            then(turned(K + "ot", onat, oT, 4, [dve_made[K + "dsa", "out", 31]]))

            A = Area(work)
            xd = A.take(NT, D)
            st = A.take(3, D)
            bn = hv[:, 0:2, :].rearrange("p a (t w) -> p (a t) w", t=2)
            cbt = hv[:, 2:4, :]
            B = Area()
            xds, eb, dg, ce = (B.take(2, SEQ) for _ in range(4))
            natd = B.take(3, NT, 16)
            acs3 = mask[:, 0:SEQ]
            lastd = B.take(16, NT)
            cd = small[:, 168:232].rearrange("p (h t) -> p h t", h=16)
            after_att = [filled[K + "ot", 3]]

            def pe_ssd(pe):
                for n in range(12):
                    pe.wait_ge(*act_made[K + "xbc", "silu", n])
                for t in range(NT):
                    pe.wait_ge(*act_made[K + "ds", t])
                bank = banks.take(pe, (K + "nat", 0))
                for j, row in enumerate((0, 3, 2)):
                    for t in range(NT):
                        o = (j * NT + t) * 16
                        tp(pe, bank[:, o:o + 16], dts[0:16, row, t * P:(t + 1) * P], ident[0:16, 0:16],
                           done=(K + "nat", 0) if (j, t) == (2, NT - 1) else None)
                pe.wait_ge(*dve_made[K + "lastd"])
                bank = banks.take(pe, (K + "last", 0))
                mm(pe, bank[:, 0:16 * NT], lhsT=cst("ones")[0:16, 0:P], rhs=lastd[0:16, :, :].rearrange("p a b -> p (a b)"),
                   start=True, stop=True, done=(K + "last", 0))
                for g in range(2):
                    bank = banks.take(pe, (K + "cb", g))
                    for t in range(NT):
                        s = slice(t * P, (t + 1) * P)
                        mm(pe, bank[:, s], lhsT=xbc[:, 8 + g, s], rhs=xbc[:, 10 + g, s], start=True, stop=True,
                           done=(K + "cb", g) if t == NT - 1 else None)
                    bank = banks.take(pe, (K + "bn", g))
                    for t in range(NT):
                        s = slice(t * P, (t + 1) * P)
                        tp(pe, bank[:, s], xbc[:, 8 + g, s], ident, done=(K + "bn", g) if t == NT - 1 else None)
                for t in range(NT):
                    for half in range(2):
                        bank = banks.take(pe, (K + "xt", t, half))
                        for j in range(4):
                            tp(pe, bank[:, j * P:(j + 1) * P], xbc[:, half * 4 + j, t * P:(t + 1) * P], ident,
                               done=(K + "xt", t, half) if j == 3 else None)
                for g in range(2):
                    pe.wait_ge(*act_made[K + "bn", g])
                for t in range(NT - 1):
                    for g in range(2):
                        pe.wait_ge(*dve_made[K + "xds", t, g])
                        bank = banks.take(pe, (K + "st", t, g))
                        mm(pe, bank[:, :], lhsT=bn[:, t, g * P:(g + 1) * P], rhs=xds[:, g, :], start=True, stop=True,
                           done=(K + "st", t, g))

                def spread(h):
                    bank = banks.take(pe, (K + "bc", h))
                    mm(pe, bank[:, :], lhsT=cstb("selneg")[0:96, h:h + 1].to_broadcast([96, P]), rhs=acs3[0:96, :],
                       start=True, stop=True, done=(K + "bc", h))
                    bank = banks.take(pe, (K + "seg", h))
                    mm(pe, bank[:, :], lhsT=cstb("selneg")[0:96, h:h + 1].to_broadcast([96, P]), rhs=acs3[0:96, :],
                       start=True, stop=False)
                    for t in range(NT):
                        mm(pe, bank[:, t * P:(t + 1) * P], lhsT=acs3[0:96, t * P:(t + 1) * P],
                           rhs=cstb("sel")[0:96, h:h + 1].to_broadcast([96, P]), start=False, stop=False)
                        mm(pe, bank[:, t * P:(t + 1) * P], lhsT=identb, rhs=cstb("later"), start=False, stop=t == NT - 1,
                           done=(K + "seg", h) if t == NT - 1 else None)

                pe.wait_ge(*dve_made[K + "acs3"])
                spread(0)
                spread(1)
                pe.wait_ge(*dve_made[K + "st", NT - 2, 1])
                for h in range(16):
                    if h + 2 < 16:
                        spread(h + 2)
                    r = slice(DH * (h % 2), DH * (h % 2) + DH)
                    if h % 2 == 0:
                        bank = banks.take(pe, (K + "y", h // 2))
                    pe.wait_ge(*dve_made[K + "g", h])
                    pe.wait_ge(*pool_made[K + "ce", h])
                    for t in range(NT):
                        s = slice(t * P, (t + 1) * P)
                        last = t == NT - 1
                        mm(pe, bank[r, s], lhsT=xd[:, t, h * DH:(h + 1) * DH], rhs=dg[:, h % 2, s], start=True,
                           stop=(t == 0))
                        if t:
                            mm(pe, bank[r, s], lhsT=st[:, t - 1, h * DH:(h + 1) * DH], rhs=ce[:, h % 2, s],
                               start=False, stop=True,
                               done=((K + "y", h // 2) if h % 2 else (K + "yh", h)) if last else None)

            def act_ssd(act):
                act.wait_ge(*filled[K + "last", 0])
                act.activation(cd.rearrange("p a b -> p (a b)"), banks[K + "last", 0][:, 0:16 * NT], ACT.Exp)\
                   .then_inc(*act_made.mark(K + "cd"))
                banks.drain((K + "last", 0), "act_made")
                for g in range(2):
                    act.wait_ge(*filled[K + "cb", g])
                    act.activation(cbt[:, g, :], banks[K + "cb", g][:, :], ACT.Copy)\
                       .then_inc(*act_made.mark((K + "cb", g)))
                    banks.drain((K + "cb", g), "act_made")
                    act.wait_ge(*filled[K + "bn", g])
                    act.activation(bn[:, :, g * P:(g + 1) * P],
                                   banks[K + "bn", g][:, :].rearrange("p (t w) -> p t w", t=NT), ACT.Copy)\
                       .then_inc(*act_made.mark((K + "bn", g)))
                    banks.drain((K + "bn", g), "act_made")
                for h in range(16):
                    act.wait_ge(*filled[K + "bc", h])
                    if h >= 2:
                        act.wait_ge(*pool_made[K + "ce", h - 2])
                    act.activation(eb[:, h % 2, :], banks[K + "bc", h][:, :], ACT.Exp, scale=-1.0)\
                       .then_inc(*act_made.mark((K + "eb", h)))
                    banks.drain((K + "bc", h), "act_made")
                    act.wait_ge(*filled[K + "seg", h])
                    if h >= 2:
                        act.wait_ge(*filled[(K + "y", (h - 2) // 2) if h % 2 else (K + "yh", h - 2)])
                    act.activation(dg[:, h % 2, :], banks[K + "seg", h][:, :], ACT.Exp, scale=-1.0)\
                       .then_inc(*act_made.mark((K + "dg", h)))
                    banks.drain((K + "seg", h), "act_made")

            def heads_of(a, t, g, row):
                return natd[:, row, t, 8 * g:8 * g + 8].rearrange("p (h c) -> p h c", c=1).to_broadcast([P, 8, DH])

            def dve_ssd(dve):
                for w in after_att:
                    dve.wait_ge(*w)
                for t in range(NT):
                    dve.wait_ge(*dve_made[K + "acs", t])
                last = dts[0:16, 3, P - 1:SEQ:P].rearrange("p (a t) -> p a t", a=1).to_broadcast([16, 16, NT])
                dve.tensor_tensor(lastd[0:16, :, :], last,
                                  ident[0:16, 0:16].rearrange("p (h c) -> p h c", c=1).to_broadcast([16, 16, NT]),
                                  ALU.mult).then_inc(*dve_made.mark(K + "lastd"))
                dve.wait_ge(*filled[K + "nat", 0])
                b = banks[K + "nat", 0]
                dve.tensor_copy(natd.rearrange("p a t c -> p (a t c)"), b[:, 0:192]).then_inc(*dve_made.mark(K + "nat"))
                banks.drain((K + "nat", 0), "dve_made")
                dve.wait_ge(*dve_made[K + "nat"])
                acs, left, mid = dts[0:16, 3, :], dts[0:16, 1, :], mask[0:16, SEQ:2 * SEQ]
                dve.memset(acs3[0:96, :], 0.0).then_inc(*dve_made.mark((K + "part", 0)))
                dve.wait_ge(*dve_made[K + "part", 0])
                dve.tensor_copy(acs3[0:16, :], acs).then_inc(*dve_made.mark((K + "part", 1)))
                dve.wait_ge(*dve_made[K + "part", 1])
                dve.tensor_tensor(left, acs, acs3[0:16, :], ALU.subtract).then_inc(*dve_made.mark((K + "part", 2)))
                dve.wait_ge(*dve_made[K + "part", 2])
                dve.tensor_copy(mid, left).then_inc(*dve_made.mark((K + "part", 3)))
                dve.wait_ge(*dve_made[K + "part", 3])
                dve.tensor_copy(acs3[32:48, :], mid).then_inc(*dve_made.mark((K + "part", 4)))
                dve.tensor_tensor(left, left, mid, ALU.subtract).then_inc(*dve_made.mark((K + "part", 5)))
                dve.wait_ge(*dve_made[K + "part", 5])
                dve.tensor_copy(acs3[64:80, :], left).then_inc(*dve_made.mark(K + "acs3"))
                for t in range(NT):
                    for g in range(2):
                        dve.wait_ge(*filled[K + "xt", t, g])
                        d = xd[:, t, g * 512:(g + 1) * 512].rearrange("p (h c) -> p h c", h=8)
                        dve.tensor_tensor(d, banks[K + "xt", t, g][:, :].rearrange("p (h c) -> p h c", h=8),
                                          heads_of(None, t, g, 0), ALU.mult).then_inc(*dve_made.mark((K + "xd", t, g)))
                        banks.drain((K + "xt", t, g), "dve_made")
                for t in range(NT - 1):
                    for g in range(2):
                        d = xd[:, t, g * 512:(g + 1) * 512].rearrange("p (h c) -> p h c", h=8)
                        dve.wait_ge(*dve_made[K + "xd", t, g])
                        if t:
                            dve.wait_ge(*filled[K + "st", t - 1, g])
                        dve.tensor_tensor(xds[:, g, :].rearrange("p (h c) -> p h c", h=8), d, heads_of(None, t, g, 2),
                                          ALU.mult).then_inc(*dve_made.mark((K + "xds", t, g)))
                    for g in range(2):
                        dst = st[:, t, g * 512:(g + 1) * 512]
                        bank = banks[K + "st", t, g][:, :]
                        if t == 0:
                            dve.wait_ge(*filled[K + "st", t, g])
                            dve.tensor_copy(dst, bank).then_inc(*dve_made.mark((K + "st", t, g)))
                        else:
                            dve.wait_ge(*act_made[K + "cd"])
                            dve.wait_ge(*dve_made[K + "st", t - 1, g])
                            prev = st[:, t - 1, g * 512:(g + 1) * 512].rearrange("p (h c) -> p h c", h=8)
                            decay = cd[:, 8 * g:8 * g + 8, t:t + 1].to_broadcast([P, 8, DH])
                            dve.tensor_tensor(dst.rearrange("p (h c) -> p h c", h=8), prev, decay, ALU.mult)\
                               .then_inc(*dve_made.mark((K + "std", t, g)))
                            dve.wait_ge(*dve_made[K + "std", t, g])
                            dve.wait_ge(*filled[K + "st", t, g])
                            dve.tensor_tensor(dst, dst, bank, ALU.add).then_inc(*dve_made.mark((K + "st", t, g)))
                        banks.drain((K + "st", t, g), "dve_made")

                for g in range(2):
                    dve.wait_ge(*act_made[K + "cb", g])
                for h in range(16):
                    dve.wait_ge(*act_made[K + "dg", h])
                    dve.tensor_tensor(dg[:, h % 2, :], dg[:, h % 2, :], cbt[:, h // 8, :], ALU.mult)\
                       .then_inc(*dve_made.mark((K + "g", h)))
                    if h % 2:
                        c = h // 2
                        if c:
                            drain_y(dve, c - 1)
                drain_y(dve, KD - 1)

            def drain_y(dve, c):
                dve.wait_ge(*filled[K + "y", c])
                dve.scalar_tensor_tensor(out=xbc[:, c, :], in0=xbc[:, c, :], scalar=col("d_skip", l, c),
                                         in1=banks[K + "y", c][:, :], op0=ALU.mult, op1=ALU.add)\
                   .then_inc(*dve_made.mark((K + "y", c)))
                banks.drain((K + "y", c), "dve_made")

            def pool_ssd(pool):
                for h in range(16):
                    pool.wait_ge(*act_made[K + "eb", h])
                    if h >= 2:
                        pool.wait_ge(*filled[(K + "y", (h - 2) // 2) if h % 2 else (K + "yh", h - 2)])
                    pool.tensor_tensor(ce[:, h % 2, :], eb[:, h % 2, :], xbc[:, 10 + h // 8, :], ALU.mult)\
                       .then_inc(*pool_made.mark((K + "ce", h)))

            then(pe=pe_ssd, act=act_ssd, dve=dve_ssd, pool=pool_ssd)

            A = Area(gate_at)
            sg = A.take(2, 2, SEQ)
            at = A.at
            sil = A.take(3, SEQ)
            A.at = at
            mg = A.take_r(2, KD, SEQ)
            sq2 = Area().take(KD, SEQ)
            ys_hi = Area(xbc_at).take_r(KD, SEQ)
            ys_lo = Area().take_r(KD, SEQ)
            oa = Area(oT_at).take_r(4, SEQ), Area(xbc_at + KD * SEQ).take_r(4, SEQ)

            def pe_gate(pe):
                for n in range(4):
                    pe_linear(pe, K + "ga", n, hT, KD, None)
                for n in range(KD):
                    pe_linear(pe, K + "z", n, hT, KD, None)

            def act_gate(act):
                act.wait_ge(*filled[K + "y", KD - 1])
                for i in range(12):
                    key = (K + "ga", i) if i < 4 else (K + "z", i - 4)
                    act_bank(act, key)
                    if i >= 3:
                        act.wait_ge(*(dve_made[(K + "oa", i - 3), "lo"] if i < 7 else dve_made[K + "gated", i - 3]))
                    act.activation(sil[:, i % 3, :], banks[key][:, :], ACT.Silu)\
                       .then_inc(*act_made.mark((K + "sil", i)))
                    banks.drain(key, "act_made")
                    if i < 4:
                        act.wait_ge(*dve_made[K + "gated", i])
                        act_hi(act, oa[0][:, i, :], sil[:, i % 3, :], (K + "oa", i))
                    else:
                        act.wait_ge(*dve_made[K + "gated", i])
                        act.activation(sq2[:, i - 4, :], xbc[:, i - 4, :], ACT.Square)\
                           .then_inc(*act_made.mark((K + "gn", "sq", i - 4)))

            def dve_gate(dve):
                dve.wait_ge(*filled[K + "y", KD - 1])
                for i in range(12):
                    key = (K + "ga", i) if i < 4 else (K + "z", i - 4)
                    keep_up(dve, "dve", key)
                    dve.wait_ge(*act_made[K + "sil", i])
                    if i < 4:
                        dve.wait_ge(*turned_at(K + "ot")(i))
                        dve.tensor_tensor(sil[:, i % 3, :], oT[:, i, :], sil[:, i % 3, :], ALU.mult)\
                           .then_inc(*dve_made.mark((K + "gated", i)))
                        dve_lo(dve, oa[0][:, i, :], oa[1][:, i, :], sil[:, i % 3, :], (K + "oa", i))
                    else:
                        dve.wait_ge(*dve_made[K + "y", i - 4])
                        d = xbc[:, i - 4, :]
                        dve.tensor_tensor(d, d, sil[:, i % 3, :], ALU.mult).then_inc(*dve_made.mark((K + "gated", i)))

            then(pe=pe_gate, act=act_gate, dve=dve_gate)

            gn = K + "gn"
            AHEAD = {0: "ya", 3: "gla", 6: "gls"}

            def act_gn(act):
                act_root(act, gn, roots)
                for k in range(KD):
                    if k in AHEAD:
                        keep_up(act, "act", (K + AHEAD[k], 0))
                    act.wait_ge(*dve_made[gn, "scaled", k])
                    act_hi(act, ys_hi[:, k, :], hv[:, k % 4, :], (K + "ys in", k))

            def pe_gn(pe):
                for k in range(KD):
                    pe.wait_ge(*act_made[gn, "sq", k])
                    i = pe_squares(pe, sq2[:, k, :], cst("mean_g"), 4 * (k // 4), k == 0)
                i.then_inc(*filled.mark((gn, "mean")))
                for g in range(2):
                    pe_all_partitions(pe, gn, rstd[:, g, :], g)

            def dve_gn(dve):
                dve_inverse(dve, gn, roots, (gn, "mean"))
                for g in range(2):
                    dve_diagonal(dve, gn, roots[:, NT * g:NT * g + NT], rstd[:, g, :], g)
                for k in range(KD):
                    if k in AHEAD:
                        keep_up(dve, "dve", (K + AHEAD[k], 0))
                    dve.wait_ge(*filled[gn, "rep", k // 4])
                    if k >= 4:
                        dve.wait_ge(*dve_made[(K + "ys in", k - 4), "lo"])
                    dve.scalar_tensor_tensor(out=hv[:, k % 4, :], in0=xbc[:, k, :], scalar=col("ssm_g", l, k),
                                             in1=banks[gn, "rep", k // 4][:, :], op0=ALU.mult, op1=ALU.mult)\
                       .then_inc(*dve_made.mark((gn, "scaled", k)))
                    if k % 4 == 3:
                        banks.drain((gn, "rep", k // 4), "dve_made")
                    dve_lo(dve, ys_hi[:, k, :], ys_lo[:, k, :], hv[:, k % 4, :], (K + "ys in", k))

            then(pe=pe_gn, act=act_gn, dve=dve_gn)

            def pe_merge(pe):
                for k in range(4):
                    pe.wait_ge(*dve_made[(K + "oa", k), "lo"])
                oa_in, ys_in = Pair(*oa), Pair(ys_hi, ys_lo)
                for n in range(0, KD, 2):
                    for m in (n, n + 1):
                        pe_linear(pe, K + "ya", m, oa_in, 4, None)
                    for m in (n, n + 1):
                        pe_linear(pe, K + "gla", m, hT, KD, None)
                        pe_linear(pe, K + "gls", m, hT, KD, None)
                        pe_linear(pe, K + "ys", m, ys_in, KD, lo_of(K + "ys in") if m == 0 else None)

            def act_merge(act):
                for n in range(0, KD, 2):
                    for m in (n, n + 1):
                        keep_up(act, "act", (K + "ya", m))
                    for m in (n, n + 1):
                        for j, key in enumerate(("gla", "gls")):
                            act_bank(act, (K + key, m))
                            if m >= 2:
                                act.wait_ge(*dve_made[(K + "mg", m - 2), "lo"])
                            act.activation(sg[:, m % 2, j, :], banks[K + key, m][:, :], ACT.Sigmoid)\
                               .then_inc(*act_made.mark((K + "sg", m, j)))
                            banks.drain((K + key, m), "act_made")
                        keep_up(act, "act", (K + "ys", m))
                        act.wait_ge(*pool_made[K + "mg", m])
                        act_hi(act, mg[:, 0, m, :], sg[:, m % 2, 0, :], (K + "mg", m))

            def dve_merge(dve):
                for n in range(0, KD, 2):
                    for m in (n, n + 1):
                        keep_up(dve, "dve", (K + "ya", m))
                    for m in (n, n + 1):
                        keep_up(dve, "dve", (K + "gls", m))
                        for j, key in enumerate(("ya", "ys")):
                            dve.wait_ge(*act_made[K + "sg", m, j])
                            dve_bank(dve, (K + key, m))
                            dve.tensor_tensor(sg[:, m % 2, j, :], sg[:, m % 2, j, :], banks[K + key, m][:, :],
                                              ALU.mult).then_inc(*dve_made.mark((K + "tg", m, j)))
                            banks.drain((K + key, m), "dve_made")
                        dve.wait_ge(*pool_made[K + "mg", m])
                        dve_lo(dve, mg[:, 0, m, :], mg[:, 1, m, :], sg[:, m % 2, 0, :], (K + "mg", m))

            def pool_merge(pool):
                for n in range(KD):
                    for j in range(2):
                        pool.wait_ge(*dve_made[K + "tg", n, j])
                    pool.tensor_tensor(sg[:, n % 2, 0, :], sg[:, n % 2, 0, :], sg[:, n % 2, 1, :], ALU.add)\
                        .then_inc(*pool_made.mark((K + "mg", n)))

            then(pe=pe_merge, act=act_merge, dve=dve_merge, pool=pool_merge)
            then(back_to_x(K + "out", mg, KD, lo_of(K + "mg"), nxt, lambda n: mod[:, 24 * l + 16 + n:24 * l + 17 + n]))

        block2(0, "L1h", filled[("f1", "b"), FC - 1], filled[("f1", "y"), KD - 1])
        block2(1, "fin", filled["L0gls", KD - 1], filled["L0out", KD - 1])
        then(norm("fin", ("final_g", 0), to_x=True))

        A = Area()
        y_nat = A.take(NT, D)

        def pe_back(pe):
            for k in range(KD):
                pe.wait_ge(*dve_made["fin", "scaled", k])
            for t in range(NT):
                for half in range(2):
                    bank = banks.take(pe, ("back", t, half))
                    for j in range(4):
                        tp(pe, bank[:, j * P:(j + 1) * P], xT[:, half * 4 + j, t * P:(t + 1) * P], ident,
                           done=("back", t, half) if j == 3 else None)

        def act_back(act):
            act.wait_ge(*filled["L1out", KD - 1])
            for t in range(NT):
                act.wait_ge(*filled["back", t, 0])
                act.activation(y_nat[:, t, 0:512], banks["back", t, 0][:, :], ACT.Copy)\
                   .then_inc(*act_made.mark(("back", t)))
                banks.drain(("back", t, 0), "act_made")
                act.wait_ge(*act_made["back", t])
                act.wait_ge(*dve_made["back", t])
                act.dma_start(out[t * P:(t + 1) * P, :], y_nat[:, t, :]).then_inc(out_stored, 16)
            act.wait_ge(out_stored, 16 * NT)

        def dve_back(dve):
            for t in range(NT):
                dve.wait_ge(*filled["back", t, 1])
                dve.tensor_copy(y_nat[:, t, 512:1024], banks["back", t, 1][:, :])\
                   .then_inc(*dve_made.mark(("back", t)))
                banks.drain(("back", t, 1), "dve_made")

        then(pe=pe_back, act=act_back, dve=dve_back)

        block = ctx.enter_context(nc.Block())
        n_panels = stream_of.shape[0]

        @block.sync
        def _(sp):
            for t in range(NT):
                sp.dma_start(x_nat[:, t, :], x_in[t * P:(t + 1) * P, :]).then_inc(x_landed[t], 16)
            for i in range(n_panels):
                if i >= RAW:
                    old = i - RAW
                    kind = kinds[old]
                    sp.wait_ge(*(dve_made["w_lo", old] if kind == "split" else filled["panel", old] if kind == "PE"
                                 else dve_made["ada panel", old]))
                sp.dma_start(ring[:, i % RAW, :, :].rearrange("p k w -> p (k w)"), stream_of[i])\
                  .then_inc(panel_landed[i % RAW], 16)

        @block.scalar
        def _(act):
            act.dma_start(cf[:, :], cf_in).then_inc(cf_landed, 16)
            act.dma_start(vec[:, :], vec_in).then_inc(const_landed, 16)
            act.dma_start(cb[:, :], cb_in).then_inc(const_landed, 16)
            act.dma_start(rot[:, :, :].rearrange("p a b -> p (a b)"), rot_in[:, 0:2 * SEQ]).then_inc(rot_landed, 16)
            for part in prog["act"]:
                finish(part(act))

        @block.tensor
        def _(pe):
            for part in prog["pe"]:
                finish(part(pe))

        @block.vector
        def _(dve):
            for part in prog["dve"]:
                finish(part(dve))

        @block.gpsimd
        def _(pool):
            for part in prog["pool"]:
                finish(part(pool))

    assert tile_no[0] == n_tiles, (tile_no[0], n_tiles)
    return {"signals": {n: dict(s.at) for n, s in signals.items()}, "at": dict(banks.at),
            "drained": dict(banks.drained), "panel_of": dict(banks.panel_of)}


def pack_stream(inputs):
    tiles = stream()
    assert len(tiles) % KD == 0
    a = np.zeros((len(tiles) // KD, P, KD, P), np.float32)
    for t, (name, layer, row, cols) in enumerate(tiles):
        w = inputs[name][layer]
        d = a[t // KD, :, t % KD, :]
        if isinstance(cols, str):
            d[0:DH, 0:DH] = w[row:row + DH]
            d[DH:P, DH:P] = w[row:row + DH]
        elif cols[-1] - cols[0] == len(cols) - 1:
            d[:, 0:len(cols)] = w[row:row + P, cols[0]:cols[-1] + 1]
        else:
            d[:, 0:len(cols)] = w[row:row + P][:, cols]
    return a.reshape(len(tiles) // KD, P, KD * P)


def pack_vec(inputs):
    a = np.zeros((P, NVEC), np.float32)

    def put(name, layer, v, chunks):
        a[:, VEC[name, layer]:VEC[name, layer] + chunks] = v.reshape(chunks, P).T

    for l in range(2):
        put("attn_norm", l, inputs["attn_norm"][l], KD)
        put("ffn_norm", l, inputs["ffn_norm"][l], KD)
        for j in range(3):
            put("conv_w", (l, j), inputs["ffn_conv_w"][l, j], FC)
        put("conv_b", l, inputs["ffn_conv_b"][l], FC)
        put("b_ada", l, inputs["b_ada_2"][l], 24)
        put("norm_g", l, inputs["norm_g_2"][l], KD)
        for j in range(4):
            put("xconv_w", (l, j), inputs["conv_w_2"][l, j], 12)
        put("xconv_b", l, inputs["conv_b_2"][l], 12)
        a[0:16, VEC["dt_bias", l]] = inputs["dt_bias_2"][l]
        a[0:16, VEC["a_log", l]] = inputs["a_log_2"][l]
        put("d_skip", l, np.repeat(inputs["d_skip_2"][l], DH), KD)
        put("ssm_g", l, inputs["ssm_norm_g_2"][l], KD)
    put("final_norm", 0, inputs["final_norm"], KD)
    put("final_g", 0, inputs["final_g_2"], KD)
    put("c", 0, inputs["c_2"][0], KD)
    for name, src in (("pos_k", "ev_cmp_pos_k"), ("pos_v", "ev_cmp_pos_v")):
        o = VEC[name, 0]
        a[0:DH, o:o + CMP_LEN] = inputs[src][0].T
        a[DH:P, o:o + CMP_LEN] = inputs[src][0].T
    a[0:16, VEC["b_f", 0]] = inputs["od_b_f"][0]
    return a


def kernel(**inputs):
    import ml_dtypes
    import concourse.bacc as bacc
    from concourse.bass_utils import run_bass_kernel_spmd as run

    inputs = {k: np.ascontiguousarray(v) for k, v in inputs.items()}
    cf, cb, rot = constants()
    arrays = {"weights": pack_stream(inputs), "x": inputs["x"][0], "vec": pack_vec(inputs), "cf": cf,
              "cb": cb.astype(ml_dtypes.bfloat16), "rot": rot}

    def program(known, final=False):
        nc = bacc.Bacc("TRN2", target_bir_lowering=False, num_devices=1)
        ins = [nc.dram_tensor(n + "_dram", a.shape, mybir.dt.from_np(a.dtype), kind="ExternalInput").ap()
               for n, a in arrays.items()]
        out = nc.dram_tensor("out_dram", (SEQ, D), F32, kind="ExternalOutput").ap()
        return nc, build(nc, ins, out, known, final)

    _, known = program(None)
    _, known = program(known)
    nc, _ = program(known, final=True)
    r = run(nc, [{n + "_dram": a for n, a in arrays.items()}], core_ids=[0])
    return np.asarray(r.results[0]["out_dram"]).reshape(1, SEQ, D)
```
